# Optimizing a Trainium2 kernel written in Bass

```python
import math
import jax, jax.numpy as jnp
from jax import lax
import numpy as np

D_MODEL = 1024
BATCH = 1
SEQ = 256
DEPTH = 2

N_MIXERS = 2
MLA_HEADS = 8
MLA_Q_RANK = 384
MLA_KV_RANK = 256
MLA_NOPE_DIM = 128
MLA_ROPE_DIM = 64
MLA_V_DIM = 128
ROPE_THETA = 10000.0
MOBA_HEADS = 8
MOBA_HEAD_DIM = D_MODEL // MOBA_HEADS
MOBA_BLOCK = 256
MOBA_TOP_K = 3
REL_BUCKETS = 32
REL_MAX_DISTANCE = 1024
D_FF = 4 * D_MODEL
Q_BLOCK = 128
RMS_EPS = 1e-6
N_MLA_LAYERS = (DEPTH + 1) // 2
N_MOBA_LAYERS = DEPTH // 2


def rms_norm(x, g):
    xf = x.astype(jnp.float32)
    y = xf * lax.rsqrt(jnp.mean(xf * xf, axis=-1, keepdims=True) + RMS_EPS)
    return (y * g.astype(jnp.float32)).astype(x.dtype)

def rope_tables(positions):
    inv_freq = ROPE_THETA ** (-jnp.arange(0, MLA_ROPE_DIM, 2, dtype=jnp.float32) / MLA_ROPE_DIM)
    ang = positions.astype(jnp.float32)[..., None] * inv_freq
    return jnp.cos(ang), jnp.sin(ang)

def rope(x, cos, sin):
    half = x.shape[-1] // 2
    x1 = x[..., :half].astype(jnp.float32)
    x2 = x[..., half:].astype(jnp.float32)
    return jnp.concatenate([x1 * cos - x2 * sin, x2 * cos + x1 * sin], axis=-1).astype(x.dtype)

def t5_bucket(dist):
    n = jnp.maximum(dist, 0)
    max_exact = REL_BUCKETS // 2
    nf = jnp.maximum(n, 1).astype(jnp.float32)
    large = max_exact + (jnp.log(nf / max_exact) / math.log(REL_MAX_DISTANCE / max_exact)
                         * (REL_BUCKETS - max_exact)).astype(jnp.int32)
    large = jnp.minimum(large, REL_BUCKETS - 1)
    return jnp.where(n < max_exact, n, large)

def sq_relu_mlp(h, w_in, w_out):
    a = jax.nn.relu(h @ w_in)
    return (a * a) @ w_out

def mla_attention(q_nope, q_pe, k_nope, k_pe, v):
    B, H, S, _ = q_nope.shape
    nqb = S // Q_BLOCK
    scale = 1.0 / math.sqrt(MLA_NOPE_DIM + MLA_ROPE_DIM)
    k_idx = jnp.arange(S)

    def to_blocks(t):
        return jnp.moveaxis(t.reshape(B, H, nqb, Q_BLOCK, t.shape[-1]), 2, 0)

    def body(args):
        qn, qp, c = args
        logits = (jnp.einsum('bhqd,bhkd->bhqk', qn, k_nope)
                  + jnp.einsum('bhqd,bkd->bhqk', qp, k_pe)).astype(jnp.float32) * scale
        q_idx = c * Q_BLOCK + jnp.arange(Q_BLOCK)
        causal = k_idx[None, :] <= q_idx[:, None]
        logits = jnp.where(causal, logits, -jnp.inf)
        p = jax.nn.softmax(logits, axis=-1).astype(v.dtype)
        return jnp.einsum('bhqk,bhkd->bhqd', p, v)

    out = lax.map(body, (to_blocks(q_nope), to_blocks(q_pe), jnp.arange(nqb, dtype=jnp.int32)))
    return jnp.moveaxis(out, 0, 2).reshape(B, H, S, v.shape[-1])

def mla_mixer(h, w_in, q_a_norm, kv_a_norm, w_uq, w_ukv, q_nope_norm, q_rope_norm,
              k_nope_norm, k_rope_norm, w_o, cos, sin):
    B, S, _ = h.shape
    proj = h @ w_in
    c_q = proj[..., :MLA_Q_RANK]
    c_kv = proj[..., MLA_Q_RANK:MLA_Q_RANK + MLA_KV_RANK]
    k_pe = proj[..., MLA_Q_RANK + MLA_KV_RANK:]
    q = (rms_norm(c_q, q_a_norm) @ w_uq).reshape(B, S, MLA_HEADS, MLA_NOPE_DIM + MLA_ROPE_DIM)
    kv = (rms_norm(c_kv, kv_a_norm) @ w_ukv).reshape(B, S, MLA_HEADS, MLA_NOPE_DIM + MLA_V_DIM)
    q_nope = rms_norm(q[..., :MLA_NOPE_DIM], q_nope_norm)
    q_pe = rope(rms_norm(q[..., MLA_NOPE_DIM:], q_rope_norm), cos[:, :, None, :], sin[:, :, None, :])
    k_nope = rms_norm(kv[..., :MLA_NOPE_DIM], k_nope_norm)
    v = kv[..., MLA_NOPE_DIM:]
    k_pe = rope(rms_norm(k_pe, k_rope_norm), cos, sin)
    out = mla_attention(q_nope.transpose(0, 2, 1, 3), q_pe.transpose(0, 2, 1, 3),
                        k_nope.transpose(0, 2, 1, 3), k_pe, v.transpose(0, 2, 1, 3))
    return out.transpose(0, 2, 1, 3).reshape(B, S, MLA_HEADS * MLA_V_DIM) @ w_o

def moba_attention(q, k, v, positions, rel_bias_table):
    B, H, S, dh = q.shape
    nb = -(-S // MOBA_BLOCK)
    pad = nb * MOBA_BLOCK - S
    n_sel = min(MOBA_TOP_K, nb - 1)
    nqb = S // Q_BLOCK
    scale = 1.0 / math.sqrt(dh)
    kb = jnp.pad(k, ((0, 0), (0, 0), (0, pad), (0, 0))).reshape(B, H, nb, MOBA_BLOCK, dh)
    vb = jnp.pad(v, ((0, 0), (0, 0), (0, pad), (0, 0))).reshape(B, H, nb, MOBA_BLOCK, dh)
    k_mean = jnp.mean(kb.astype(jnp.float32), axis=3)
    pos_b = jnp.pad(positions, ((0, 0), (0, pad)), mode='edge').reshape(B, nb, MOBA_BLOCK)
    pos_q = jnp.moveaxis(positions.reshape(B, nqb, Q_BLOCK), 1, 0)
    q_blocks = jnp.moveaxis(q.reshape(B, H, nqb, Q_BLOCK, dh), 2, 0)
    table_h = rel_bias_table.T
    b_i = jnp.arange(B)[:, None, None]
    h_i = jnp.arange(H)[None, :, None]
    h_i4 = jnp.arange(H)[None, :, None, None]
    blk_ids = jnp.arange(nb)
    t_ids = jnp.arange(MOBA_BLOCK)

    def rel_bias(pq, pk):
        return table_h[h_i4, t5_bucket(pq - pk)].astype(jnp.float32)

    def body(args):
        qi, pq, c = args
        q_start = c * Q_BLOCK
        own = q_start // MOBA_BLOCK
        q_idx = q_start + jnp.arange(Q_BLOCK)
        pq4 = pq[:, None, :, None]
        parts = []
        sel = None
        if n_sel > 0:
            gate = jnp.einsum('bhqd,bhnd->bhqn', qi.astype(jnp.float32), k_mean)
            gate = jnp.where(blk_ids < own, gate, -jnp.inf)
            _, sel = lax.top_k(gate, n_sel)
            for r in range(n_sel):
                sel_r = sel[..., r]
                k_sel = kb[b_i, h_i, sel_r]
                lg = (jnp.einsum('bhqd,bhqtd->bhqt', qi, k_sel).astype(jnp.float32) * scale
                      + rel_bias(pq4, pos_b[b_i, sel_r]))
                parts.append(jnp.where(r < own, lg, -jnp.inf))
        k_own = lax.dynamic_index_in_dim(kb, own, axis=2, keepdims=False)
        v_own = lax.dynamic_index_in_dim(vb, own, axis=2, keepdims=False)
        pos_own = lax.dynamic_index_in_dim(pos_b, own, axis=1, keepdims=False)
        lg_own = (jnp.einsum('bhqd,bhtd->bhqt', qi, k_own).astype(jnp.float32) * scale
                  + rel_bias(pq4, pos_own[:, None, None, :]))
        causal = (own * MOBA_BLOCK + t_ids)[None, :] <= q_idx[:, None]
        parts.append(jnp.where(causal, lg_own, -jnp.inf))
        p = jax.nn.softmax(jnp.concatenate(parts, axis=-1), axis=-1).astype(v.dtype)
        p = p.reshape(B, H, Q_BLOCK, n_sel + 1, MOBA_BLOCK)
        out = jnp.einsum('bhqt,bhtd->bhqd', p[..., n_sel, :], v_own)
        for r in range(n_sel):
            v_sel = vb[b_i, h_i, sel[..., r]]
            out = out + jnp.einsum('bhqt,bhqtd->bhqd', p[..., r, :], v_sel)
        return out

    out = lax.map(body, (q_blocks, pos_q, jnp.arange(nqb, dtype=jnp.int32)))
    return jnp.moveaxis(out, 0, 2).reshape(B, H, S, dh)

def moba_mixer(h, w_qkv, q_norm, k_norm, w_o, positions, rel_bias_table):
    B, S, _ = h.shape
    qkv = (h @ w_qkv).reshape(B, S, 3, MOBA_HEADS, MOBA_HEAD_DIM)
    q = rms_norm(qkv[:, :, 0], q_norm).transpose(0, 2, 1, 3)
    k = rms_norm(qkv[:, :, 1], k_norm).transpose(0, 2, 1, 3)
    v = qkv[:, :, 2].transpose(0, 2, 1, 3)
    out = moba_attention(q, k, v, positions, rel_bias_table)
    return out.transpose(0, 2, 1, 3).reshape(B, S, MOBA_HEADS * MOBA_HEAD_DIM) @ w_o

def first_inputs(seed: int = 0) -> dict:
    key = jax.random.key(seed)
    ks = jax.random.split(key, 24)

    def nrm(k, shape, scale):
        return scale * jax.random.normal(k, shape, jnp.float32)

    def gain(k, shape):
        return 1.0 + 0.05 * jax.random.normal(k, shape, jnp.float32)

    qk_dim = MLA_NOPE_DIM + MLA_ROPE_DIM
    offset = jax.random.randint(ks[1], (BATCH,), 0, 4096, dtype=jnp.int32)
    positions = offset[:, None] + jnp.arange(SEQ, dtype=jnp.int32)[None, :]
    return {
        "x": nrm(ks[0], (BATCH, SEQ, D_MODEL), 1.0),
        "positions": positions,
        "rel_bias_table": nrm(ks[2], (REL_BUCKETS, MOBA_HEADS), 0.5),
        "attn_norm": gain(ks[3], (DEPTH, D_MODEL)),
        "mlp_norm": gain(ks[4], (DEPTH, D_MODEL)),
        "mla_w_in": nrm(ks[5], (N_MLA_LAYERS, D_MODEL, MLA_Q_RANK + MLA_KV_RANK + MLA_ROPE_DIM), D_MODEL ** -0.5),
        "mla_q_a_norm": gain(ks[6], (N_MLA_LAYERS, MLA_Q_RANK)),
        "mla_kv_a_norm": gain(ks[7], (N_MLA_LAYERS, MLA_KV_RANK)),
        "mla_w_uq": nrm(ks[8], (N_MLA_LAYERS, MLA_Q_RANK, MLA_HEADS * qk_dim), MLA_Q_RANK ** -0.5),
        "mla_w_ukv": nrm(ks[9], (N_MLA_LAYERS, MLA_KV_RANK, MLA_HEADS * (MLA_NOPE_DIM + MLA_V_DIM)), MLA_KV_RANK ** -0.5),
        "mla_q_nope_norm": gain(ks[10], (N_MLA_LAYERS, MLA_NOPE_DIM)),
        "mla_q_rope_norm": gain(ks[11], (N_MLA_LAYERS, MLA_ROPE_DIM)),
        "mla_k_nope_norm": gain(ks[12], (N_MLA_LAYERS, MLA_NOPE_DIM)),
        "mla_k_rope_norm": gain(ks[13], (N_MLA_LAYERS, MLA_ROPE_DIM)),
        "mla_w_o": nrm(ks[14], (N_MLA_LAYERS, MLA_HEADS * MLA_V_DIM, D_MODEL), (MLA_HEADS * MLA_V_DIM) ** -0.5),
        "moba_w_qkv": nrm(ks[15], (N_MOBA_LAYERS, D_MODEL, 3 * MOBA_HEADS * MOBA_HEAD_DIM), D_MODEL ** -0.5),
        "moba_q_norm": gain(ks[16], (N_MOBA_LAYERS, MOBA_HEAD_DIM)),
        "moba_k_norm": gain(ks[17], (N_MOBA_LAYERS, MOBA_HEAD_DIM)),
        "moba_w_o": nrm(ks[18], (N_MOBA_LAYERS, MOBA_HEADS * MOBA_HEAD_DIM, D_MODEL), (MOBA_HEADS * MOBA_HEAD_DIM) ** -0.5),
        "mlp_w_in": nrm(ks[19], (DEPTH, D_MODEL, D_FF), D_MODEL ** -0.5),
        "mlp_w_out": nrm(ks[20], (DEPTH, D_FF, D_MODEL), D_FF ** -0.5),
    }

def first_block(x, positions, rel_bias_table, attn_norm, mlp_norm, mla_w_in, mla_q_a_norm, mla_kv_a_norm,
              mla_w_uq, mla_w_ukv, mla_q_nope_norm, mla_q_rope_norm, mla_k_nope_norm, mla_k_rope_norm,
              mla_w_o, moba_w_qkv, moba_q_norm, moba_k_norm, moba_w_o, mlp_w_in, mlp_w_out):
    cos, sin = rope_tables(positions)
    for i in range(DEPTH):
        h = rms_norm(x, attn_norm[i])
        j = i // N_MIXERS
        if i % N_MIXERS == 0:
            x = x + mla_mixer(h, mla_w_in[j], mla_q_a_norm[j], mla_kv_a_norm[j], mla_w_uq[j], mla_w_ukv[j],
                              mla_q_nope_norm[j], mla_q_rope_norm[j], mla_k_nope_norm[j], mla_k_rope_norm[j],
                              mla_w_o[j], cos, sin)
        else:
            x = x + moba_mixer(h, moba_w_qkv[j], moba_q_norm[j], moba_k_norm[j], moba_w_o[j],
                               positions, rel_bias_table)
        h = rms_norm(x, mlp_norm[i])
        x = x + sq_relu_mlp(h, mlp_w_in[i], mlp_w_out[i])
    return x


DEPTH_2 = 1

GRID_W = 64
CTX_LEN = 256
EPS = 1e-6

NA_HEADS = 8
HEAD_DIM = 64
NA_WIDTH = NA_HEADS * HEAD_DIM
NA_ROWS = 8
NA_COLS = 16

SSD_HEADS = 8
SSD_HEAD_DIM = 64
SSD_WIDTH = SSD_HEADS * SSD_HEAD_DIM
SSD_GROUPS = 2
SSD_STATE = 128
SSD_CONV = 3
SSD_CHUNK = 128
GN = SSD_GROUPS * SSD_STATE
XBC_WIDTH = SSD_WIDTH + 2 * GN

MIX_WIDTH = NA_WIDTH + SSD_WIDTH
IN_WIDTH = 3 * NA_WIDTH + SSD_WIDTH + XBC_WIDTH + 2 * SSD_HEADS

D_FF_2 = 2816
FFN_CONV = 3


def rms_norm_2(x, w):
    xf = x.astype(jnp.float32)
    y = xf * lax.rsqrt(jnp.mean(xf * xf, axis=-1, keepdims=True) + EPS)
    return (y * w.astype(jnp.float32)).astype(x.dtype)

def modulate(h, shift, scale):
    return h * (1.0 + scale) + shift

def flip(t):
    return jnp.flip(t, axis=1)

def depthwise_conv(x, w, b):
    k, ch = w.shape
    y = lax.conv_general_dilated(
        x, w[:, None, :].astype(x.dtype), window_strides=(1,),
        padding=[(k // 2, k // 2)], dimension_numbers=("NWC", "WIO", "NWC"),
        feature_group_count=ch)
    return y + b

def axial_rope(x, row_pos, col_pos):
    n_freq = x.shape[-1] // 4
    freqs = ROPE_THETA ** (-jnp.arange(n_freq, dtype=jnp.float32) / n_freq)
    ang = jnp.concatenate([row_pos[:, None] * freqs, col_pos[:, None] * freqs], axis=-1)
    cos = jnp.cos(ang)[None, :, None, :]
    sin = jnp.sin(ang)[None, :, None, :]
    x1, x2 = jnp.split(x.astype(jnp.float32), 2, axis=-1)
    return jnp.concatenate([x1 * cos - x2 * sin, x1 * sin + x2 * cos], axis=-1).astype(x.dtype)

def neighbourhood_attention(q, k, v, k_ctx, v_ctx, rpb, rows):
    bsz, s, nh, dh = q.shape
    kh = min(NA_ROWS, rows)
    scale = dh ** -0.5
    qg = q.reshape(bsz, rows, GRID_W, nh, dh)
    kg = k.reshape(bsz, rows, GRID_W, nh, dh)
    vg = v.reshape(bsz, rows, GRID_W, nh, dh)
    col = np.arange(GRID_W)
    col_start = np.clip(col - NA_COLS // 2, 0, GRID_W - NA_COLS)
    col_idx = col_start[:, None] + np.arange(NA_COLS)
    dc = col_idx - col[:, None] + (NA_COLS - 1)
    n_loc = kh * NA_COLS

    def row_block(r):
        rs = jnp.clip(r - kh // 2, 0, rows - kh)
        k_win = lax.dynamic_slice_in_dim(kg, rs, kh, axis=1)[:, :, col_idx]
        v_win = lax.dynamic_slice_in_dim(vg, rs, kh, axis=1)[:, :, col_idx]
        q_r = lax.dynamic_index_in_dim(qg, r, axis=1, keepdims=False)
        dr = rs + jnp.arange(kh) - r + (NA_ROWS - 1)
        bias = rpb[:, dr[None, :, None], dc[:, None, :]]
        s_loc = jnp.einsum("bwhd,brwkhd->bhwrk", q_r, k_win) * scale + bias
        s_ctx = jnp.einsum("bwhd,bchd->bhwc", q_r, k_ctx) * scale
        scores = jnp.concatenate([s_loc.reshape(bsz, nh, GRID_W, n_loc), s_ctx], axis=-1)
        p = jax.nn.softmax(scores.astype(jnp.float32), axis=-1).astype(v.dtype)
        p_loc = p[..., :n_loc].reshape(bsz, nh, GRID_W, kh, NA_COLS)
        return (jnp.einsum("bhwrk,brwkhd->bwhd", p_loc, v_win)
                + jnp.einsum("bhwc,bchd->bwhd", p[..., n_loc:], v_ctx))

    out = lax.map(row_block, jnp.arange(rows))
    return out.transpose(1, 0, 2, 3, 4).reshape(bsz, s, nh * dh)

def context_attention(q, k, v):
    bsz, lc, nh, dh = q.shape
    s = jnp.einsum("bqhd,bkhd->bhqk", q, k) * dh ** -0.5
    p = jax.nn.softmax(s.astype(jnp.float32), axis=-1).astype(v.dtype)
    return jnp.einsum("bhqk,bkhd->bqhd", p, v).reshape(bsz, lc, nh * dh)

def ssd_prep(p_xbc_dt, conv_w, conv_b, dt_bias):
    bsz, l, _ = p_xbc_dt.shape
    xbc = jax.nn.silu(depthwise_conv(p_xbc_dt[..., :XBC_WIDTH], conv_w, conv_b))
    xs = xbc[..., :SSD_WIDTH].reshape(bsz, l, SSD_HEADS, SSD_HEAD_DIM)
    bm = xbc[..., SSD_WIDTH:SSD_WIDTH + GN].reshape(bsz, l, SSD_GROUPS, SSD_STATE)
    cm = xbc[..., SSD_WIDTH + GN:].reshape(bsz, l, SSD_GROUPS, SSD_STATE)
    dt_raw = p_xbc_dt[..., XBC_WIDTH:].reshape(bsz, l, 2, SSD_HEADS).astype(jnp.float32)
    dt = jax.nn.softplus(dt_raw + dt_bias.astype(jnp.float32))
    return xs, bm, cm, dt

def ssd_chunked(xs, dt, a, bm, cm, h0):
    bsz, l, nh, hp = xs.shape
    g, n = bm.shape[2], bm.shape[3]
    e = nh // g
    q = SSD_CHUNK
    nc = l // q
    xc = xs.reshape(bsz, nc, q, g, e, hp)
    bc = bm.reshape(bsz, nc, q, g, n)
    cc = cm.reshape(bsz, nc, q, g, n)
    dtc = dt.reshape(bsz, nc, q, g, e)
    cum = jnp.cumsum(dtc * a.reshape(g, e), axis=2)
    seg = cum[:, :, :, None] - cum[:, :, None, :]
    lower = np.tril(np.ones((q, q), dtype=bool))[:, :, None, None]
    decay = jnp.exp(jnp.where(lower, seg, -jnp.inf))
    cb = jnp.einsum("bcign,bcjgn->bcijg", cc, bc)
    m = cb[..., None] * decay * dtc[:, :, None]
    y_diag = jnp.einsum("bcijge,bcjgep->bcigep", m, xc)
    w_end = jnp.exp(cum[:, :, -1:] - cum) * dtc
    states = jnp.einsum("bcjgn,bcjge,bcjgep->bcgepn", bc, w_end, xc)
    chunk_decay = jnp.exp(cum[:, :, -1])

    def step(h, inp):
        dec, st = inp
        return h * dec[..., None, None] + st, h

    h_final, h_in = lax.scan(step, h0.reshape(bsz, g, e, hp, n).astype(states.dtype),
                             (jnp.moveaxis(chunk_decay, 1, 0), jnp.moveaxis(states, 1, 0)))
    h_in = jnp.moveaxis(h_in, 0, 1)
    y_off = jnp.einsum("bcign,bcgepn,bcige->bcigep", cc, h_in, jnp.exp(cum))
    return (y_diag + y_off).reshape(bsz, l, nh, hp), h_final.reshape(bsz, nh, hp, n)

def ssd_final_state(xs, dt, a, bm):
    bsz, l, nh, hp = xs.shape
    g, n = bm.shape[2], bm.shape[3]
    e = nh // g
    cum = jnp.cumsum(dt * a, axis=1)
    w = (jnp.exp(cum[:, -1:] - cum) * dt).reshape(bsz, l, g, e)
    h = jnp.einsum("blgn,blge,blgep->bgepn", bm, w, xs.reshape(bsz, l, g, e, hp))
    return h.reshape(bsz, nh, hp, n)

def ssd_bidirectional(z, xs, bm, cm, dt, a, d_skip, norm_w, h0_fwd, h0_bwd):
    y_f, h_f = ssd_chunked(xs, dt[..., 0, :], a[0], bm, cm, h0_fwd)
    y_b, h_b = ssd_chunked(flip(xs), flip(dt[..., 1, :]), a[1], flip(bm), flip(cm), h0_bwd)
    y = y_f + flip(y_b) + d_skip[:, None] * xs
    bsz, l = xs.shape[:2]
    y = y.reshape(bsz, l, SSD_WIDTH) * jax.nn.silu(z)
    return rms_norm_2(y, norm_w), h_f, h_b

def conv_glu(h, w_up, conv_w, conv_b, w_down):
    gate, val = jnp.split(h @ w_up, 2, axis=-1)
    gate = depthwise_conv(gate, conv_w, conv_b)
    return (jax.nn.silu(gate) * val) @ w_down

def hybrid_layer(x, ctx, c, c_ctx, ada_w, ada_b, norm1_w, w_in, rpb, ssd_conv_w, ssd_conv_b,
                 dt_bias, a_log, ssd_d, ssd_norm_w, w_out, norm2_w, ffn_w_up, ffn_conv_w,
                 ffn_conv_b, ffn_w_down, rows, row_pos, col_pos, update_ctx):
    bsz, s, _ = x.shape
    lc = ctx.shape[1]
    mod = (jax.nn.silu(c) @ ada_w + ada_b)[:, None, :]
    mod_c = (jax.nn.silu(c_ctx) @ ada_w + ada_b)[None, None, :]
    sh1, sc1, g1, sh2, sc2, g2 = jnp.split(mod, 6, axis=-1)
    sh1c, sc1c, g1c, sh2c, sc2c, g2c = jnp.split(mod_c, 6, axis=-1)
    a = -jnp.exp(a_log.astype(jnp.float32))

    h = modulate(rms_norm_2(x, norm1_w), sh1, sc1)
    hc = modulate(rms_norm_2(ctx, norm1_w), sh1c, sc1c)
    p = h @ w_in
    col_ssd = 3 * NA_WIDTH + SSD_WIDTH
    if update_ctx:
        pc = hc @ w_in
        qc = pc[..., :NA_WIDTH].reshape(bsz, lc, NA_HEADS, HEAD_DIM)
        kvc = pc[..., NA_WIDTH:3 * NA_WIDTH]
        zc = pc[..., 3 * NA_WIDTH:col_ssd]
        sc_in = pc[..., col_ssd:]
    else:
        kvc = hc @ w_in[:, NA_WIDTH:3 * NA_WIDTH]
        sc_in = hc @ w_in[:, col_ssd:]
    kc = kvc[..., :NA_WIDTH].reshape(bsz, lc, NA_HEADS, HEAD_DIM)
    vc = kvc[..., NA_WIDTH:].reshape(bsz, lc, NA_HEADS, HEAD_DIM)

    q = axial_rope(p[..., :NA_WIDTH].reshape(bsz, s, NA_HEADS, HEAD_DIM), row_pos, col_pos)
    k = axial_rope(p[..., NA_WIDTH:2 * NA_WIDTH].reshape(bsz, s, NA_HEADS, HEAD_DIM), row_pos, col_pos)
    v = p[..., 2 * NA_WIDTH:3 * NA_WIDTH].reshape(bsz, s, NA_HEADS, HEAD_DIM)
    attn = neighbourhood_attention(q, k, v, kc, vc, rpb, rows)

    xs_c, bm_c, cm_c, dt_c = ssd_prep(sc_in, ssd_conv_w, ssd_conv_b, dt_bias)
    if update_ctx:
        zero = jnp.zeros((bsz, SSD_HEADS, SSD_HEAD_DIM, SSD_STATE), jnp.float32)
        y_c, h_fwd, h_bwd = ssd_bidirectional(zc, xs_c, bm_c, cm_c, dt_c, a, ssd_d, ssd_norm_w, zero, zero)
    else:
        h_fwd = ssd_final_state(xs_c, dt_c[..., 0, :], a[0], bm_c)
        h_bwd = ssd_final_state(flip(xs_c), flip(dt_c[..., 1, :]), a[1], flip(bm_c))
    xs, bm, cm, dt = ssd_prep(p[..., col_ssd:], ssd_conv_w, ssd_conv_b, dt_bias)
    y_ssd, _, _ = ssd_bidirectional(p[..., 3 * NA_WIDTH:col_ssd], xs, bm, cm, dt, a, ssd_d,
                                    ssd_norm_w, h_fwd, h_bwd)

    x = x + g1 * (jnp.concatenate([attn, y_ssd], axis=-1) @ w_out)
    x = x + g2 * conv_glu(modulate(rms_norm_2(x, norm2_w), sh2, sc2), ffn_w_up, ffn_conv_w, ffn_conv_b, ffn_w_down)

    if update_ctx:
        attn_c = context_attention(qc, kc, vc)
        ctx = ctx + g1c * (jnp.concatenate([attn_c, y_c], axis=-1) @ w_out)
        ctx = ctx + g2c * conv_glu(modulate(rms_norm_2(ctx, norm2_w), sh2c, sc2c), ffn_w_up, ffn_conv_w, ffn_conv_b, ffn_w_down)
    return x, ctx

def second_inputs(seed: int = 0) -> dict:
    key = jax.random.key(seed)
    ks = jax.random.split(key, 24)
    f32 = jnp.float32

    def nrm(k, shape, s):
        return s * jax.random.normal(k, shape, f32)

    dt0 = jnp.exp(jax.random.uniform(ks[11], (DEPTH_2, 2, SSD_HEADS), f32, math.log(1e-3), math.log(1e-1)))
    return {
        "x": nrm(ks[0], (BATCH, SEQ, D_MODEL), 1.0),
        "c": nrm(ks[1], (BATCH, D_MODEL), 1.0),
        "ctx": nrm(ks[2], (BATCH, CTX_LEN, D_MODEL), 1.0),
        "c_ctx": nrm(ks[3], (D_MODEL,), 1.0),
        "ada_w": nrm(ks[4], (DEPTH_2, D_MODEL, 6 * D_MODEL), 0.5 * D_MODEL ** -0.5),
        "ada_b": nrm(ks[5], (DEPTH_2, 6 * D_MODEL), 0.02),
        "norm1_w": 1.0 + nrm(ks[6], (DEPTH_2, D_MODEL), 0.1),
        "w_in": nrm(ks[7], (DEPTH_2, D_MODEL, IN_WIDTH), D_MODEL ** -0.5),
        "rpb": nrm(ks[8], (DEPTH_2, NA_HEADS, 2 * NA_ROWS - 1, 2 * NA_COLS - 1), 0.5),
        "ssd_conv_w": nrm(ks[9], (DEPTH_2, SSD_CONV, XBC_WIDTH), SSD_CONV ** -0.5),
        "ssd_conv_b": nrm(ks[10], (DEPTH_2, XBC_WIDTH), 0.01),
        "dt_bias": dt0 + jnp.log(-jnp.expm1(-dt0)),
        "a_log": jnp.log(jax.random.uniform(ks[12], (DEPTH_2, 2, SSD_HEADS), f32, 1.0, 16.0)),
        "ssd_d": 1.0 + nrm(ks[13], (DEPTH_2, SSD_HEADS), 0.1),
        "ssd_norm_w": 1.0 + nrm(ks[14], (DEPTH_2, SSD_WIDTH), 0.1),
        "w_out": nrm(ks[15], (DEPTH_2, MIX_WIDTH, D_MODEL), MIX_WIDTH ** -0.5),
        "norm2_w": 1.0 + nrm(ks[16], (DEPTH_2, D_MODEL), 0.1),
        "ffn_w_up": nrm(ks[17], (DEPTH_2, D_MODEL, 2 * D_FF_2), D_MODEL ** -0.5),
        "ffn_conv_w": nrm(ks[18], (DEPTH_2, FFN_CONV, D_FF_2), FFN_CONV ** -0.5),
        "ffn_conv_b": nrm(ks[19], (DEPTH_2, D_FF_2), 0.01),
        "ffn_w_down": nrm(ks[20], (DEPTH_2, D_FF_2, D_MODEL), D_FF_2 ** -0.5),
        "final_norm_w": 1.0 + nrm(ks[21], (D_MODEL,), 0.1),
    }

def second_block(x, c, ctx, c_ctx, ada_w, ada_b, norm1_w, w_in, rpb, ssd_conv_w, ssd_conv_b,
              dt_bias, a_log, ssd_d, ssd_norm_w, w_out, norm2_w, ffn_w_up, ffn_conv_w,
              ffn_conv_b, ffn_w_down, final_norm_w):
    s = x.shape[1]
    rows = s // GRID_W
    t = jnp.arange(s)
    row_pos = (t // GRID_W).astype(jnp.float32)
    col_pos = (t % GRID_W).astype(jnp.float32)
    for i in range(DEPTH_2):
        x, ctx = hybrid_layer(x, ctx, c, c_ctx, ada_w[i], ada_b[i], norm1_w[i], w_in[i], rpb[i],
                              ssd_conv_w[i], ssd_conv_b[i], dt_bias[i], a_log[i], ssd_d[i],
                              ssd_norm_w[i], w_out[i], norm2_w[i], ffn_w_up[i], ffn_conv_w[i],
                              ffn_conv_b[i], ffn_w_down[i], rows, row_pos, col_pos,
                              update_ctx=(i < DEPTH_2 - 1))
    return rms_norm_2(x, final_norm_w)


def setup_inputs(seed=0):
    out = dict(first_inputs(seed))
    for name, value in second_inputs(seed + 1).items():
        if name != "x":
            out[name + "_2"] = value
    return out


def reference(
    x, positions, rel_bias_table, attn_norm, mlp_norm, mla_w_in, mla_q_a_norm, mla_kv_a_norm,
    mla_w_uq, mla_w_ukv, mla_q_nope_norm, mla_q_rope_norm, mla_k_nope_norm, mla_k_rope_norm,
    mla_w_o, moba_w_qkv, moba_q_norm, moba_k_norm, moba_w_o, mlp_w_in, mlp_w_out, c_2, ctx_2,
    c_ctx_2, ada_w_2, ada_b_2, norm1_w_2, w_in_2, rpb_2, ssd_conv_w_2, ssd_conv_b_2, dt_bias_2,
    a_log_2, ssd_d_2, ssd_norm_w_2, w_out_2, norm2_w_2, ffn_w_up_2, ffn_conv_w_2, ffn_conv_b_2,
    ffn_w_down_2, final_norm_w_2,
):
    x = first_block(
        x, positions, rel_bias_table, attn_norm, mlp_norm, mla_w_in, mla_q_a_norm,
        mla_kv_a_norm, mla_w_uq, mla_w_ukv, mla_q_nope_norm, mla_q_rope_norm, mla_k_nope_norm,
        mla_k_rope_norm, mla_w_o, moba_w_qkv, moba_q_norm, moba_k_norm, moba_w_o, mlp_w_in,
        mlp_w_out,
    )
    return second_block(
        x, c_2, ctx_2, c_ctx_2, ada_w_2, ada_b_2, norm1_w_2, w_in_2, rpb_2, ssd_conv_w_2,
        ssd_conv_b_2, dt_bias_2, a_log_2, ssd_d_2, ssd_norm_w_2, w_out_2, norm2_w_2, ffn_w_up_2,
        ffn_conv_w_2, ffn_conv_b_2, ffn_w_down_2, final_norm_w_2,
    )


_drawn_inputs = setup_inputs


def setup_inputs(seed=0):
    import zlib

    import numpy as np

    out = dict(_drawn_inputs(seed))
    spreads = {}
    factors = {'mla_q_a_norm': 5.154,
     'mla_kv_a_norm': 3.461,
     'mla_q_nope_norm': 5.835,
     'mla_q_rope_norm': 8.0,
     'mla_k_nope_norm': 7.248,
     'mla_k_rope_norm': 8.0,
     'moba_q_norm': 8.0,
     'moba_k_norm': 8.0,
     'ctx_2': 5.284,
     'ada_b_2': 4.563,
     'norm1_w_2': 3.671,
     'rpb_2': 8.0,
     'ssd_conv_b_2': 57.518,
     'a_log_2': 3.469,
     'ssd_d_2': 64.0,
     'ssd_norm_w_2': 5.502,
     'norm2_w_2': 3.37,
     'ffn_conv_b_2': 35.345}
    for name, (base, spread) in spreads.items():
        noise = np.random.default_rng([zlib.crc32(name.encode()), seed]).standard_normal(out[name].shape)
        drawn = base * np.exp(spread * noise) if base else spread * noise
        out[name] = __import__('jax').numpy.asarray(drawn.astype(out[name].dtype))
    for name, factor in factors.items():
        out[name] = (out[name] * factor).astype(out[name].dtype)
    return out
```

```python
import math
from contextlib import ExitStack

import numpy as np

import concourse.bass as bass
from concourse import mybir

F32 = mybir.dt.float32
I32 = mybir.dt.int32
ALU = mybir.AluOpType
ACT = mybir.ActivationFunctionType
AX = mybir.AxisListType

P = 128
T = 256
D = 1024
KD = D // P
EPS = 1e-6
H = 8
QR, KVR, NOPE, ROPE, VD = 384, 256, 128, 64, 128
FF = 4096
BUCKETS = 32
NA = 512
NST = 128
FF2 = 2816
KF2 = FF2 // P
NEG = -1e30
SLOT = 4096
MAGIC = 12582912.0

COLS = dict(attn_norm=16, mlp_norm=16, c_norm=5, q_nope=1, k_nope=1, moba_q=1, moba_k=1, norm1=8, norm2=8,
            ada_cols=32, conv_w=24, conv_b=8, fconv_w=3 * KF2, fconv_b=KF2, ssd_norm=4, c=8, c_ctx=8)
ROWS = dict(q_rope=ROPE, k_rope=ROPE, table=BUCKETS * H, dt_bias=16, a_log=16, ssd_d=8, final=D, ada_g=2 * D)
CONSTS = dict(ident=128, upto=256, since=256, after=128, before=128, ones=128, causal=384, grid=128, inv_freq=32,
              thresholds=32)


def starts(sizes):
    at, out = 0, {}
    for name, n in sizes.items():
        out[name] = at
        at += n
    out[None] = at
    return out


CA, RA, KA = starts(COLS), starts(ROWS), starts(CONSTS)

GEMMS = [("mla_in", 2, 2), ("mla_uq", 2, 4), ("mla_ukv", 2, 4), ("mla_o", 2, 2), ("up0", 8, 2), ("down0", 8, 0),
         ("qkv", 6, 2), ("moba_o", 2, 2), ("up1", 8, 2), ("down1", 8, 0),
         ("dt", 1, 1), ("xs", 1, 4), ("bc", 1, 4), ("q", 1, 2), ("k", 1, 4), ("z", 1, 2), ("v", 1, 4),
         ("out", 2, 2), ("glu", 11, 2), ("down2", 6, 0)]
SMALL = [("h0", 4), ("cT", 3), ("kpe", 1), ("qn", 4), ("kn", 4), ("qp", 2), ("att0", 24), ("m0", 4),
         ("h1", 4), ("q1", 4), ("k1", 4), ("att1", 24), ("m1", 4), ("ada", 5), ("hc", 4), ("hx", 4),
         ("cum", 1), ("cumcol", 1), ("later", 1), ("xsrow", 5), ("state", 2), ("cb", 2),
         ("nq", 2), ("nk", 2), ("na", 32), ("seg", 8), ("yoff", 4), ("yT", 2), ("m2", 4)]


def plan():
    chunk, unit, down = 0, 0, 0
    first_chunk, first_unit, released = {}, {}, []
    for name, n, per in GEMMS:
        first_chunk[name], first_unit[name] = chunk, unit
        for j in range(n):
            if per:
                unit += per
                released.append(("gemm", unit))
            elif j < n - 1:
                down += 1
                released.append(("down", down))
            else:
                unit += 4
                released.append(("gemm", unit))
        chunk += n
        if name == "v":
            first_unit["na_o"], first_unit["y"] = unit, unit + 4
            unit += 6
    small, at = {}, 0
    for name, n in SMALL:
        small[name] = at
        at += n
    return first_chunk, first_unit, released, small


GC, GU, RELEASED, SU = plan()
ROOTS = [(0, 2), (2, 8), (8, 56), (0, 2), (0, 2), (8, 40), (0, 2), (0, 2), (0, 2), (0, 2), (0, 2), (0, 2)]


def causal_order():
    seq = [("S", 0), ("S", 1)]
    for h in range(H):
        seq.append(("P", h))
        if h + 2 < H:
            seq.append(("S", h + 2))
        seq.append(("O", h))
    return seq, {x: n for n, x in enumerate(seq)}


def window_order():
    seq = [("S", 0), ("S", 1)]
    for i in range(2 * H):
        seq.append(("P", i))
        if i + 2 < 2 * H:
            seq.append(("S", i + 2))
        if i % 2 == 0 and i:
            seq.append(("O", i // 2 - 1))
    seq.append(("O", H - 1))
    units, n = {}, 0
    for kind, i in seq:
        if kind != "O":
            units[(kind, i)] = n
            n += 1
    return seq, units


def spread(ap, at, n):
    dims = [list(x) for x in ap.ap]
    dims.insert(1 + at, [0, n])
    return bass.AP(ap.tensor, ap.offset, dims)


def program(nc, weights, x_in, ctx_in, cols_in, rows_in, consts_in, select_in, pos_col_in, pos_row_in, rpb_in, out):
    with ExitStack() as stack:
        def sbuf(name, shape, dt=F32):
            return stack.enter_context(nc.sbuf_tensor(name, shape, dt))

        def sem(name):
            return stack.enter_context(nc.semaphore(name))

        ring = sbuf("ring", [P, 2, SLOT])
        x = sbuf("x", [P, 2, D])
        hT = sbuf("hT", [P, KD, 2 * T])
        work = sbuf("work", [P, 8192])
        bias = sbuf("bias", [P, 4096])
        gates = sbuf("gates", [P, 2, D])
        stage = sbuf("stage", [P, 4096])
        arena = sbuf("arena", [P, 14000])
        cols = sbuf("cols", [P, CA[None]])
        rows = sbuf("rows", [P, RA[None]])
        consts = sbuf("consts", [P, KA[None]])
        stat = sbuf("stat", [P, 384])
        half = sbuf("half", [P, 48])
        posc = sbuf("posc", [P, 2], I32)
        posr = sbuf("posr", [P, T], I32)
        posf = sbuf("posf", [P, 2])
        rot = sbuf("rot", [P, 2, 2, 32])
        adac = sbuf("adac", [P, 80])
        sc = sbuf("sc", [P, 2, 8])
        ps = [stack.enter_context(nc.psum_tensor(f"bank{i}", [P, 512], F32)) for i in range(8)]

        def col(name, a=0, n=None):
            n = COLS[name] - a if n is None else n
            return cols[:, CA[name] + a:CA[name] + a + n]

        def row(name, a=0, n=None):
            n = ROWS[name] - a if n is None else n
            return rows[:, RA[name] + a:RA[name] + a + n]

        def const(name, a=0, n=None):
            n = CONSTS[name] - a if n is None else n
            return consts[:, KA[name] + a:KA[name] + a + n]

        def view(buf, at, *shape):
            n = int(np.prod(shape))
            flat = buf[:, at:at + n]
            if len(shape) == 1:
                return flat
            names = "abcd"[:len(shape)]
            return flat.rearrange(f"p ({' '.join(names)}) -> p {' '.join(names)}", **dict(zip(names, shape)))

        att = work[:, 0:4096]
        xn = view(work, 4096, 2, D)
        OT = view(work, 6144, KD, T)
        part = view(work, 0, 16, 512)
        ident = const("ident")
        q0 = view(arena, 0, 2, H * 192)
        kv = view(arena, 3072, 2, H * 256)
        qnT = view(arena, 7168, H, T)
        knT = view(arena, 9216, H, T)
        qpT = view(arena, 11264, 4, T)
        kpT = view(arena, 12288, T)
        kpe2 = view(arena, 12544, 2, 128)
        proj = view(arena, 7168, 2, 704)
        cT = view(arena, 8576, 5, T)
        qkv = view(arena, 0, 2, 3 * D)
        q1T = view(arena, 6144, H, T)
        k1T = view(arena, 8192, H, T)
        aT = arena[:, 0:32 * T]
        ctx = view(arena, 10240, 2, D)
        nqk = view(arena, 0, 2, 2 * NA)
        nv = view(arena, 2048, 2, NA)
        ncv = view(arena, 3072, 2, NA)
        sz = view(arena, 4096, 2, NA)
        nqT = view(arena, 5120, 4, T)
        nkT = view(arena, 6144, 4, 2 * T)
        BT = view(arena, 8192, 2, 2 * T)
        CT = view(arena, 9216, 2, T)
        xsr = view(arena, 9728, 2, NA)
        cxsr = view(arena, 10752, 2, NA)
        Bcr = view(arena, 11776, 2, 2, P)
        E = view(arena, 12288, 2, 768)
        Wm = view(arena, 0, 2, 768)
        xsT = view(work, 4096, 4, 2 * T)
        hflat = hT[:, :, :].rearrange("p a b -> p (a b)")
        xw = hflat[:, 0:2048].rearrange("p (l d n) -> p l d n", l=2, d=2)
        h0T = hflat[:, 2048:3072].rearrange("p (d n) -> p d n", d=2)
        yrow = hflat[:, 3072:4096].rearrange("p (t n) -> p t n", t=2)
        select = stage[0:16, 0:2048]
        cbm = view(stage, 2048, 2, 768)
        cum = stage[0:16, 3584:4096]
        gact = view(arena, 8192, 2, 2, T)
        uT = arena[:, 0:KF2 * T]

        x_in_sb = sem("x_loaded")
        ctx_in_sb = sem("ctx_loaded")
        params_in = sem("params_loaded")
        select_in_sb = sem("select_loaded")
        rpb_loaded = sem("rpb_loaded")
        w_ready = [sem(f"w_ready{i}") for i in range(2)]
        gemm_ready, down_used = sem("gemm_ready"), sem("down_used")
        gemm_free = [sem(f"gemm_free{i}") for i in range(4)]
        small_ready = sem("small_ready")
        small_free = [sem(f"small_free{i}") for i in range(4)]
        dve_step, act_step, pool_step = sem("dve_step"), sem("act_step"), sem("pool_step")
        normed = sem("rows_normed")
        latents_normed, heads_normed = sem("latents_normed"), sem("heads_normed")
        sq_ready, sq_used = sem("squares_ready"), sem("squares_used")
        angles, rotations = sem("angles_ready"), sem("rotations_ready")
        max_ready, exp_done, probs_ready = sem("max_ready"), sem("exp_done"), sem("probs_ready")
        squared = sem("relu_squared")
        silu_c = sem("silu_c")
        ada_in = [sem(f"ada_in{i}") for i in range(2)]
        ada_used = sem("ada_used")
        means_ready, roots_ready, half_set = sem("means_ready"), sem("roots_ready"), sem("half_set")
        conv_mid, conv_act = sem("conv_centre"), sem("conv_activated")
        sp_abs, sp_exp, sp_u, sp_ln = (sem("softplus_" + n) for n in ("abs", "exp", "one_plus", "ln"))
        a_exp, dA_ready, ecum_ready = sem("a_exp"), sem("dA_ready"), sem("exp_cum")
        later_exp, xw_ready, seg_exp = sem("later_exp"), sem("xw_ready"), sem("seg_exp")
        w_mat, y_used, nqk_ready = sem("mask_matrix_ready"), sem("mask_matrix_used"), sem("nqk_rotated")
        glu_mid, glu_act = sem("glu_centre"), sem("glu_activated")
        out_ready, stored = sem("out_ready"), sem("stored")

        def gbank(u):
            return ps[u % 4]

        def sbank(u):
            return ps[4 + u % 4]

        def gemm_out(eng, u, i=None):
            eng.wait_ge(gemm_ready, u + 1 if i is None else 4 * i + (u + 1))

        def gemm_gone(eng, u):
            eng.wait_ge(gemm_free[u % 4], u // 4 + 1)

        def small_out(eng, u):
            eng.wait_ge(small_ready, u + 1)

        def small_gone(eng, u):
            eng.wait_ge(small_free[u % 4], u // 4 + 1)

        class Steps:

            def __init__(self, eng, semaphore):
                self.eng, self.sem, self.n, self.turn = eng, semaphore, 0, 0

            def step(self, ins):
                ins.then_inc(self.sem, 1)
                self.n += 1

            def settle(self):
                self.eng.wait_ge(self.sem, self.n + self.turn)

            def enter(self, i, per):
                self.turn, self.per, self.before = per * i, per, self.n

            def leave(self, turns):
                assert self.n == self.before + self.per
                self.turn, self.n = 0, self.before + self.per * turns

        seq_c, unit_c = causal_order()
        seq_w, unit_w = window_order()
        block = stack.enter_context(nc.Block())

        @block.sync
        def _(sp):
            sp.dma_start(x[:, :, :], x_in).then_inc(x_in_sb, 16)

            def release_sem(kind):
                return gemm_ready if kind == "gemm" else down_used

            def load(name, c, j):
                if c >= 2:
                    kind, value = RELEASED[c - 2]
                    sp.wait_ge(release_sem(kind), value)
                w = weights[name]
                sp.dma_start(ring[:, c % 2, 0:w.shape[2]], w[j]).then_inc(w_ready[c % 2], 16)

            def load_all(name, n):
                for j in range(n):
                    load(name, GC[name] + j, j)

            def load_loop(name, n):
                c0 = GC[name]
                load(name, c0, 0)
                load(name, c0 + 1, 1)
                w = weights[name]
                with sp.Fori(1, n // 2) as i:
                    for u in range(2):
                        kind, value = RELEASED[c0 + u]
                        step = RELEASED[c0 + u + 2][1] - value if n > 4 else 0
                        sp.wait_ge(release_sem(kind), step * i + (value - step))
                        sp.dma_start(ring[:, (c0 + u) % 2, 0:w.shape[2]], w[2 * i + u])\
                            .then_inc(w_ready[(c0 + u) % 2], 16)
                if n % 2:
                    load(name, c0 + n - 1, n - 1)

            load_all("mla_in", 2)
            load_all("mla_uq", 2)
            load_all("mla_ukv", 2)
            load_all("mla_o", 2)
            load_loop("up0", 8)
            load_all("down0", 8)
            load_loop("qkv", 6)
            load_all("moba_o", 2)
            load_loop("up1", 8)
            sp.wait_ge(gemm_ready, GU["up1"])
            sp.dma_start(ctx, ctx_in).then_inc(ctx_in_sb, 16)
            small_out(sp, SU["m1"] - 1)
            sp.dma_start(bias[:, :], rpb_in).then_inc(rpb_loaded, 16)
            load_all("down1", 8)
            sp.wait_ge(ada_used, 24)
            sp.dma_start(select, select_in).then_inc(select_in_sb, 16)
            for name in ("dt", "xs", "bc", "q", "k", "z", "v"):
                load_all(name, 1)
            load_all("out", 2)
            load_loop("glu", 11)
            load_all("down2", 6)
            for t in range(2):
                sp.wait_ge(out_ready, t + 1)
                sp.dma_start(out[:, t, :], xn[:, t, :]).then_inc(stored, 16)
            sp.wait_ge(stored, 32)

        @block.gpsimd
        def _(pool):
            pool.memset(half[:, :], -0.5).then_inc(half_set, 1)
            pool.wait_ge(half_set, 1)

            def roots(first, last):
                for n in range(first, last):
                    a, b = ROOTS[n]
                    pool.wait_ge(means_ready, n + 1)
                    pool.tensor_tensor(stat[:, a:b], stat[:, a:b], half[:, 0:b - a], ALU.pow).then_inc(roots_ready, 1)

            for j in range(2):
                pool.dma_start(stage[:, 2048 * j:2048 * j + 2048], weights["ada"][j]).then_inc(ada_in[j], 16)
            roots(0, 8)
            with pool.Fori(1, 12) as i:
                for u in range(2):
                    pool.wait_ge(ada_used, 2 * i + (u - 1))
                    pool.dma_start(stage[:, 2048 * u:2048 * u + 2048], weights["ada"][2 * i + u])\
                        .then_inc(ada_in[u], 16)
            roots(8, len(ROOTS))

        @block.tensor
        def _(pe):
            def small_start(u):
                if u >= 4:
                    pe.wait_ge(small_free[u % 4], u // 4)

            def gemm_start(u, i=None):
                if u >= 4:
                    pe.wait_ge(gemm_free[u % 4], u // 4 if i is None else i + u // 4)

            def weights_in(c, i=None):
                pe.wait_ge(w_ready[c % 2], 16 * (c // 2 + 1) if i is None else 16 * i + 16 * (c // 2 + 1))

            def flip(u, pieces):
                small_start(u)
                for at, src in pieces:
                    k, m = src.shape[0], src.shape[1]
                    ins = pe.transpose(sbank(u)[0:m, at:at + k], src, ident[0:k, 0:k])
                ins.then_inc(small_ready, 1)

            def rows_to_cols(name, count):
                for t in range(2):
                    pe.wait_ge(normed, count + t + 1)
                    for half in range(2):
                        flip(SU[name] + 2 * t + half,
                             [(P * f, xn[:, t, (4 * half + f) * P:(4 * half + f + 1) * P]) for f in range(4)])

            def rows_gemm(name, chunks, lhs, kts, width, piece):
                u = GU[name]
                for j in range(chunks):
                    c = GC[name] + j
                    weights_in(c)
                    w = view(ring[:, c % 2, :], 0, kts, width)
                    for a in range(0, width, piece):
                        for t in range(2):
                            gemm_start(u)
                            for k in range(kts):
                                ins = pe.matmul(gbank(u)[:, 0:piece], lhs(k, t), w[:, k, a:a + piece],
                                                start=k == 0, stop=k == kts - 1)
                            ins.then_inc(gemm_ready, 1)
                            u += 1

            def x_tile(k, t):
                return hT[:, k, t * P:(t + 1) * P]

            def c_tile(k, t):
                return hT[:, k, T + t * P:T + (t + 1) * P]

            def up(name):
                c0, u0 = GC[name], GU[name]
                with pe.Fori(0, 4) as i:
                    for j in range(2):
                        weights_in(c0 + j, i)
                        w = view(ring[:, (c0 + j) % 2, :], 0, KD, 512)
                        for pair in range(2):
                            u = u0 + 2 * j + pair
                            gemm_start(u, i)
                            for f in range(2):
                                for k in range(KD):
                                    ins = pe.matmul(gbank(u)[:, f * T:(f + 1) * T],
                                                    w[:, k, (2 * pair + f) * P:(2 * pair + f + 1) * P],
                                                    hT[:, k, 0:T], start=k == 0, stop=k == KD - 1)
                            ins.then_inc(gemm_ready, 1)

            def down(name, chunks, tiles, hidden, inputs_in, before_last=None):
                u0 = GU[name]
                for u in range(u0, u0 + 4):
                    gemm_start(u)
                for j in range(chunks):
                    c = GC[name] + j
                    if before_last and j == chunks - 1:
                        before_last()
                    weights_in(c)
                    inputs_in(j)
                    w = view(ring[:, c % 2, :], 0, 4, D)
                    n = min(4, tiles - 4 * j)
                    for half in range(2):
                        for t in range(2):
                            for k in range(n):
                                kt = 4 * j + k
                                ins = pe.matmul(gbank(u0 + 2 * half + t)[:, :],
                                                hidden[:, kt * T + t * P:kt * T + (t + 1) * P],
                                                w[:, k, half * 512:(half + 1) * 512],
                                                start=kt == 0, stop=kt == tiles - 1)
                            if j == chunks - 1:
                                ins.then_inc(gemm_ready, 1)
                    if j < chunks - 1:
                        ins.then_inc(down_used, 1)

            def causal_attention(name, scores, value, count):
                for kind, h in seq_c:
                    u = SU[name] + unit_c[(kind, h)]
                    if kind == "S":
                        small_start(u)
                        scores(u, h)
                    elif kind == "P":
                        pe.wait_ge(probs_ready, count + h + 1)
                        pr = att[:, 1024 + 512 * (h % 2):1024 + 512 * (h % 2) + 384]
                        flip(u, [(0, pr[:, 256:384]), (P, pr[:, 0:128]), (2 * P, pr[:, 128:256])])
                    else:
                        small_gone(pe, SU[name] + unit_c[("P", h)])
                        small_start(u)
                        pt = att[:, 2048 + 1024 * (h % 2):2048 + 1024 * (h % 2) + 384]
                        pe.matmul(sbank(u)[:, 0:T], value(0, h), pt[:, 0:T], start=True, stop=False)
                        pe.matmul(sbank(u)[:, P:T], value(1, h), pt[:, T:384], start=False, stop=True)\
                            .then_inc(small_ready, 1)

            pe.wait_ge(params_in, 80)
            rows_to_cols("h0", 0)
            for u in range(4):
                small_gone(pe, SU["h0"] + u)
            rows_gemm("mla_in", 2, x_tile, KD, 352, 352)
            pe.wait_ge(latents_normed, 1)
            for n, fs in enumerate(((0, 1), (2, 3), (4,))):
                flip(SU["cT"] + n, [(T * a + P * t, proj[:, t, f * P:(f + 1) * P])
                                    for a, f in enumerate(fs) for t in range(2)])
            for u in range(3):
                small_gone(pe, SU["cT"] + u)
            rows_gemm("mla_uq", 2, lambda k, t: cT[:, k, t * P:(t + 1) * P], 3, 768, 384)
            rows_gemm("mla_ukv", 2, lambda k, t: cT[:, 3 + k, t * P:(t + 1) * P], 2, 1024, 512)
            pe.wait_ge(heads_normed, 1)
            flip(SU["kpe"], [(P * t, kpe2[:, t, :]) for t in range(2)])
            for n in range(4):
                flip(SU["qn"] + n, [(T * a + P * t, q0[:, t, (2 * n + a) * 192:(2 * n + a) * 192 + NOPE])
                                    for a in range(2) for t in range(2)])
            for n in range(4):
                flip(SU["kn"] + n, [(T * a + P * t, kv[:, t, (2 * n + a) * 256:(2 * n + a) * 256 + NOPE])
                                    for a in range(2) for t in range(2)])
            pe.wait_ge(heads_normed, 2)
            for n in range(2):
                flip(SU["qp"] + n, [(T * a + P * t, xn[:, t, (2 * n + a) * P:(2 * n + a + 1) * P])
                                    for a in range(2) for t in range(2)])
            for u in range(SU["kpe"], SU["qp"] + 2):
                small_gone(pe, u)

            def scores0(u, h):
                a = 64 * (h % 2)
                b = sbank(u)
                pe.matmul(b[:, 0:T], qnT[:, h, P:T], knT[:, h, :], start=True, stop=False)
                pe.matmul(b[:, 0:T], qpT[a:a + 64, h // 2, P:T], kpT[a:a + 64, :], start=False, stop=True)
                pe.matmul(b[:, T:384], qnT[:, h, 0:P], knT[:, h, 0:P], start=True, stop=False)
                pe.matmul(b[:, T:384], qpT[a:a + 64, h // 2, 0:P], kpT[a:a + 64, 0:P], start=False, stop=True)\
                    .then_inc(small_ready, 1)

            causal_attention("att0", scores0, lambda t, h: kv[:, t, h * 256 + NOPE:(h + 1) * 256], 0)
            for h in range(H):
                small_gone(pe, SU["att0"] + unit_c[("O", h)])
            o_tile = lambda k, t: OT[:, k, t * P:(t + 1) * P]
            rows_gemm("mla_o", 2, o_tile, KD, 512, 512)
            rows_to_cols("m0", 2)
            for u in range(4):
                small_gone(pe, SU["m0"] + u)
            up("up0")
            down("down0", 8, 32, aT, lambda j: pe.wait_ge(squared, 2 * j + 2))
            rows_to_cols("h1", 4)
            for u in range(4):
                small_gone(pe, SU["h1"] + u)
            c0, u0 = GC["qkv"], GU["qkv"]
            with pe.Fori(0, 3) as i:
                for j in range(2):
                    weights_in(c0 + j, i)
                    w = view(ring[:, (c0 + j) % 2, :], 0, KD, 512)
                    for t in range(2):
                        u = u0 + 2 * j + t
                        gemm_start(u, i)
                        for k in range(KD):
                            ins = pe.matmul(gbank(u)[:, :], x_tile(k, t), w[:, k, :], start=k == 0, stop=k == KD - 1)
                        ins.then_inc(gemm_ready, 1)
            pe.wait_ge(heads_normed, 3)
            for n in range(8):
                flip(SU["q1"] + n, [(T * a + P * t, qkv[:, t, (2 * n + a) * P:(2 * n + a + 1) * P])
                                    for a in range(2) for t in range(2)])
            for u in range(SU["q1"], SU["q1"] + 8):
                small_gone(pe, u)

            def scores1(u, h):
                b = sbank(u)
                pe.matmul(b[:, 0:T], q1T[:, h, P:T], k1T[:, h, :], start=True, stop=True)
                pe.matmul(b[:, T:384], q1T[:, h, 0:P], k1T[:, h, 0:P], start=True, stop=True)\
                    .then_inc(small_ready, 1)

            causal_attention("att1", scores1, lambda t, h: qkv[:, t, 2 * D + h * P:2 * D + (h + 1) * P], H)
            for h in range(H):
                small_gone(pe, SU["att1"] + unit_c[("O", h)])
            rows_gemm("moba_o", 2, o_tile, KD, 512, 512)
            rows_to_cols("m1", 6)
            for u in range(4):
                small_gone(pe, SU["m1"] + u)
            up("up1")

            def ada_sums():
                pe.wait_ge(ada_used, 24)
                u = SU["ada"]
                small_start(u)
                n = 0
                for chunk in (0, 1, 2, 3, 6, 7, 8, 9, 12, 13, 14, 15):
                    for f in range(4):
                        ins = pe.matmul(sbank(u)[:, n:n + 1], part[:, chunk, f * P:(f + 1) * P], const("ones", 0, 1),
                                        start=True, stop=True)
                        n += 1
                ins.then_inc(small_ready, 1)
                for g, chunk in enumerate((4, 5, 10, 11)):
                    small_start(u + 1 + g)
                    pe.matmul(sbank(u + 1 + g)[:, :], const("ones"), part[:, chunk, :], start=True, stop=True)\
                        .then_inc(small_ready, 1)

            down("down1", 8, 32, aT, lambda j: pe.wait_ge(squared, 16 + 2 * j + 2), ada_sums)

            pe.wait_ge(normed, 10)
            for t in range(2):
                for half in range(2):
                    flip(SU["hc"] + 2 * t + half,
                         [(P * f, ctx[:, t, (4 * half + f) * P:(4 * half + f + 1) * P]) for f in range(4)])
            rows_to_cols("hx", 10)
            for u in range(SU["hx"], SU["hx"] + 4):
                small_gone(pe, u)

            def one_chunk(name, width):
                c = GC[name]
                weights_in(c)
                return view(ring[:, c % 2, :], 0, KD, width)

            def row_units(u, w, tiles):
                for n, (tile, t) in enumerate(tiles):
                    gemm_start(u + n)
                    for k in range(KD):
                        ins = pe.matmul(gbank(u + n)[:, :], tile(k, t), w[:, k, :], start=k == 0, stop=k == KD - 1)
                    ins.then_inc(gemm_ready, 1)

            def col_units(u, w, feats, a, n):
                for i, f in enumerate(feats):
                    gemm_start(u + i)
                    for k in range(KD):
                        ins = pe.matmul(gbank(u + i)[:, 0:n], w[:, k, f * P:(f + 1) * P], hT[:, k, a:a + n],
                                        start=k == 0, stop=k == KD - 1)
                    ins.then_inc(gemm_ready, 1)

            both = [(x_tile, 0), (x_tile, 1), (c_tile, 0), (c_tile, 1)]
            w = one_chunk("dt", 16)
            gemm_start(GU["dt"])
            for n, (tile, t) in enumerate(both):
                for k in range(KD):
                    ins = pe.matmul(gbank(GU["dt"])[:, 16 * n:16 * n + 16], tile(k, t), w[:, k, :],
                                    start=k == 0, stop=k == KD - 1)
            ins.then_inc(gemm_ready, 1)
            col_units(GU["xs"], one_chunk("xs", 512), range(4), 0, 2 * T)
            w = one_chunk("bc", 512)
            col_units(GU["bc"], w, (0, 1), 0, 2 * T)
            col_units(GU["bc"] + 2, w, (2, 3), 0, T)
            row_units(GU["q"], one_chunk("q", 512), both[:2])
            w = one_chunk("k", 512)
            row_units(GU["k"], w, both[:2])
            for pair in range(2):
                u = GU["k"] + 2 + pair
                gemm_start(u)
                for f in range(2):
                    for k in range(KD):
                        ins = pe.matmul(gbank(u)[:, f * T:(f + 1) * T],
                                        w[:, k, (2 * pair + f) * P:(2 * pair + f + 1) * P], hT[:, k, T:2 * T],
                                        start=k == 0, stop=k == KD - 1)
                ins.then_inc(gemm_ready, 1)
            row_units(GU["z"], one_chunk("z", 512), both[:2])
            row_units(GU["v"], one_chunk("v", 512), both)

            pe.wait_ge(dA_ready, 1)
            dA = lambda t: stat[:, 160 + 16 * t:176 + 16 * t]
            u = SU["cum"]
            small_start(u)
            b = sbank(u)
            pe.matmul(b[0:16, 0:T], dA(0), const("upto"), start=True, stop=False)
            pe.matmul(b[0:16, P:T], dA(1), const("upto", 0, P), start=False, stop=True)
            pe.matmul(b[0:16, T:2 * T], dA(1), const("since"), start=True, stop=False)
            pe.matmul(b[0:16, T:T + P], dA(0), const("since", P, P), start=False, stop=True).then_inc(small_ready, 1)
            small_gone(pe, u)
            u = SU["cumcol"]
            small_start(u)
            for n in range(4):
                ins = pe.transpose(sbank(u)[:, 16 * n:16 * n + 16], cum[:, P * n:P * n + P], ident[0:16, 0:16])
            ins.then_inc(small_ready, 1)
            u = SU["later"]
            small_start(u)
            b = sbank(u)
            for n, (parts) in enumerate((
                    [("after", 0), ("ones", 1)], [("before", 0)], [("after", 1)], [("before", 1), ("ones", 0)])):
                for m, (tri, t) in enumerate(parts):
                    ins = pe.matmul(b[:, 16 * n:16 * n + 16], const(tri), dA(2 + t), start=m == 0,
                                    stop=m == len(parts) - 1)
            ins.then_inc(small_ready, 1)
            pe.wait_ge(conv_act, 8)
            for t in range(2):
                flip(SU["xsrow"] + t, [(P * f, xsT[:, f, t * P:(t + 1) * P]) for f in range(4)])
            for t in range(2):
                flip(SU["xsrow"] + 2 + t, [(P * f, xsT[:, f, T + t * P:T + (t + 1) * P]) for f in range(4)])
            flip(SU["xsrow"] + 4, [(P * (2 * t + g), BT[:, g, T + t * P:T + (t + 1) * P])
                                   for t in range(2) for g in range(2)])
            small_gone(pe, SU["xsrow"] + 4)
            pe.wait_ge(xw_ready, 4)
            for d in range(2):
                u = SU["state"] + d
                small_start(u)
                for g in range(2):
                    for t in range(2):
                        ins = pe.matmul(sbank(u)[:, g * 256:(g + 1) * 256], Bcr[:, t, g, :],
                                        xw[:, t, d, g * 256:(g + 1) * 256], start=t == 0, stop=t == 1)
                ins.then_inc(small_ready, 1)
            for g in range(2):
                u = SU["cb"] + g
                small_start(u)
                for t in range(2):
                    ins = pe.matmul(sbank(u)[:, t * T:(t + 1) * T], BT[:, g, t * P:(t + 1) * P], CT[:, g, :],
                                    start=True, stop=True)
                ins.then_inc(small_ready, 1)
            pe.wait_ge(nqk_ready, 1)
            for n in range(2):
                flip(SU["nq"] + n, [(T * a + P * t, nqk[:, t, (2 * n + a) * P:(2 * n + a + 1) * P])
                                    for a in range(2) for t in range(2)])
            for n in range(2):
                flip(SU["nk"] + n, [(T * a + P * t, nqk[:, t, NA + (2 * n + a) * P:NA + (2 * n + a + 1) * P])
                                    for a in range(2) for t in range(2)])
            for u in range(SU["nq"], SU["nq"] + 4):
                small_gone(pe, u)
            for u in range(GU["k"] + 2, GU["k"] + 4):
                gemm_gone(pe, u)
            for u in range(GU["v"], GU["v"] + 4):
                gemm_gone(pe, u)
            for kind, i in seq_w:
                if kind == "S":
                    u = SU["na"] + unit_w[(kind, i)]
                    h, t = i // 2, i % 2
                    a = 64 * (h % 2)
                    small_start(u)
                    pe.matmul(sbank(u)[:, :], nqT[a:a + 64, h // 2, t * P:(t + 1) * P], nkT[a:a + 64, h // 2, :],
                              start=True, stop=True).then_inc(small_ready, 1)
                elif kind == "P":
                    pe.wait_ge(probs_ready, 2 * H + i + 1)
                    pr = att[:, 1024 + 512 * (i % 2):1536 + 512 * (i % 2)]
                    flip(SU["na"] + unit_w[(kind, i)], [(P * k, pr[:, P * k:P * k + P]) for k in range(4)])
                else:
                    u = GU["na_o"] + i // 2
                    a = 64 * (i % 2)
                    for t in range(2):
                        small_gone(pe, SU["na"] + unit_w[("P", 2 * i + t)])
                    if i % 2 == 0:
                        gemm_start(u)
                    pt = view(att, 2048 + 1024 * (i % 2), 4, T)
                    for k in range(4):
                        val = (nv if k < 2 else ncv)[:, k % 2, i * 64:(i + 1) * 64]
                        ins = pe.matmul(gbank(u)[a:a + 64, 0:T], val, pt[:, k, :], start=k == 0, stop=k == 3)
                    if i % 2:
                        ins.then_inc(gemm_ready, 1)
            pe.wait_ge(select_in_sb, 16)
            for u in range(2):
                small_gone(pe, SU["xsrow"] + u)

            def segment(h):
                u = SU["seg"] + h
                small_start(u)
                for d in range(2):
                    ins = pe.matmul(sbank(u)[:, d * T:(d + 1) * T], select[:, (8 * d + h) * P:(8 * d + h + 1) * P],
                                    cum[:, d * T:(d + 1) * T], start=True, stop=True)
                ins.then_inc(small_ready, 1)

            segment(0)
            segment(1)
            yu = GU["y"]
            for u in (yu, yu + 1):
                gemm_start(u)
            for h in range(H):
                pe.wait_ge(w_mat, h + 1)
                wm = Wm[:, h % 2, :]
                for t, parts in enumerate(([(0, 0), (384, 0), (512, 1)], [(128, 0), (256, 1), (640, 1)])):
                    for m, (at, tile) in enumerate(parts):
                        ins = pe.matmul(gbank(yu + t)[:, h * 64:(h + 1) * 64], wm[:, at:at + P],
                                        xsr[:, tile, h * 64:(h + 1) * 64], start=m == 0, stop=m == 2)
                    if h == H - 1:
                        ins.then_inc(gemm_ready, 1)
                if h < H - 1:
                    ins.then_inc(y_used, 1)
                if h + 2 < H:
                    segment(h + 2)
            for d in range(2):
                small_gone(pe, SU["state"] + d)
            for t in range(2):
                for d in range(2):
                    u = SU["yoff"] + 2 * t + d
                    small_start(u)
                    for g in range(2):
                        ins = pe.matmul(sbank(u)[:, g * 256:(g + 1) * 256], CT[:, g, t * P:(t + 1) * P],
                                        h0T[:, d, g * 256:(g + 1) * 256], start=True, stop=True)
                    ins.then_inc(small_ready, 1)
            pe.wait_ge(normed, 13)
            for n in range(2):
                flip(SU["yT"] + n, [(T * a + P * t, yrow[:, t, (2 * n + a) * P:(2 * n + a + 1) * P])
                                    for a in range(2) for t in range(2)])
            for n in range(2):
                small_gone(pe, SU["yT"] + n)
            for p in range(4):
                gemm_gone(pe, GU["na_o"] + p)
            rows_gemm("out", 2, o_tile, KD, 512, 512)
            rows_to_cols("m2", 13)
            for u in range(4):
                small_gone(pe, SU["m2"] + u)
            c0, u0 = GC["glu"], GU["glu"]

            def glu_chunk(j, i=None):
                weights_in(c0 + j, i)
                w = view(ring[:, (c0 + j) % 2, :], 0, KD, 512)
                for part_ in range(2):
                    u = u0 + 2 * j + part_
                    gemm_start(u, i)
                    for f in range(2):
                        for k in range(KD):
                            ins = pe.matmul(gbank(u)[:, f * T:(f + 1) * T],
                                            w[:, k, (2 * part_ + f) * P:(2 * part_ + f + 1) * P], hT[:, k, 0:T],
                                            start=k == 0, stop=k == KD - 1)
                    ins.then_inc(gemm_ready, 1)

            with pe.Fori(0, 5) as i:
                for j in range(2):
                    glu_chunk(j, i)
            glu_chunk(10)
            down("down2", 6, KF2, uT, lambda j: gemm_gone(pe, u0 + 2 * min(2 * j + 1, 10) + 1))

        @block.scalar
        def _(act):
            st = Steps(act, act_step)
            for dst, src in ((cols[:, :], cols_in), (rows[:, :], rows_in), (consts[:, :], consts_in),
                             (posc[:, :], pos_col_in), (posr[:, :], pos_row_in)):
                act.dma_start(dst, src).then_inc(params_in, 16)

            def copy(out_, in_, scale=None):
                if scale is None:
                    return act.activation(out_, in_, ACT.Copy)
                return act.activation(out_, in_, ACT.Copy, scale=scale)

            def empty(u, dst, n=512, scale=None, a=0):
                gemm_out(act, u)
                src = gbank(u)[:, a:a + n]
                copy(dst, src, scale).then_inc(gemm_free[u % 4], 1)

            def small_empty(u, dst, n=512, scale=None):
                small_out(act, u)
                copy(dst, sbank(u)[:, 0:n], scale).then_inc(small_free[u % 4], 1)

            def pair(buf, n):
                return buf[:, 2 * n:2 * n + 2, 0:T]

            def halves(u, n=2, m=T):
                return sbank(u)[:, 0:n * m].rearrange("p (a b) -> p a b", a=n)

            def pair_empty(u, dst, scale=None):
                small_out(act, u)
                copy(dst, halves(u), scale).then_inc(small_free[u % 4], 1)

            act.wait_ge(params_in, 80)
            act.activation(sc[:, :, :], col("c", 0, 16).rearrange("p (a b) -> p a b", a=2), ACT.Silu)\
                .then_inc(silu_c, 1)
            act.wait_ge(angles, 1)
            act.activation(rot[:, :, :, :].rearrange("p a b c -> p (a b c)"), att[:, 3072:3200], ACT.Sin)\
                .then_inc(rotations, 1)
            for n in range(4):
                empty(GU["mla_in"] + n, proj[:, n % 2, 352 * (n // 2):352 * (n // 2) + 352], 352)
            n = 0
            for name, dst, each in (("mla_uq", q0, 192), ("mla_ukv", kv, 256)):
                for m in range(8):
                    u, t, p = GU[name] + m, m % 2, m // 2
                    gemm_out(act, u)
                    if n >= 2:
                        act.wait_ge(sq_used, n - 1)
                    w = 192 if each == 192 else NOPE
                    src = gbank(u)[:, 0:2 * each].rearrange("p (a b) -> p a b", a=2)[:, :, 0:w]
                    sq = att[:, 512 * (n % 2):512 * (n % 2) + 2 * w].rearrange("p (a b) -> p a b", a=2)
                    act.activation(sq, src, ACT.Square).then_inc(sq_ready, 1)
                    copy(dst[:, t, 2 * each * p:2 * each * (p + 1)], gbank(u)[:, 0:2 * each])\
                        .then_inc(gemm_free[u % 4], 1)
                    n += 1
            small_empty(SU["kpe"], kpT, T)
            for n in range(4):
                pair_empty(SU["qn"] + n, pair(qnT, n), col("q_nope"))
            for n in range(4):
                pair_empty(SU["kn"] + n, pair(knT, n), col("k_nope"))
            for n in range(2):
                pair_empty(SU["qp"] + n, pair(qpT, n))

            def causal_attention(name, count):
                def probabilities(h):
                    b = h % 2
                    act.wait_ge(max_ready, count + h + 1)
                    for tile, a, n in ((1, 0, 256), (0, 256, 128)):
                        ins = act.activation(att[:, 1024 + 512 * b + a:1024 + 512 * b + a + n],
                                             att[:, 512 * b + a:512 * b + a + n], ACT.Exp,
                                             bias=stat[:, 56 + 2 * b + tile:57 + 2 * b + tile],
                                             accum_out=stat[:, 60 + 2 * b + tile:61 + 2 * b + tile])
                    ins.then_inc(exp_done, 1)

                def transposed(h):
                    u = SU[name] + unit_c[("P", h)]
                    small_empty(u, att[:, 2048 + 1024 * (h % 2):2048 + 1024 * (h % 2) + 384], 384)

                def head_out(h):
                    small_empty(SU[name] + unit_c[("O", h)], OT[:, h, :], T)

                for h in range(H + 2):
                    if h < H:
                        probabilities(h)
                    if 1 <= h <= H:
                        transposed(h - 1)
                    if h >= 2:
                        head_out(h - 2)

            causal_attention("att0", 0)

            def relu(name):
                u0 = GU[name]
                with act.Fori(0, 4) as i:
                    for m in range(4):
                        u = u0 + m
                        gemm_out(act, u, i)
                        act.activation(aT[:, bass.ds(i * 2048 + 512 * m, 512)], gbank(u)[:, :], ACT.Relu)\
                            .then_inc(gemm_free[u % 4], 1)

            relu("up0")
            u0 = GU["qkv"]
            with act.Fori(0, 2) as i:
                for m in range(4):
                    u = u0 + m
                    gemm_out(act, u, i)
                    act.wait_ge(sq_used, 4 * i + (15 + m))
                    act.activation(att[:, 512 * (m % 2):512 * (m % 2) + 512], gbank(u)[:, :], ACT.Square)\
                        .then_inc(sq_ready, 1)
                    copy(qkv[:, m % 2, bass.ds(i * 1024 + 512 * (m // 2), 512)], gbank(u)[:, :])\
                        .then_inc(gemm_free[u % 4], 1)
            for m in range(4):
                empty(u0 + 8 + m, qkv[:, m % 2, 2048 + 512 * (m // 2):2560 + 512 * (m // 2)])
            for n in range(4):
                pair_empty(SU["q1"] + n, pair(q1T, n), col("moba_q"))
            for n in range(4):
                pair_empty(SU["k1"] + n, pair(k1T, n), col("moba_k"))
            causal_attention("att1", H)
            relu("up1")

            act.wait_ge(sp_abs, 1)
            tmp = lambda k: arena[:, 12288 + 64 * k:12352 + 64 * k]
            act.activation(tmp(2), tmp(1), ACT.Exp, scale=-1.0).then_inc(sp_exp, 1)
            act.activation(stat[:, 80:96], row("a_log"), ACT.Exp).then_inc(a_exp, 1)
            act.wait_ge(sp_u, 1)
            act.activation(tmp(4), tmp(3), ACT.Ln).then_inc(sp_ln, 1)
            conv_units = [(GU["xs"] + f, xsT[:, f, :], 512) for f in range(4)] \
                + [(GU["bc"] + g, BT[:, g, :], 512) for g in range(2)] \
                + [(GU["bc"] + 2 + g, CT[:, g, :], 256) for g in range(2)]
            for n in range(9):
                if n < 8:
                    u, y, m = conv_units[n]
                    gemm_out(act, u)
                    act.activation(y, gbank(u)[:, 0:m], ACT.Identity, scale=col("conv_w", 3 * n + 1, 1),
                                   bias=col("conv_b", n, 1)).then_inc(conv_mid, 1)
                if n:
                    u, y, m = conv_units[n - 1]
                    gemm_gone(act, u)
                    act.activation(y, y, ACT.Silu).then_inc(conv_act, 1)
            for pr in range(2):
                u = GU["k"] + 2 + pr
                gemm_out(act, u)
                copy(nkT[:, 2 * pr:2 * pr + 2, T:2 * T], gbank(u)[:, :].rearrange("p (a b) -> p a b", a=2))\
                    .then_inc(gemm_free[u % 4], 1)
            for t in range(2):
                u = GU["z"] + t
                gemm_out(act, u)
                act.activation(sz[:, t, :], gbank(u)[:, :], ACT.Silu).then_inc(gemm_free[u % 4], 1)
            for m in range(4):
                empty(GU["v"] + m, (nv if m < 2 else ncv)[:, m % 2, :])
            small_gone(act, SU["cumcol"])
            act.activation(stat[:, 320:384], stat[:, 256:320], ACT.Exp).then_inc(ecum_ready, 1)
            u = SU["later"]
            small_out(act, u)
            act.activation(tmp(7), sbank(u)[:, 0:64], ACT.Exp).then_inc(small_free[u % 4], 1)
            for n in range(5):
                dst = (xsr[:, 0], xsr[:, 1], cxsr[:, 0], cxsr[:, 1], Bcr[:, :, :, :].rearrange("p a b c -> p (a b c)"))[n]
                small_empty(SU["xsrow"] + n, dst)
            for d in range(2):
                small_empty(SU["state"] + d, h0T[:, d, :])
            for n in range(2):
                pair_empty(SU["nq"] + n, pair(nqT, n), 0.125)
            for n in range(2):
                pair_empty(SU["nk"] + n, pair(nkT, n))
            for i in range(2 * H + 1):
                if i < 2 * H:
                    u = SU["na"] + unit_w[("S", i)]
                    act.wait_ge(max_ready, 2 * H + i + 1)
                    act.activation(att[:, 1024 + 512 * (i % 2):1536 + 512 * (i % 2)], sbank(u)[:, :], ACT.Exp,
                                   bias=stat[:, 56 + i % 2:57 + i % 2], accum_out=stat[:, 60 + i % 2:61 + i % 2])\
                        .then_inc(small_free[u % 4], 1)
                if i:
                    h, t = (i - 1) // 2, (i - 1) % 2
                    u = SU["na"] + unit_w[("P", i - 1)]
                    small_out(act, u)
                    copy(view(att, 2048 + 1024 * (h % 2), 4, T)[:, :, t * P:(t + 1) * P], halves(u, 4, P))\
                        .then_inc(small_free[u % 4], 1)
                if i >= 8 and i % 4 == 0 and i < 2 * H:
                    empty(GU["na_o"] + i // 4 - 2, OT[:, i // 4 - 2, :], T)
            for p in (2, 3):
                empty(GU["na_o"] + p, OT[:, p, :], T)
            for h in range(H):
                small_gone(act, SU["seg"] + h)
                act.activation(E[:, h % 2, :], E[:, h % 2, :], ACT.Exp).then_inc(seg_exp, 1)
            for n in range(2):
                u = SU["yT"] + n
                small_out(act, u)
                for a in range(2):
                    ins = copy(OT[:, 4 + 2 * n + a, :], sbank(u)[:, T * a:T * (a + 1)],
                               col("ssd_norm", 2 * n + a, 1))
                ins.then_inc(small_free[u % 4], 1)

            u0 = GU["glu"]

            def glu_chunk(j, i=None):
                b = j % 2
                gate, value = u0 + 2 * j, u0 + 2 * j + 1
                k = 0 if i is None else i
                gemm_out(act, gate, i)
                act.wait_ge(gemm_free[value % 4], value // 4 + k)
                for f in range(2):
                    n = 2 * j + f
                    w = cols[:, bass.ds(12 * k + (CA["fconv_w"] + 3 * n + 1), 1)]
                    bb = cols[:, bass.ds(4 * k + (CA["fconv_b"] + n), 1)]
                    ins = act.activation(gact[:, b, f, :], gbank(gate)[:, T * f:T * (f + 1)], ACT.Identity,
                                         scale=w, bias=bb)
                ins.then_inc(glu_mid, 1)
                act.wait_ge(gemm_free[gate % 4], gate // 4 + 1 + k)
                act.activation(gact[:, b, :, :], gact[:, b, :, :], ACT.Silu).then_inc(glu_act, 1)

            with act.Fori(0, 5) as i:
                for j in range(2):
                    glu_chunk(j, i)
            glu_chunk(10)

        @block.vector
        def _(v):
            st = Steps(v, dve_step)
            step, settle = st.step, st.settle
            roots = []

            def inverse_rms(at, widths):
                a = at
                for n, width in widths:
                    ins = v.tensor_scalar(stat[:, a:a + n], stat[:, a:a + n], 1.0 / width, EPS, ALU.mult, ALU.add)
                    a += n
                    if (n, width) != widths[-1] or a - at != sum(w[0] for w in widths):
                        step(ins)
                ins.then_inc(means_ready, 1)
                roots.append((at, a))
                assert roots[-1] == ROOTS[len(roots) - 1]
                v.wait_ge(roots_ready, len(roots))

            def sum_squares(src, junk, at):
                step(v.tensor_tensor_reduce(out=junk, in0=src, in1=src, scale=1.0, scalar=0.0, op0=ALU.mult,
                                            op1=ALU.add, accum_out=stat[:, at:at + 1]))

            def norm_rows(src, dst, junk):
                for t in range(2):
                    sum_squares(src[:, t, :], junk[:, t, :], t)
                settle()
                inverse_rms(0, [(2, D)])
                for t in range(2):
                    v.tensor_scalar(dst[:, t, :], src[:, t, :], stat[:, t:t + 1], None, ALU.mult).then_inc(normed, 1)

            def quarters(u):
                return sbank(u)[:, :].rearrange("p (a b) -> p a b", a=4)

            def to_hT(name, gain, shift=None, at=0):
                for t in range(2):
                    for half in range(2):
                        u = SU[name] + 2 * t + half
                        dst = hT[:, 4 * half:4 * half + 4, at + t * P:at + (t + 1) * P]
                        small_out(v, u)
                        g = spread(gain[:, 4 * half:4 * half + 4], 1, P)
                        ins = v.tensor_tensor(dst, quarters(u), g, ALU.mult)
                        if shift is not None:
                            step(ins)
                            settle()
                            ins = v.tensor_tensor(dst, dst, spread(shift[:, 4 * half:4 * half + 4], 1, P), ALU.add)
                        ins.then_inc(small_free[u % 4], 1)

            def add_to_x(name, units, gate=None):
                for n in range(4):
                    u, half, t = units + n, n // 2, n % 2
                    dst = x[:, t, 512 * half:512 * (half + 1)]
                    gemm_out(v, u)
                    if gate is None:
                        v.tensor_tensor(dst, gbank(u)[:, :], dst, ALU.add).then_inc(gemm_free[u % 4], 1)
                        gemm_gone(v, u)
                    else:
                        tmp = att[:, 512 * n:512 * (n + 1)]
                        v.tensor_tensor(tmp, gbank(u)[:, :], gates[:, gate, 512 * half:512 * (half + 1)], ALU.mult)\
                            .then_inc(gemm_free[u % 4], 1)
                        gemm_gone(v, u)
                        step(v.tensor_tensor(dst, dst, tmp, ALU.add))
                settle()

            v.wait_ge(x_in_sb, 16)
            norm_rows(x, xn, xn)
            v.wait_ge(params_in, 80)
            ang, turns, sines, cosines = (att[:, a:a + 64] for a in (2944, 3008, 3136, 3072))
            step(v.tensor_copy(posf[:, :], posc[:, :]))
            settle()
            for t in range(2):
                step(v.tensor_scalar(ang[:, 32 * t:32 * t + 32], const("inv_freq"), posf[:, t:t + 1], None, ALU.mult))
            settle()
            step(v.tensor_scalar(turns, ang, 1.0 / (2 * math.pi), MAGIC, ALU.mult, ALU.add))
            settle()
            step(v.tensor_scalar(turns, turns, MAGIC, None, ALU.subtract))
            settle()
            rest = 2 * math.pi
            for bits in (3, 14, 34):
                part_ = math.floor(rest * 2 ** (bits + 2)) / 2 ** (bits + 2) if bits < 34 else rest
                rest -= part_
                step(v.scalar_tensor_tensor(ang, turns, -part_, ang, ALU.mult, ALU.add))
                settle()
            pi32 = 3.1415925
            step(v.tensor_scalar(sines, ang, pi32, -pi32, ALU.min, ALU.max))
            settle()
            step(v.scalar_tensor_tensor(cosines, sines, -1.0, sines, ALU.mult, ALU.min))
            settle()
            v.tensor_scalar(cosines, cosines, math.pi / 2, None, ALU.add).then_inc(angles, 1)
            to_hT("h0", col("attn_norm", 0, 8))
            for u in range(4):
                gemm_gone(v, GU["mla_in"] + u)
            widths = ((0, QR), (QR, KVR), (QR + KVR, ROPE))
            for s_, (a, n) in enumerate(widths):
                for t in range(2):
                    sum_squares(proj[:, t, a:a + n], xn[:, t, a:a + n], 2 + 2 * s_ + t)
            settle()
            inverse_rms(2, [(2, n) for _, n in widths])
            for s_, (a, n) in enumerate(widths[:2]):
                for t in range(2):
                    ins = v.tensor_scalar(proj[:, t, a:a + n], proj[:, t, a:a + n],
                                          stat[:, 2 + 2 * s_ + t:3 + 2 * s_ + t], None, ALU.mult)
                    if (s_, t) == (1, 1):
                        ins.then_inc(latents_normed, 1)
                    else:
                        step(ins)
            kp = [proj[:, t, QR + KVR:QR + KVR + ROPE] for t in range(2)]
            for t in range(2):
                step(v.scalar_tensor_tensor(kp[t], kp[t], stat[:, 6 + t:7 + t], row("k_rope"), ALU.mult, ALU.mult))
            settle()
            v.wait_ge(rotations, 1)
            kpv = proj[:, :, QR + KVR:QR + KVR + ROPE]
            kt = [view(att, 2048 + 64 * k, 2, 32) for k in range(4)]
            for k, (a, r) in enumerate(((0, 0), (1, 1), (1, 0), (0, 1))):
                step(v.tensor_tensor(kt[k], kpv[:, :, 32 * a:32 * a + 32], rot[:, r, :, :], ALU.mult))
            settle()
            step(v.tensor_tensor(kpe2[:, :, 0:32], kt[0], kt[1], ALU.subtract))
            step(v.tensor_tensor(kpe2[:, :, 32:64], kt[2], kt[3], ALU.add))
            settle()
            step(v.tensor_copy(kpe2[:, :, 64:128], kpe2[:, :, 0:64]))
            for n, fs in enumerate((2, 2, 1)):
                u = SU["cT"] + n
                small_out(v, u)
                v.tensor_tensor(cT[:, 2 * n:2 * n + fs, :], sbank(u)[:, 0:T * fs].rearrange("p (a b) -> p a b", a=fs),
                                spread(col("c_norm", 2 * n, fs), 1, T), ALU.mult).then_inc(small_free[u % 4], 1)
            for n in range(16):
                t, p = n % 2, n % 8 // 2
                v.wait_ge(sq_ready, n + 1)
                w = 192 if n < 8 else NOPE
                sq = att[:, 512 * (n % 2):512 * (n % 2) + 2 * w].rearrange("p (a b) -> p a b", a=2)
                at = (8 if n < 8 else 40) + 8 * t + 2 * p
                if n < 8:
                    step(v.tensor_reduce(stat[:, at + 16:at + 18], sq[:, :, NOPE:192], AX.X, ALU.add))
                v.tensor_reduce(stat[:, at:at + 2], sq[:, :, 0:NOPE], AX.X, ALU.add).then_inc(sq_used, 1)
            v.wait_ge(sq_used, 16)
            settle()
            inverse_rms(8, [(16, NOPE), (16, ROPE), (16, NOPE)])
            for u in range(8):
                gemm_gone(v, GU["mla_uq"] + u)
                gemm_gone(v, GU["mla_ukv"] + u)
            qh = q0[:, :, :].rearrange("p t (h d) -> p (t h) d", d=192)
            kh = kv[:, :, :].rearrange("p t (h d) -> p (t h) d", d=256)
            step(v.tensor_tensor(qh[:, :, 0:NOPE], qh[:, :, 0:NOPE], spread(stat[:, 8:24], 1, NOPE), ALU.mult))
            v.tensor_tensor(kh[:, :, 0:NOPE], kh[:, :, 0:NOPE], spread(stat[:, 40:56], 1, NOPE), ALU.mult)\
                .then_inc(heads_normed, 1)
            qp = qh[:, :, NOPE:192]
            step(v.tensor_tensor(qp, qp, spread(stat[:, 24:40], 1, ROPE), ALU.mult))
            settle()
            step(v.tensor_tensor(qp, qp, spread(row("q_rope"), 0, 16), ALU.mult))
            settle()
            qr = q0[:, :, :].rearrange("p t (h d) -> p t h d", d=192)
            xr = xn[:, :, 0:512].rearrange("p t (h d) -> p t h d", d=64)
            tm = [view(att, 2048 + 512 * k, 2, 8, 32) for k in range(4)]
            for k, (a, r) in enumerate(((0, 0), (1, 1), (1, 0), (0, 1))):
                for t in range(2):
                    step(v.tensor_tensor(tm[k][:, t], qr[:, t, :, NOPE + 32 * a:NOPE + 32 * a + 32],
                                         spread(rot[:, r, t, :], 0, 8), ALU.mult))
            settle()
            for t in range(2):
                step(v.tensor_tensor(xr[:, t, :, 0:32], tm[0][:, t], tm[1][:, t], ALU.subtract))
                ins = v.tensor_tensor(xr[:, t, :, 32:64], tm[2][:, t], tm[3][:, t], ALU.add)
                if t:
                    ins.then_inc(heads_normed, 1)
                else:
                    step(ins)

            def causal_attention(name, scale, bias_of, count):
                def logits(h):
                    b = h % 2
                    u = SU[name] + unit_c[("S", h)]
                    small_out(v, u)
                    lg = att[:, 512 * b:512 * b + 384]
                    v.scalar_tensor_tensor(lg, sbank(u)[:, 0:384], scale, bias_of(h), ALU.mult, ALU.add)\
                        .then_inc(small_free[u % 4], 1)
                    small_gone(v, u)
                    step(v.tensor_reduce(stat[:, 57 + 2 * b:58 + 2 * b], lg[:, 0:256], AX.X, ALU.max, negate=True))
                    v.tensor_reduce(stat[:, 56 + 2 * b:57 + 2 * b], lg[:, 256:384], AX.X, ALU.max, negate=True)\
                        .then_inc(max_ready, 1)

                def normalise(h):
                    b = h % 2
                    v.wait_ge(exp_done, count + h + 1)
                    step(v.reciprocal(stat[:, 64 + 2 * b:66 + 2 * b], stat[:, 60 + 2 * b:62 + 2 * b]))
                    settle()
                    pr = att[:, 1024 + 512 * b:1024 + 512 * b + 384]
                    step(v.tensor_scalar(pr[:, 0:256], pr[:, 0:256], stat[:, 65 + 2 * b:66 + 2 * b], None, ALU.mult))
                    v.tensor_scalar(pr[:, 256:384], pr[:, 256:384], stat[:, 64 + 2 * b:65 + 2 * b], None, ALU.mult)\
                        .then_inc(probs_ready, 1)

                for h in range(H + 1):
                    if h < H:
                        logits(h)
                    if h:
                        normalise(h - 1)

            causal_attention("att0", 1.0 / math.sqrt(NOPE + ROPE), lambda h: const("causal"), 0)
            add_to_x("mla_o", GU["mla_o"])
            norm_rows(x, xn, xn)
            to_hT("m0", col("mlp_norm", 0, 8))

            def squares(name):
                u0 = GU[name]
                with v.Fori(0, 4) as i:
                    for m in range(4):
                        u = u0 + m
                        v.wait_ge(gemm_free[u % 4], i + (u // 4 + 1))
                        a = aT[:, bass.ds(i * 2048 + 512 * m, 512)]
                        v.tensor_tensor(a, a, a, ALU.mult).then_inc(squared, 1)

            squares("up0")
            dist, above, deltas = bias[:, 3072:3456], bias[:, 3456:3840], bias[:, 3840:4096]
            table = row("table")
            step(v.tensor_scalar(dist[:, 0:256], posr[:, :], -1.0, posf[:, 1:2], ALU.mult, ALU.add))
            step(v.tensor_scalar(dist[:, 256:384], posr[:, 0:P], -1.0, posf[:, 0:1], ALU.mult, ALU.add))
            step(v.tensor_tensor(deltas[:, H:], table[:, H:], table[:, 0:-H], ALU.subtract))
            for h in range(H):
                step(v.tensor_scalar(bias[:, 384 * h:384 * h + 384], const("causal"), table[:, h:h + 1], None, ALU.add))
            settle()
            with v.Fori(1, BUCKETS) as b:
                base = st.n
                v.wait_ge(dve_step, (H + 1) * b + (base - H - 1))
                v.tensor_scalar(above, dist, const("thresholds")[:, bass.ds(b, 1)], None, ALU.is_ge)\
                    .then_inc(dve_step, 1)
                v.wait_ge(dve_step, (H + 1) * b + (base - H))
                for h in range(H):
                    acc = bias[:, 384 * h:384 * h + 384]
                    v.scalar_tensor_tensor(acc, above, deltas[:, bass.ds(H * b + h, 1)], acc, ALU.mult, ALU.add)\
                        .then_inc(dve_step, 1)
            st.n = base + (H + 1) * (BUCKETS - 1)
            settle()
            add_to_x("down0", GU["down0"])
            norm_rows(x, xn, xn)
            to_hT("h1", col("attn_norm", 8, 8))
            with v.Fori(0, 2) as i:
                for m in range(4):
                    v.wait_ge(sq_ready, 4 * i + (17 + m))
                    sq = att[:, 512 * (m % 2):512 * (m % 2) + 512].rearrange("p (a b) -> p a b", a=4)
                    v.tensor_reduce(stat[:, bass.ds(8 * i + (8 + 16 * (m % 2) + 4 * (m // 2)), 4)], sq, AX.X, ALU.add)\
                        .then_inc(sq_used, 1)
            v.wait_ge(sq_used, 24)
            inverse_rms(8, [(32, P)])
            for u in range(12):
                gemm_gone(v, GU["qkv"] + u)
            for t in range(2):
                qk = qkv[:, t, 0:2 * D].rearrange("p (h d) -> p h d", d=P)
                ins = v.tensor_tensor(qk, qk, spread(stat[:, 8 + 16 * t:24 + 16 * t], 1, P), ALU.mult)
                if t:
                    ins.then_inc(heads_normed, 1)
                else:
                    step(ins)
            causal_attention("att1", 1.0 / math.sqrt(P), lambda h: bias[:, 384 * h:384 * h + 384], H)
            add_to_x("moba_o", GU["moba_o"])
            norm_rows(x, xn, xn)
            to_hT("m1", col("mlp_norm", 8, 8))
            v.wait_ge(ctx_in_sb, 16)
            norm_rows(ctx, ctx, xn)
            squares("up1")
            v.wait_ge(silu_c, 1)

            def ada_chunk(i, with_ctx, base):
                for half in range(2):
                    v.wait_ge(ada_in[half], 16 * i + 16)
                    for kk in range(4):
                        k = 4 * half + kk
                        w = stage[:, 2048 * half + 512 * kk:2048 * half + 512 * (kk + 1)]
                        outs = [(0, i * 512)] + ([(1, i * 512 + 12 * 512)] if with_ctx else [])
                        if kk == 0 and half:
                            v.wait_ge(ada_used, 2 * i + 1)
                        elif k:
                            settle()
                        for who, at in outs:
                            dst = work[:, bass.ds(at, 512)]
                            if k == 0:
                                ins = v.tensor_scalar(dst, w, sc[:, who, 0:1], None, ALU.mult)
                            else:
                                ins = v.scalar_tensor_tensor(dst, w, sc[:, who, k:k + 1], dst, ALU.mult, ALU.add)
                            if kk == 3 and (who, at) == outs[-1]:
                                ins.then_inc(ada_used, 1)
                            else:
                                step(ins)

            with v.Fori(0, 4) as i:
                st.enter(i, 14)
                ada_chunk(i, True, None)
            st.leave(4)
            with v.Fori(4, 12) as i:
                st.enter(i, 6)
                st.turn = 6 * i - 24
                ada_chunk(i, False, None)
            st.leave(8)
            u = SU["ada"]
            small_out(v, u)
            step(v.tensor_tensor(adac[:, 0:32], sbank(u)[:, 0:32], col("ada_cols"), ALU.add))
            v.tensor_tensor(adac[:, 32:48], sbank(u)[:, 32:48], col("ada_cols", 0, 16), ALU.add)\
                .then_inc(small_free[u % 4], 1)
            settle()
            small_gone(v, u)
            for dst, scale, gain in ((48, 8, "norm1"), (56, 24, "norm2"), (64, 40, "norm1")):
                step(v.scalar_tensor_tensor(adac[:, dst:dst + 8], adac[:, scale:scale + 8], 1.0, col(gain),
                                            ALU.add, ALU.mult))
            for g in range(4):
                u = SU["ada"] + 1 + g
                small_out(v, u)
                v.tensor_tensor(gates[:, g // 2, 512 * (g % 2):512 * (g % 2) + 512], sbank(u)[:, :],
                                row("ada_g", 512 * g, 512), ALU.add).then_inc(small_free[u % 4], 1)
            settle()
            for g in range(4):
                small_gone(v, SU["ada"] + 1 + g)
            add_to_x("down1", GU["down1"])

            norm_rows(x, xn, xn)
            to_hT("hc", adac[:, 64:72], adac[:, 32:40], T)
            to_hT("hx", adac[:, 48:56], adac[:, 0:8])
            tmp = lambda k: arena[:, 12288 + 64 * k:12352 + 64 * k]
            z_, az, ez, uz, lz, se, mk = (tmp(k) for k in range(7))
            dt = stat[:, 96:160]
            u = GU["dt"]
            gemm_out(v, u)
            v.tensor_tensor(z_.rearrange("p (a b) -> p a b", a=4), gbank(u)[:, 0:64].rearrange("p (a b) -> p a b", a=4),
                            spread(row("dt_bias"), 0, 4), ALU.add).then_inc(gemm_free[u % 4], 1)
            gemm_gone(v, u)
            v.scalar_tensor_tensor(az, z_, -1.0, z_, ALU.mult, ALU.max).then_inc(sp_abs, 1)
            v.wait_ge(sp_exp, 1)
            v.tensor_scalar(uz, ez, 1.0, None, ALU.add).then_inc(sp_u, 1)
            step(v.tensor_scalar(se, ez, 1.0 / 3, -0.5, ALU.mult, ALU.add))
            step(v.tensor_scalar(mk, ez, 0.01, None, ALU.is_lt))
            settle()
            step(v.tensor_tensor(se, se, ez, ALU.mult))
            settle()
            step(v.scalar_tensor_tensor(se, se, 1.0, ez, ALU.add, ALU.mult))
            settle()
            v.wait_ge(sp_ln, 1)
            for op, b in ((ALU.subtract, lz), (ALU.mult, mk), (ALU.add, lz)):
                step(v.tensor_tensor(se, se, b, op))
                settle()
            step(v.scalar_tensor_tensor(dt, z_, 0.0, se, ALU.max, ALU.add))
            settle()
            v.wait_ge(a_exp, 1)
            v.scalar_tensor_tensor(stat[:, 160:224].rearrange("p (a b) -> p a b", a=4), dt.rearrange("p (a b) -> p a b", a=4),
                                   -1.0, spread(stat[:, 80:96], 0, 4), ALU.mult, ALU.mult).then_inc(dA_ready, 1)
            conv_units = [(GU["xs"] + f, xsT[:, f, :], 2) for f in range(4)] \
                + [(GU["bc"] + g, BT[:, g, :], 2) for g in range(2)] + [(GU["bc"] + 2 + g, CT[:, g, :], 1) for g in range(2)]
            for n, (u, y, m) in enumerate(conv_units):
                v.wait_ge(conv_mid, n + 1)
                y = y.rearrange("p (a b) -> p a b", a=m)
                src = gbank(u)[:, 0:m * T].rearrange("p (a b) -> p a b", a=m)
                step(v.scalar_tensor_tensor(y[:, :, 1:T], src[:, :, 0:T - 1], col("conv_w", 3 * n, 1), y[:, :, 1:T],
                                            ALU.mult, ALU.add))
                settle()
                v.scalar_tensor_tensor(y[:, :, 0:T - 1], src[:, :, 1:T], col("conv_w", 3 * n + 2, 1), y[:, :, 0:T - 1],
                                       ALU.mult, ALU.add).then_inc(gemm_free[u % 4], 1)
            for n in range(4):
                u, t, kind = (GU["q"] if n < 2 else GU["k"]) + n % 2, n % 2, n // 2
                gemm_out(v, u)
                src = gbank(u)[:, :].rearrange("p (h d) -> p h d", d=64)
                tm = [view(att, 2048 + 1024 * (n % 2) + 256 * k, 8, 32) for k in range(4)]
                grid = const("grid")
                for k, (a, r) in enumerate(((0, 0), (1, 1), (1, 0), (0, 1))):
                    ins = v.tensor_tensor(tm[k], src[:, :, 32 * a:32 * a + 32],
                                          spread(grid[:, 64 * t + 32 * r:64 * t + 32 * r + 32], 0, 8), ALU.mult)
                    if k == 3:
                        ins.then_inc(gemm_free[u % 4], 1)
                    else:
                        step(ins)
                settle()
                gemm_gone(v, u)
                dst = nqk[:, t, NA * kind:NA * (kind + 1)].rearrange("p (h d) -> p h d", d=64)
                step(v.tensor_tensor(dst[:, :, 0:32], tm[0], tm[1], ALU.subtract))
                ins = v.tensor_tensor(dst[:, :, 32:64], tm[2], tm[3], ALU.add)
                if n == 3:
                    ins.then_inc(nqk_ready, 1)
                else:
                    step(ins)
            u = SU["cum"]
            small_out(v, u)
            v.tensor_copy(cum, sbank(u)[0:16, :]).then_inc(small_free[u % 4], 1)
            u = SU["cumcol"]
            small_out(v, u)
            v.tensor_copy(stat[:, 256:320], sbank(u)[:, 0:64]).then_inc(small_free[u % 4], 1)
            small_gone(v, SU["later"])
            lx = tmp(7).rearrange("p (l d h) -> p l d h", l=2, d=2)
            wl = tmp(8)[:, 0:32].rearrange("p (l d h) -> p l d h", l=2, d=2)
            dtv = dt.rearrange("p (a b) -> p a b", a=4)
            for d in range(2):
                step(v.tensor_tensor(wl[:, :, d, :], lx[:, :, d, 8 * d:8 * d + 8], dtv[:, 2:4, 8 * d:8 * d + 8], ALU.mult))
            settle()
            for t in range(2):
                small_gone(v, SU["xsrow"] + 2 + t)
            for t in range(2):
                for d in range(2):
                    v.tensor_tensor(xw[:, t, d, :].rearrange("p (h q) -> p h q", q=64),
                                    cxsr[:, t, :].rearrange("p (h q) -> p h q", q=64),
                                    spread(wl[:, t, d, :], 1, 64), ALU.mult).then_inc(xw_ready, 1)
            for g in range(2):
                u = SU["cb"] + g
                small_out(v, u)
                b = sbank(u)
                upto, since = const("upto", 0, P), const("since", P, P)
                step(v.tensor_tensor(cbm[:, g, 0:128], b[:, 0:128], upto, ALU.mult))
                step(v.tensor_copy(cbm[:, g, 128:256], b[:, 128:256]))
                step(v.tensor_tensor(cbm[:, g, 256:384], b[:, 384:512], upto, ALU.mult))
                step(v.tensor_tensor(cbm[:, g, 384:512], b[:, 0:128], since, ALU.mult))
                step(v.tensor_copy(cbm[:, g, 512:640], b[:, 256:384]))
                v.tensor_tensor(cbm[:, g, 640:768], b[:, 384:512], since, ALU.mult).then_inc(small_free[u % 4], 1)
            v.wait_ge(rpb_loaded, 16)

            def window_logits(i):
                h, t, b = i // 2, i % 2, i % 2
                u = SU["na"] + unit_w[("S", i)]
                small_out(v, u)
                bs = bias[:, (8 * t + h) * T:(8 * t + h + 1) * T]
                step(v.tensor_tensor(sbank(u)[:, 0:T], sbank(u)[:, 0:T], bs, ALU.add))
                settle()
                v.tensor_reduce(stat[:, 56 + b:57 + b], sbank(u)[:, :], AX.X, ALU.max, negate=True)\
                    .then_inc(max_ready, 1)

            def window_normalise(i):
                b = i % 2
                small_gone(v, SU["na"] + unit_w[("S", i)])
                step(v.reciprocal(stat[:, 64 + b:65 + b], stat[:, 60 + b:61 + b]))
                settle()
                pr = att[:, 1024 + 512 * b:1536 + 512 * b]
                v.tensor_scalar(pr, pr, stat[:, 64 + b:65 + b], None, ALU.mult).then_inc(probs_ready, 1)

            for i in range(2 * H + 1):
                if i < 2 * H:
                    window_logits(i)
                if i:
                    window_normalise(i - 1)

            parts = ((0, 256, 0, 0), (256, 384, 128, 1), (384, 512, 256, 0), (512, 768, 256, 1))

            def decay(h):
                u = SU["seg"] + h
                small_out(v, u)
                for n, (a, e, src, t) in enumerate(parts):
                    c = 256 + 16 * t + h if n < 2 else 256 + 32 + 16 * t + 8 + h
                    ins = v.tensor_scalar(E[:, h % 2, a:e], sbank(u)[:, src:src + e - a], stat[:, c:c + 1], 0.0,
                                          ALU.subtract, ALU.min)
                    if n == 3:
                        ins.then_inc(small_free[u % 4], 1)
                    else:
                        step(ins)

            def matrix(h):
                v.wait_ge(seg_exp, h + 1)
                if h >= 2:
                    v.wait_ge(y_used, h - 1)
                for n, (a, e, src, t) in enumerate(parts):
                    c = 96 + 16 * t + h if n < 2 else 96 + 16 * t + 8 + h
                    ins = v.scalar_tensor_tensor(Wm[:, h % 2, a:e], E[:, h % 2, a:e], stat[:, c:c + 1],
                                                 cbm[:, h // 4, a:e], ALU.mult, ALU.mult)
                    if n == 3:
                        ins.then_inc(w_mat, 1)
                    else:
                        step(ins)

            for g in range(2):
                small_gone(v, SU["cb"] + g)
            small_gone(v, SU["cumcol"])
            settle()
            decay(0)
            for h in range(H):
                if h + 1 < H:
                    decay(h + 1)
                matrix(h)
            v.wait_ge(ecum_ready, 1)
            for t in range(2):
                small_gone(v, SU["xsrow"] + t)
            heads = lambda ap: ap.rearrange("p (h q) -> p h q", q=64)
            for t in range(2):
                step(v.tensor_tensor(heads(yrow[:, t, :]), heads(xsr[:, t, :]), spread(row("ssd_d"), 1, 64), ALU.mult))
            settle()
            for t in range(2):
                u = GU["y"] + t
                gemm_out(v, u)
                v.tensor_tensor(yrow[:, t, :], gbank(u)[:, :], yrow[:, t, :], ALU.add).then_inc(gemm_free[u % 4], 1)
                gemm_gone(v, u)
                for d in range(2):
                    u = SU["yoff"] + 2 * t + d
                    tm = att[:, 512 * d:512 * (d + 1)]
                    small_out(v, u)
                    c = 320 + 32 * d + 16 * t + 8 * d
                    v.tensor_tensor(heads(tm), heads(sbank(u)[:, :]), spread(stat[:, c:c + 8], 1, 64), ALU.mult)\
                        .then_inc(small_free[u % 4], 1)
                    small_gone(v, u)
                    step(v.tensor_tensor(yrow[:, t, :], yrow[:, t, :], tm, ALU.add))
                    settle()
                step(v.tensor_tensor(yrow[:, t, :], yrow[:, t, :], sz[:, t, :], ALU.mult))
            settle()
            for t in range(2):
                sum_squares(yrow[:, t, :], att[:, 512 * t:512 * (t + 1)], t)
            settle()
            inverse_rms(0, [(2, NA)])
            for t in range(2):
                ins = v.tensor_scalar(yrow[:, t, :], yrow[:, t, :], stat[:, t:t + 1], None, ALU.mult)
                if t:
                    ins.then_inc(normed, 1)
                else:
                    step(ins)
            add_to_x("out", GU["out"], 0)
            norm_rows(x, xn, xn)
            to_hT("m2", adac[:, 56:64], adac[:, 16:24])
            u0 = GU["glu"]

            def glu_chunk(j, i=None):
                b = j % 2
                gate, value = u0 + 2 * j, u0 + 2 * j + 1
                k = 0 if i is None else i
                v.wait_ge(glu_mid, 2 * k + (j + 1))
                for f in range(2):
                    for tap in (0, 2):
                        w = cols[:, bass.ds(12 * k + (CA["fconv_w"] + 3 * (2 * j + f) + tap), 1)]
                        y = gact[:, b, f, 1:T] if tap == 0 else gact[:, b, f, 0:T - 1]
                        src = gbank(gate)[:, T * f:T * f + T - 1] if tap == 0 else gbank(gate)[:, T * f + 1:T * f + T]
                        if tap:
                            settle()
                        ins = v.scalar_tensor_tensor(y, src, w, y, ALU.mult, ALU.add)
                        if (f, tap) == (1, 2):
                            ins.then_inc(gemm_free[gate % 4], 1)
                        else:
                            step(ins)
                v.wait_ge(glu_act, 2 * k + (j + 1))
                gemm_out(v, value, i)
                v.tensor_tensor(uT[:, bass.ds(k * 1024 + 2 * j * T, 2 * T)], gbank(value)[:, :],
                                gact[:, b, :, :].rearrange("p a b -> p (a b)"), ALU.mult)\
                    .then_inc(gemm_free[value % 4], 1)

            with v.Fori(0, 5) as i:
                st.enter(i, 6)
                for j in range(2):
                    glu_chunk(j, i)
            st.leave(5)
            glu_chunk(10)
            add_to_x("down2", GU["down2"], 1)
            for t in range(2):
                sum_squares(x[:, t, :], xn[:, t, :], t)
            settle()
            inverse_rms(0, [(2, D)])
            for t in range(2):
                v.scalar_tensor_tensor(xn[:, t, :], x[:, t, :], stat[:, t:t + 1], row("final"), ALU.mult, ALU.mult)\
                    .then_inc(out_ready, 1)



def t5_thresholds():
    n = np.arange(1, 4096)
    exact = BUCKETS // 2
    large = exact + (np.log(n.astype(np.float32) / np.float32(exact)) / np.float32(math.log(1024 / exact))
                     * np.float32(BUCKETS - exact)).astype(np.int32)
    bucket = np.where(n < exact, n, np.minimum(large, BUCKETS - 1))
    return np.array([0] + [n[bucket >= b][0] for b in range(1, BUCKETS)], np.float32)


def constants():
    i = np.arange(P)
    upto = (i[:, None] <= i[None, :]).astype(np.float32)
    one = np.ones((P, P), np.float32)
    c = np.zeros((P, KA[None]), np.float32)

    def put(name, a):
        c[:, KA[name]:KA[name] + CONSTS[name]] = a

    mask = np.where(i[None, :] <= i[:, None], 0.0, NEG)
    put("ident", np.eye(P))
    put("upto", np.concatenate([upto, one], 1))
    put("since", np.concatenate([one, upto.T], 1))
    put("after", (i[:, None] > i[None, :]))
    put("before", (i[:, None] < i[None, :]))
    put("ones", one)
    put("causal", np.concatenate([np.zeros((P, P)), mask, mask], 1))
    tok = np.arange(T)
    freqs = np.float32(10000.0) ** (-np.arange(16, dtype=np.float32) / np.float32(16))
    ang = np.concatenate([(tok // 64).astype(np.float32)[:, None] * freqs, (tok % 64).astype(np.float32)[:, None] * freqs], 1)
    grid = np.stack([np.cos(ang), np.sin(ang)], 1)
    put("grid", grid.reshape(2, P, 64).transpose(1, 0, 2).reshape(P, 128))
    put("inv_freq", np.float32(10000.0) ** (-np.arange(0, 64, 2, dtype=np.float32) / np.float32(64)))
    put("thresholds", t5_thresholds())
    select = np.zeros((16, 16, P), np.float32)
    select[np.arange(16), np.arange(16)] = 1.0
    return c, select.reshape(16, 16 * P)


def kernel(**inputs):
    import concourse.bacc as bacc
    from concourse.bass_utils import run_bass_kernel_spmd as run

    g = {k: np.asarray(a) for k, a in inputs.items()}

    def chunks(w, kts, width):
        k, n = w.shape
        w = w.reshape(k // (P * kts), kts, P, n // width, width)
        return np.ascontiguousarray(w.transpose(0, 3, 2, 1, 4).reshape(-1, P, kts * width))

    w2 = g["w_in_2"][0]
    up, nf = g["ffn_w_up_2"][0], FF2 // 256
    glu = np.concatenate([chunks(up[:, :FF2], KD, 256).reshape(nf, P, KD, 256),
                          chunks(up[:, FF2:], KD, 256).reshape(nf, P, KD, 256)], 3).reshape(nf, P, SLOT)
    down2 = np.concatenate([g["ffn_w_down_2"][0], np.zeros((2 * P, D), np.float32)], 0)
    ada = g["ada_w_2"][0].reshape(2, 4, P, 12, 512).transpose(3, 0, 2, 1, 4).reshape(24, P, 2048)
    weights = {
        "mla_in": chunks(g["mla_w_in"][0], 8, 352), "mla_uq": chunks(g["mla_w_uq"][0], 3, 768),
        "mla_ukv": chunks(g["mla_w_ukv"][0], 2, 1024), "mla_o": chunks(g["mla_w_o"][0], 8, 512),
        "up0": chunks(g["mlp_w_in"][0], 8, 512), "down0": chunks(g["mlp_w_out"][0], 4, D),
        "qkv": chunks(g["moba_w_qkv"][0], 8, 512), "moba_o": chunks(g["moba_w_o"][0], 8, 512),
        "up1": chunks(g["mlp_w_in"][1], 8, 512), "down1": chunks(g["mlp_w_out"][1], 4, D),
        "ada": np.ascontiguousarray(ada), "dt": chunks(w2[:, 3072:], 8, 16),
        "xs": chunks(w2[:, 2048:2560], 8, 512), "bc": chunks(w2[:, 2560:3072], 8, 512),
        "q": chunks(w2[:, 0:512], 8, 512), "k": chunks(w2[:, 512:1024], 8, 512),
        "v": chunks(w2[:, 1024:1536], 8, 512), "z": chunks(w2[:, 1536:2048], 8, 512),
        "out": chunks(g["w_out_2"][0], 8, 512), "glu": glu, "down2": chunks(down2, 4, D),
    }

    def tiles(a):
        return a.reshape(-1, P).T

    ada_b = g["ada_b_2"][0].reshape(6, D)
    col = {
        "attn_norm": tiles(g["attn_norm"]), "mlp_norm": tiles(g["mlp_norm"]),
        "c_norm": np.concatenate([tiles(g["mla_q_a_norm"]), tiles(g["mla_kv_a_norm"])], 1),
        "q_nope": tiles(g["mla_q_nope_norm"]), "k_nope": tiles(g["mla_k_nope_norm"]),
        "moba_q": tiles(g["moba_q_norm"]), "moba_k": tiles(g["moba_k_norm"]),
        "norm1": tiles(g["norm1_w_2"]), "norm2": tiles(g["norm2_w_2"]),
        "ada_cols": tiles(ada_b[[0, 1, 3, 4]]),
        "conv_w": g["ssd_conv_w_2"][0].reshape(3, 8, P).transpose(2, 1, 0).reshape(P, 24),
        "conv_b": tiles(g["ssd_conv_b_2"]),
        "fconv_w": g["ffn_conv_w_2"][0].reshape(3, KF2, P).transpose(2, 1, 0).reshape(P, 3 * KF2),
        "fconv_b": tiles(g["ffn_conv_b_2"]), "ssd_norm": tiles(g["ssd_norm_w_2"]),
        "c": tiles(g["c_2"]), "c_ctx": tiles(g["c_ctx_2"]),
    }
    row = {
        "q_rope": g["mla_q_rope_norm"], "k_rope": g["mla_k_rope_norm"], "table": g["rel_bias_table"],
        "dt_bias": g["dt_bias_2"], "a_log": g["a_log_2"], "ssd_d": g["ssd_d_2"], "final": g["final_norm_w_2"],
        "ada_g": ada_b[[2, 5]],
    }
    rpb = g["rpb_2"][0]
    wide = np.full((H, 15, 64 + 127), NEG, np.float32)
    wide[:, :, 48:79] = rpb
    col_start = np.clip(np.arange(64) - 8, 0, 48)
    per_w = np.full((64, H, 15, 64), NEG, np.float32)
    for w in range(64):
        a = col_start[w]
        per_w[w, :, :, a:a + 16] = wide[:, :, 63 - w + a:63 - w + a + 16]
    rpb_l = np.empty((2, 64, 2, H, 4, 64), np.float32)
    for r in range(4):
        rpb_l[r % 2, :, r // 2] = per_w[:, :, 7 - r:11 - r, :]

    consts, select = constants()
    rows_tiled = lambda a: np.ascontiguousarray(a.reshape(2, P, D).transpose(1, 0, 2))
    data = {
        "x": rows_tiled(g["x"][0]), "ctx": rows_tiled(g["ctx_2"][0]),
        "cols": np.ascontiguousarray(np.concatenate([col[k] for k in COLS], 1)),
        "rows": np.concatenate([row[k].reshape(-1) for k in ROWS])[None],
        "consts": consts, "select": select,
        "pos_col": np.ascontiguousarray(g["positions"].reshape(2, P).T), "pos_row": g["positions"].reshape(1, T),
        "rpb": np.ascontiguousarray(rpb_l.reshape(P, 4096)),
    }
    nc = bacc.Bacc("TRN2", target_bir_lowering=False, num_devices=1)
    arrays = {}

    def dram(name, a):
        arrays[name] = a
        return nc.dram_tensor(name, a.shape, mybir.dt.from_np(a.dtype), kind="ExternalInput").ap()

    w_aps = {k: dram("w_" + k, a) for k, a in weights.items()}
    d = {k: dram("in_" + k, a) for k, a in data.items()}
    for k in ("rows", "pos_row"):
        d[k] = bass.AP(d[k].tensor, 0, [[0, P], [1, data[k].shape[1]]])
    out = nc.dram_tensor("out", (P, 2, D), F32, kind="ExternalOutput").ap()
    program(nc, w_aps, d["x"], d["ctx"], d["cols"], d["rows"], d["consts"], d["select"], d["pos_col"], d["pos_row"],
            d["rpb"], out)
    got = run(nc, [arrays], core_ids=[0]).results[0]["out"]
    return np.ascontiguousarray(got.reshape(P, 2, D).transpose(1, 0, 2).reshape(1, T, D))
```

```python
import math
from contextlib import ExitStack

import numpy as np

import concourse.bass as bass
from concourse import mybir

F32 = mybir.dt.float32
F32R = mybir.dt.float32r
I32 = mybir.dt.int32
ALU = mybir.AluOpType
ACT = mybir.ActivationFunctionType
AX = mybir.AxisListType

P = 128
T = 256
D = 1024
KD = D // P
EPS = 1e-6
H = 8
QR, KVR, NOPE, ROPE, VD = 384, 256, 128, 64, 128
FF = 4096
BUCKETS = 32
NA = 512
NST = 128
FF2 = 2816
KF2 = FF2 // P
NEG = -1e30
SLOT = 2048
MAGIC = 12582912.0

COLS = dict(attn_norm=16, mlp_norm=16, c_norm=5, q_nope=1, k_nope=1, moba_q=1, moba_k=1, norm1=8, norm2=8,
            ada_cols=32, conv_w=24, conv_b=8, fconv_w=3 * KF2, fconv_b=KF2, ssd_norm=4, c=8, c_ctx=8)
ROWS = dict(q_rope=ROPE, k_rope=ROPE, table=BUCKETS * H, dt_bias=16, a_log=16, ssd_d=8)
CONSTS = dict(ident=128, upto=256, since=256, after=128, before=128, ones=128, causal=384, grid=128, inv_freq=32,
              thresholds=32)


def starts(sizes):
    at, out = 0, {}
    for name, n in sizes.items():
        out[name] = at
        at += n
    out[None] = at
    return out


CA, RA, KA = starts(COLS), starts(ROWS), starts(CONSTS)

GEMMS = [("mla_in", 4, 4, 2), ("mla_uq", 4, 8, 1), ("mla_ukv", 2, 8, 1), ("mla_o", 4, 4, 2), ("mlp0", 32, 16, 1),
         ("qkv", 12, 12, 2), ("moba_o", 4, 4, 2), ("mlp1", 32, 16, 1),
         ("dt", 1, 1, 1), ("xs", 2, 4, 1), ("bc", 2, 4, 1), ("q", 2, 2, 2), ("k", 2, 6, 1), ("z", 2, 2, 2),
         ("v", 2, 4, 2), ("out", 4, 4, 2), ("glu", 22, 22, 1)]


def alternate(steps):
    seq = [(0, 0), (0, 1), (1, 0)]
    for s in range(1, steps):
        seq += [(0, s + 1)] if s + 1 < steps else []
        seq.append((1, s))
    return seq


SMALL = [("h0", 4), ("cT", 3), ("kpe", 1), ("qn", 4), ("kn", 4), ("qp", 2), ("att0", 24), ("m0", 4), ("d0", 4),
         ("h1", 4), ("q1", 4), ("k1", 4), ("att1", 24), ("m1", 4), ("d1", 4), ("ada", 5), ("hc", 4), ("hx", 4),
         ("cum", 1), ("cumcol", 1), ("later", 1), ("xsrow", 5), ("state", 2), ("cb", 2),
         ("nq", 2), ("nk", 2), ("na", 32), ("seg", 8), ("yoff", 4), ("yT", 2), ("m2", 4), ("d2", 4)]


def plan():
    small, at = {}, 0
    for name, n in SMALL:
        small[name] = at
        at += n
    chunk, unit, down = 0, 0, 0
    first_chunk, first_unit, released = {}, {}, []
    for name, n, units, group in GEMMS:
        first_chunk[name], first_unit[name] = chunk, unit
        if name in MLPS:
            for is_down, step in alternate(n // 2):
                if not is_down:
                    released.append(("gemm", unit + step + 1))
                elif step < n // 2 - 1:
                    down += 1
                    released.append(("down", down))
                else:
                    released.append(("small", small[MLPS[name]] + 4))
        else:
            per = units * group // n
            for j in range(n):
                if (j + 1) % group:
                    down += 1
                    released.append(("down", down))
                else:
                    released.append(("gemm", unit + per * (j // group + 1)))
        chunk += n
        unit += units
        if name == "v":
            first_unit["na_o"], first_unit["y"] = unit, unit + 4
            unit += 6
    return first_chunk, first_unit, released, small


MLPS = {"mlp0": "d0", "mlp1": "d1"}
GC, GU, RELEASED, SU = plan()
ROOTS = [(0, 2), (2, 8), (8, 56), (0, 2), (0, 2), (8, 40), (0, 2), (0, 2), (0, 2), (0, 2), (0, 2), (0, 2)]


HI0 = dict(h0=0, cT=4, m0=7, h1=11, m1=15, hc=19, hx=23, yT=27, m2=29)
LO = dict(h0=4, m0=8, h1=28, m1=32, hc=52, hx=56, m2=60)
LO0 = dict(mlp0=8, mlp1=32, glu=60)
HID0 = dict(mlp0=0, mlp1=16, glu=32)


def causal_order():
    seq = [("S", 0), ("S", 1), ("S", 2)]
    for h in range(H):
        seq.append(("P", h))
        if h + 3 < H:
            seq.append(("S", h + 3))
        seq.append(("O", h))
    return seq, {x: n for n, x in enumerate(seq)}


def window_order():
    seq = [("S", 0), ("S", 1), ("S", 2)]
    for i in range(2 * H):
        seq.append(("P", i))
        if i + 3 < 2 * H:
            seq.append(("S", i + 3))
        if i % 2 == 0 and i:
            seq.append(("O", i // 2 - 1))
    seq.append(("O", H - 1))
    units, n = {}, 0
    for kind, i in seq:
        if kind != "O":
            units[(kind, i)] = n
            n += 1
    return seq, units


def spread(ap, at, n):
    dims = [list(x) for x in ap.ap]
    dims.insert(1 + at, [0, n])
    return bass.AP(ap.tensor, ap.offset, dims)


def program(nc, weights, x_in, ctx_in, cols_in, rows_in, consts_in, select_in, pos_col_in, pos_row_in, rpb_in, gates_dram,
            final_dram, out):
    with ExitStack() as stack:
        def sbuf(name, shape, dt=F32):
            return stack.enter_context(nc.sbuf_tensor(name, shape, dt))

        def sem(name):
            return stack.enter_context(nc.semaphore(name))

        raw = sbuf("raw", [P, 2, SLOT])
        split = sbuf("split", [P, 2, 2, SLOT], F32R)
        acts = sbuf("acts", [P, 2, 2, 2048], F32R)
        x = sbuf("x", [P, 2, D])
        work = sbuf("work", [P, 6144])
        bias = sbuf("bias", [P, 4096])
        gates = sbuf("gates", [P, 2, D])
        arena = sbuf("arena", [P, 14336])
        cols = sbuf("cols", [P, CA[None]])
        rows = sbuf("rows", [P, RA[None]])
        consts = sbuf("consts", [P, KA[None]])
        stat = sbuf("stat", [P, 384])
        half = sbuf("half", [P, 48])
        posc = sbuf("posc", [P, 2], I32)
        posr = sbuf("posr", [P, T], I32)
        posf = sbuf("posf", [P, 2])
        rot = sbuf("rot", [P, 2, 2, 32])
        adac = sbuf("adac", [P, 80])
        sc = sbuf("sc", [P, 2, 8])
        ps = [stack.enter_context(nc.psum_tensor(f"bank{i}", [P, 512], F32)) for i in range(8)]

        def col(name, a=0, n=None):
            n = COLS[name] - a if n is None else n
            return cols[:, CA[name] + a:CA[name] + a + n]

        def row(name, a=0, n=None):
            n = ROWS[name] - a if n is None else n
            return rows[:, RA[name] + a:RA[name] + a + n]

        def const(name, a=0, n=None):
            n = CONSTS[name] - a if n is None else n
            return consts[:, KA[name] + a:KA[name] + a + n]

        def view(buf, at, *shape):
            n = int(np.prod(shape))
            flat = buf[:, at:at + n]
            if len(shape) == 1:
                return flat
            names = "abcd"[:len(shape)]
            return flat.rearrange(f"p ({' '.join(names)}) -> p {' '.join(names)}", **dict(zip(names, shape)))

        att = work[:, 0:4096]
        xn = view(work, 4096, 2, D)
        part = view(arena, 4096, 16, 512)
        ident = const("ident")
        q0 = view(arena, 0, 2, H * 192)
        kv = view(arena, 3072, 2, H * 256)
        qnT = view(arena, 7168, H, T)
        knT = view(arena, 9216, H, T)
        qpT = view(arena, 11264, 4, T)
        kpT = view(arena, 12288, T)
        kpe2 = view(arena, 12544, 2, 128)
        proj = view(arena, 7168, 2, 704)
        dist, deltas = bias[:, 3072:3456], bias[:, 3840:4096]
        qkv = view(arena, 0, 2, 3 * D)
        q1T = view(arena, 6144, H, T)
        k1T = view(arena, 8192, H, T)
        relu_t = view(arena, 0, 2, 512)
        square_t = view(arena, 1024, 2, 512)
        ctx = view(work, 0, 2, D)
        nqk = view(arena, 0, 2, 2 * NA)
        nv = view(arena, 2048, 2, NA)
        ncv = view(arena, 3072, 2, NA)
        sz = view(arena, 4096, 2, NA)
        nqT = view(arena, 5120, 4, T)
        nkT = view(arena, 6144, 4, 2 * T)
        BT = view(arena, 8192, 2, 2 * T)
        CT = view(arena, 9216, 2, T)
        xsr = view(arena, 9728, 2, NA)
        cxsr = view(arena, 10752, 2, NA)
        Bcr = view(arena, 11776, 2, 2, P)
        cbm = view(arena, 12288, 2, 768)
        cum = arena[0:16, 13824:14336]
        tmp = lambda k: arena[:, 12288 + 64 * k:12352 + 64 * k]
        E = view(arena, 6144, 2, 768)
        Wm = view(arena, 2048, 2, 768)
        select = arena[0:16, 0:2048]
        xsT = view(work, 4096, 4, 2 * T)
        xw = view(work, 2048, 2, 2, NA)
        yrow = view(work, 4096, 2, NA)
        h0T = view(work, 5120, 2, NA)
        gact = view(arena, 1024, 2, T)
        prod_t = view(arena, 2048, 2, T)
        final = arena[:, 8192:8192 + D]
        raw_down = view(arena, 4096, 2, D)
        split_down = acts[:, 1, :, 1024:2048]

        def above(b):
            return bias[:, 3456:3840] if b % 2 else arena[:, 12032:12416]

        def t5_term(b, h):
            at = 8192 + 384 * (5 * (b % 2) + h - 3)
            return arena[:, at:at + 384]

        def act_pair(which, k, a, n):
            return tuple(acts[:, which, p, k * T + a:k * T + a + n] for p in range(2))

        x_in_sb = sem("x_loaded")
        ctx_in_sb = sem("ctx_loaded")
        params_in = sem("params_loaded")
        select_in_sb = sem("select_loaded")
        rpb_loaded = sem("rpb_loaded")
        w_loaded = [sem(f"w_loaded{i}") for i in range(2)]
        hi_ready, lo_ready = sem("w_hi_ready"), sem("w_lo_ready")
        gemm_ready, down_used = sem("gemm_ready"), sem("chunk_used")
        out_hi, hidden_hi, glu_taps = sem("head_out_hi_ready"), sem("hidden_hi_ready"), sem("glu_outer_taps")
        down_loaded = [sem(f"glu_down_loaded{i}") for i in range(2)]
        down_hi, down_lo, glu_used = sem("glu_down_hi"), sem("glu_down_lo"), sem("glu_down_used")
        act_hi, act_lo = sem("activation_hi_ready"), sem("activation_lo_ready")
        final_in, gates_in = sem("final_loaded"), sem("gates_loaded")
        t5_start, t5_above, t5_terms = sem("t5_started"), sem("t5_above"), sem("t5_terms")
        gemm_free = [sem(f"gemm_free{i}") for i in range(4)]
        small_ready = sem("small_ready")
        small_free = [sem(f"small_free{i}") for i in range(4)]
        dve_step, act_step, pool_step = sem("dve_step"), sem("act_step"), sem("pool_step")
        normed = sem("rows_normed")
        latents_normed, heads_normed = sem("latents_normed"), sem("heads_normed")
        sq_ready, sq_used = sem("squares_ready"), sem("squares_used")
        angles, rotations = sem("angles_ready"), sem("rotations_ready")
        max_ready, exp_done, probs_ready = sem("max_ready"), sem("exp_done"), sem("probs_ready")
        silu_c = sem("silu_c")
        ada_in = [sem(f"ada_in{i}") for i in range(2)]
        ada_used = sem("ada_used")
        means_ready, roots_ready = sem("means_ready"), sem("roots_ready")
        conv_mid, conv_act = sem("conv_centre"), sem("conv_activated")
        sp_abs, sp_exp, sp_u, sp_ln = (sem("softplus_" + n) for n in ("abs", "exp", "one_plus", "ln"))
        a_exp, dA_ready, ecum_ready = sem("a_exp"), sem("dA_ready"), sem("exp_cum")
        later_exp, xw_ready, seg_exp = sem("later_exp"), sem("xw_ready"), sem("seg_exp")
        w_mat, y_used, nqk_ready = sem("mask_matrix_ready"), sem("mask_matrix_used"), sem("nqk_rotated")
        glu_mid, glu_act = sem("glu_centre"), sem("glu_activated")
        out_ready, stored = sem("out_ready"), sem("stored")

        def gbank(u):
            return ps[u % 4]

        def sbank(u):
            return ps[4 + u % 4]

        def gemm_out(eng, u, i=None):
            eng.wait_ge(gemm_ready, u + 1 if i is None else 4 * i + (u + 1))

        def gemm_gone(eng, u):
            eng.wait_ge(gemm_free[u % 4], u // 4 + 1)

        def small_out(eng, u):
            eng.wait_ge(small_ready, u + 1)

        def small_gone(eng, u):
            eng.wait_ge(small_free[u % 4], u // 4 + 1)

        class Steps:

            def __init__(self, eng, semaphore):
                self.eng, self.sem, self.n, self.turn = eng, semaphore, 0, 0

            def step(self, ins):
                ins.then_inc(self.sem, 1)
                self.n += 1

            def settle(self):
                self.eng.wait_ge(self.sem, self.n + self.turn)

            def enter(self, i, per, first=0):
                self.turn, self.per, self.before = per * i - per * first if first else per * i, per, self.n

            def leave(self, turns):
                assert self.n == self.before + self.per
                self.turn, self.n = 0, self.before + self.per * turns

        seq_c, unit_c = causal_order()
        seq_w, unit_w = window_order()

        def released(eng, c, i=None, per=0):
            kind, value = RELEASED[c]
            semaphore = {"gemm": gemm_ready, "down": down_used, "small": small_ready}[kind]
            eng.wait_ge(semaphore, value if i is None else per * i + value)

        def chunk_width(c):
            for name, n, _, _ in GEMMS:
                j = c - GC[name]
                if 0 <= j < n:
                    return weights[name].shape[2]

        CHUNKS = GC["glu"] + KF2

        def quarters_of(n):
            return att[:, 2048 + 512 * n:2560 + 512 * n].rearrange("p (a b) -> p a b", a=4)

        def tokens_of(which, part_, k, t):
            return acts[:, which, part_, :].rearrange("p (k n) -> p k n", n=T)[:, k:k + 4, t * P:(t + 1) * P]

        block = stack.enter_context(nc.Block())

        @block.sync
        def _(sp):
            sp.dma_start(x[:, :, :], x_in).then_inc(x_in_sb, 16)

            def load(name, j, i=None, pitch=0):
                c = GC[name] + j
                w, at = weights[name], j
                if c >= 2:
                    sp.wait_ge(lo_ready, c - 1 if i is None else pitch * i + (c - 1))
                src = w[at] if i is None else w[pitch * i + at]
                sp.dma_start(raw[:, c % 2, 0:w.shape[2]], src).then_inc(w_loaded[c % 2], 16)

            def load_all(name):
                for j in range(weights[name].shape[0]):
                    load(name, j)

            def load_loop(name, a, pitch, turns):
                with sp.Fori(0, turns) as i:
                    for j in range(pitch):
                        load(name, a + j, i, pitch)

            def load_mlp(name, turns):
                for j in range(3):
                    load(name, j)
                load_loop(name, 3, 8, turns)
                for j in range(3 + 8 * turns, weights[name].shape[0]):
                    load(name, j)

            for name in ("mla_in", "mla_uq", "mla_ukv", "mla_o"):
                load_all(name)
            load_mlp("mlp0", 3)
            load_loop("qkv", 0, 4, 3)
            load_all("moba_o")
            sp.wait_ge(gemm_ready, GU["mlp1"])
            sp.dma_start(ctx, ctx_in).then_inc(ctx_in_sb, 16)
            load_mlp("mlp1", 3)
            sp.wait_ge(ada_used, 24)
            sp.dma_start(bias[:, :], rpb_in).then_inc(rpb_loaded, 16)
            for name in ("dt", "xs", "bc", "q", "k", "z", "v"):
                load_all(name)
            load("out", 0)
            load("out", 1)
            small_out(sp, SU["nk"] + 1)
            sp.dma_start(select, select_in).then_inc(select_in_sb, 16)
            load("out", 2)
            load("out", 3)
            load("glu", 0)
            load("glu", 1)
            sp.wait_ge(gemm_ready, GU["out"])
            sp.dma_start(final, final_dram).then_inc(final_in, 16)

            def load_down(step, i=None):
                if i is not None or step >= 2:
                    sp.wait_ge(down_lo, step - 1 if i is None else 4 * i + (step - 1))
                w = weights["glu_down"]
                sp.dma_start(raw_down[:, step % 2, :], w[step] if i is None else w[4 * i + step])\
                    .then_inc(down_loaded[step % 2], 16)

            sp.wait_ge(normed, 13)
            load_down(0)
            load("glu", 2)
            load_down(1)
            load("glu", 3)
            with sp.Fori(0, 4) as i:
                for step in range(2, 6):
                    load_down(step, i)
                    load("glu", step + 2, i, 4)
            load_down(18)
            load("glu", 20)
            load_down(19)
            load("glu", 21)
            load_down(20)
            load_down(21)
            for t in range(2):
                sp.wait_ge(out_ready, t + 1)
                sp.dma_start(out[:, t, :], xn[:, t, :]).then_inc(stored, 16)
            sp.wait_ge(stored, 32)

        @block.gpsimd
        def _(pool):
            pool.memset(half[:, :], -0.5).then_inc(pool_step, 1)
            pool.wait_ge(pool_step, 1)

            def roots(first, last):
                for n in range(first, last):
                    a, b = ROOTS[n]
                    pool.wait_ge(means_ready, n + 1)
                    pool.tensor_tensor(stat[:, a:b], stat[:, a:b], half[:, 0:b - a], ALU.pow).then_inc(roots_ready, 1)

            roots(0, 4)
            pool.wait_ge(t5_start, 1)
            def add_terms(b, i=None):
                pool.wait_ge(t5_terms, b if i is None else 2 * i + b)
                for h in range(3, H):
                    acc = bias[:, 384 * h:384 * (h + 1)]
                    pool.tensor_tensor(acc, acc, t5_term(b, h), ALU.add).then_inc(pool_step, 1)

            with pool.Fori(0, (BUCKETS - 2) // 2) as i:
                add_terms(1, i)
                pool.wait_ge(pool_step, 10 * i + 6)
                add_terms(2, i)
                pool.wait_ge(pool_step, 10 * i + 11)
            add_terms(BUCKETS - 1)
            pool.wait_ge(pool_step, 5 * (BUCKETS - 1) + 1)
            roots(4, 6)
            pool.wait_ge(small_ready, SU["att1"] + 24)
            for j in range(2):
                pool.dma_start(bias[:, 2048 * j:2048 * j + 2048], weights["ada"][j]).then_inc(ada_in[j], 16)
            roots(6, 8)
            with pool.Fori(1, 12) as i:
                for u in range(2):
                    pool.wait_ge(ada_used, 2 * i + (u - 1))
                    pool.dma_start(bias[:, 2048 * u:2048 * u + 2048], weights["ada"][2 * i + u])\
                        .then_inc(ada_in[u], 16)
            roots(8, len(ROOTS))

        @block.tensor
        def _(pe):
            def small_start(u):
                if u >= 4:
                    pe.wait_ge(small_free[u % 4], u // 4)

            def gemm_start(u, i=None):
                if u >= 4:
                    pe.wait_ge(gemm_free[u % 4], u // 4 if i is None else i + u // 4)

            def weights_in(c, i=None, pitch=0):
                pe.wait_ge(lo_ready, c + 1 if i is None else pitch * i + (c + 1))

            def slot(c, kts, width):
                return tuple(split[:, c % 2, p, 0:kts * width].rearrange("p (k n) -> p k n", k=kts) for p in range(2))

            def product(out_, a, b, first, last):
                pe.matmul(out_, a[0], b[0], start=first, stop=False)
                pe.matmul(out_, a[0], b[1], start=False, stop=False)
                return pe.matmul(out_, a[1], b[0], start=False, stop=last)

            def flip(u, pieces):
                small_start(u)
                for at, src in pieces:
                    k, m = src.shape[0], src.shape[1]
                    ins = pe.transpose(sbank(u)[0:m, at:at + k], src, ident[0:k, 0:k])
                ins.then_inc(small_ready, 1)

            def rows_to_cols(name, count):
                for t in range(2):
                    pe.wait_ge(normed, count + t + 1)
                    for half in range(2):
                        flip(SU[name] + 2 * t + half,
                             [(P * f, xn[:, t, (4 * half + f) * P:(4 * half + f + 1) * P]) for f in range(4)])

            def rows_units(c, u, kts, width, piece, lhs, group=1, i=None, pitch=0):
                pieces = range(0, width, piece)
                for g in range(group):
                    weights_in(c + g, i, pitch)
                    w = slot(c + g, kts, width)
                    for m, a in enumerate(pieces):
                        for t in range(len(lhs)):
                            n = u + len(lhs) * m + t
                            if g == 0:
                                gemm_start(n, i)
                            for k in range(kts):
                                ins = product(gbank(n)[:, 0:piece], lhs[t](kts * g + k),
                                              tuple(p[:, k, a:a + piece] for p in w),
                                              g == 0 and k == 0, g == group - 1 and k == kts - 1)
                            if g == group - 1:
                                ins.then_inc(gemm_ready, 1)
                    if g < group - 1:
                        ins.then_inc(down_used, 1)

            def rows_gemm(name, chunks, kts, width, piece, lhs, group=1):
                per = len(lhs) * (width // piece)
                for j in range(0, chunks, group):
                    rows_units(GC[name] + j, GU[name] + per * (j // group), kts, width, piece, lhs, group)

            def rows_of(which, kts=0):
                return [lambda k, t=t: act_pair(which, kts + k, t * P, P) for t in range(2)]

            def cols_unit(c, u, feats, which, i=None, pitch=0, start_=True):
                w = slot(c, KD, 256)
                gemm_start(u, i)
                for n, (f, wh) in enumerate(zip(feats, which)):
                    for k in range(KD):
                        ins = product(gbank(u)[:, n * T:(n + 1) * T], tuple(p[:, k, f * P:(f + 1) * P] for p in w),
                                      act_pair(wh, k, 0, T), k == 0, k == KD - 1)
                ins.then_inc(gemm_ready, 1)

            def mlp(name, steps, tiles, turns):
                c0, u0, d0 = GC[name], GU[name], SU[MLPS[name]]
                seq = alternate(steps)

                def up(n, s, i=None):
                    weights_in(c0 + n, i, 8)
                    cols_unit(c0 + n, u0 + s, (0, 1), (0, 0), i)

                def down(n, s, i=None):
                    weights_in(c0 + n, i, 8)
                    pe.wait_ge(act_lo, LO0[name] + s + 1 if i is None else 4 * i + (LO0[name] + s + 1))
                    w = slot(c0 + n, tiles, D)
                    for half_ in range(2):
                        for t in range(2):
                            for k in range(tiles):
                                kt = (s % 2) * 2 + k
                                ins = product(sbank(d0 + 2 * half_ + t)[:, :], act_pair(1, kt, t * P, P),
                                              tuple(p[:, k, 512 * half_:512 * half_ + 512] for p in w),
                                              i is None and s == 0 and k == 0,
                                              i is None and s == steps - 1 and k == tiles - 1)
                            if i is None and s == steps - 1:
                                ins.then_inc(small_ready, 1)
                    if i is not None or s < steps - 1:
                        ins.then_inc(down_used, 1)

                for n in range(3):
                    if n == 2:
                        for u in range(d0, d0 + 4):
                            small_start(u)
                    (down if seq[n][0] else up)(n, seq[n][1])
                with pe.Fori(0, turns) as i:
                    for n in range(3, 11):
                        (down if seq[n][0] else up)(n, seq[n][1], i)
                for n in range(3 + 8 * turns, len(seq)):
                    (down if seq[n][0] else up)(n, seq[n][1])

            def causal_attention(name, scores, value, count):
                for kind, h in seq_c:
                    u = SU[name] + unit_c[(kind, h)]
                    if kind == "S":
                        small_start(u)
                        scores(u, h)
                    elif kind == "P":
                        pe.wait_ge(probs_ready, count + h + 1)
                        pr = att[:, 1024 + 512 * (h % 2):1024 + 512 * (h % 2) + 384]
                        flip(u, [(0, pr[:, 256:384]), (P, pr[:, 0:128]), (2 * P, pr[:, 128:256])])
                    else:
                        small_gone(pe, SU[name] + unit_c[("P", h)])
                        small_start(u)
                        pt = att[:, 2048 + 1024 * (h % 2):2048 + 1024 * (h % 2) + 384]
                        pe.matmul(sbank(u)[:, 0:T], value(0, h), pt[:, 0:T], start=True, stop=False)
                        pe.matmul(sbank(u)[:, P:T], value(1, h), pt[:, T:384], start=False, stop=True)\
                            .then_inc(small_ready, 1)

            pe.wait_ge(params_in, 80)
            rows_to_cols("h0", 0)
            pe.wait_ge(act_lo, LO["h0"])
            rows_gemm("mla_in", 4, 4, 352, 352, rows_of(0), 2)
            pe.wait_ge(latents_normed, 1)
            for n, fs in enumerate(((0, 1), (2, 3), (4,))):
                flip(SU["cT"] + n, [(T * a + P * t, proj[:, t, f * P:(f + 1) * P])
                                    for a, f in enumerate(fs) for t in range(2)])
            for n in range(3):
                small_gone(pe, SU["cT"] + n)
            rows_gemm("mla_uq", 4, 3, 384, 384, rows_of(1))
            rows_gemm("mla_ukv", 2, 2, 1024, 512, rows_of(1, 3))
            pe.wait_ge(heads_normed, 1)
            flip(SU["kpe"], [(P * t, kpe2[:, t, :]) for t in range(2)])
            for n in range(4):
                flip(SU["qn"] + n, [(T * a + P * t, q0[:, t, (2 * n + a) * 192:(2 * n + a) * 192 + NOPE])
                                    for a in range(2) for t in range(2)])
            for n in range(4):
                flip(SU["kn"] + n, [(T * a + P * t, kv[:, t, (2 * n + a) * 256:(2 * n + a) * 256 + NOPE])
                                    for a in range(2) for t in range(2)])
            pe.wait_ge(heads_normed, 2)
            for n in range(2):
                flip(SU["qp"] + n, [(T * a + P * t, xn[:, t, (2 * n + a) * P:(2 * n + a + 1) * P])
                                    for a in range(2) for t in range(2)])
            for u in range(SU["kpe"], SU["qp"] + 2):
                small_gone(pe, u)

            def scores0(u, h):
                a = 64 * (h % 2)
                b = sbank(u)
                pe.matmul(b[:, 0:T], qnT[:, h, P:T], knT[:, h, :], start=True, stop=False)
                pe.matmul(b[:, 0:T], qpT[a:a + 64, h // 2, P:T], kpT[a:a + 64, :], start=False, stop=True)
                pe.matmul(b[:, T:384], qnT[:, h, 0:P], knT[:, h, 0:P], start=True, stop=False)
                pe.matmul(b[:, T:384], qpT[a:a + 64, h // 2, 0:P], kpT[a:a + 64, 0:P], start=False, stop=True)\
                    .then_inc(small_ready, 1)

            causal_attention("att0", scores0, lambda t, h: kv[:, t, h * 256 + NOPE:(h + 1) * 256], 0)
            for h in range(H):
                small_gone(pe, SU["att0"] + unit_c[("O", h)])
            rows_gemm("mla_o", 4, 4, 512, 512, rows_of(1), 2)
            rows_to_cols("m0", 2)
            pe.wait_ge(act_lo, LO["m0"])
            mlp("mlp0", 16, 2, 3)
            rows_to_cols("h1", 4)
            pe.wait_ge(act_lo, LO["h1"])
            with pe.Fori(0, 3) as i:
                for j in range(2):
                    rows_units(GC["qkv"] + 2 * j, GU["qkv"] + 2 * j, 4, 512, 512, rows_of(0), 2, i, 4)
            pe.wait_ge(heads_normed, 3)
            for n in range(8):
                flip(SU["q1"] + n, [(T * a + P * t, qkv[:, t, (2 * n + a) * P:(2 * n + a + 1) * P])
                                    for a in range(2) for t in range(2)])
            for u in range(SU["q1"], SU["q1"] + 8):
                small_gone(pe, u)

            def scores1(u, h):
                b = sbank(u)
                pe.matmul(b[:, 0:T], q1T[:, h, P:T], k1T[:, h, :], start=True, stop=True)
                pe.matmul(b[:, T:384], q1T[:, h, 0:P], k1T[:, h, 0:P], start=True, stop=True)\
                    .then_inc(small_ready, 1)

            causal_attention("att1", scores1, lambda t, h: qkv[:, t, 2 * D + h * P:2 * D + (h + 1) * P], H)
            for h in range(H):
                small_gone(pe, SU["att1"] + unit_c[("O", h)])
            rows_gemm("moba_o", 4, 4, 512, 512, rows_of(1), 2)
            rows_to_cols("m1", 6)
            pe.wait_ge(act_lo, LO["m1"])
            mlp("mlp1", 16, 2, 3)

            def ada_sums():
                pe.wait_ge(ada_used, 24)
                u = SU["ada"]
                small_start(u)
                n = 0
                for chunk in (0, 1, 2, 3, 6, 7, 8, 9, 12, 13, 14, 15):
                    for f in range(4):
                        ins = pe.matmul(sbank(u)[:, n:n + 1], part[:, chunk, f * P:(f + 1) * P], const("ones", 0, 1),
                                        start=True, stop=True)
                        n += 1
                ins.then_inc(small_ready, 1)
                for g, chunk in enumerate((4, 5, 10, 11)):
                    small_start(u + 1 + g)
                    pe.matmul(sbank(u + 1 + g)[:, :], const("ones"), part[:, chunk, :], start=True, stop=True)\
                        .then_inc(small_ready, 1)

            ada_sums()

            pe.wait_ge(normed, 10)
            for t in range(2):
                for half in range(2):
                    flip(SU["hc"] + 2 * t + half,
                         [(P * f, ctx[:, t, (4 * half + f) * P:(4 * half + f + 1) * P]) for f in range(4)])
            rows_to_cols("hx", 10)
            pe.wait_ge(act_lo, LO["hx"])

            both = rows_of(0) + rows_of(1)
            c, u = GC["dt"], GU["dt"]
            weights_in(c)
            gemm_start(u)
            w = slot(c, KD, 16)
            for n in range(4):
                for k in range(KD):
                    ins = product(gbank(u)[:, 16 * n:16 * n + 16], both[n](k), tuple(p[:, k, :] for p in w),
                                  k == 0, k == KD - 1)
            ins.then_inc(gemm_ready, 1)
            for j in range(2):
                weights_in(GC["xs"] + j)
                for f in range(2):
                    cols_unit(GC["xs"] + j, GU["xs"] + 2 * j + f, (f, f), (0, 1))
            weights_in(GC["bc"])
            for f in range(2):
                cols_unit(GC["bc"], GU["bc"] + f, (f, f), (0, 1))
            weights_in(GC["bc"] + 1)
            for f in range(2):
                cols_unit(GC["bc"] + 1, GU["bc"] + 2 + f, (f,), (0,))
            rows_gemm("q", 2, 4, 512, 512, both[:2], 2)
            for j in range(2):
                c, u = GC["k"] + j, GU["k"] + 3 * j
                rows_units(c, u, KD, 256, 256, both[:2])
                cols_unit(c, u + 2, (0, 1), (1, 1))
            rows_gemm("z", 2, 4, 512, 512, both[:2], 2)
            rows_gemm("v", 2, 4, 512, 512, both, 2)

            pe.wait_ge(dA_ready, 1)
            dA = lambda t: stat[:, 160 + 16 * t:176 + 16 * t]
            u = SU["cum"]
            small_start(u)
            b = sbank(u)
            pe.matmul(b[0:16, 0:T], dA(0), const("upto"), start=True, stop=False)
            pe.matmul(b[0:16, P:T], dA(1), const("upto", 0, P), start=False, stop=True)
            pe.matmul(b[0:16, T:2 * T], dA(1), const("since"), start=True, stop=False)
            pe.matmul(b[0:16, T:T + P], dA(0), const("since", P, P), start=False, stop=True).then_inc(small_ready, 1)
            small_gone(pe, u)
            u = SU["cumcol"]
            small_start(u)
            for n in range(4):
                ins = pe.transpose(sbank(u)[:, 16 * n:16 * n + 16], cum[:, P * n:P * n + P], ident[0:16, 0:16])
            ins.then_inc(small_ready, 1)
            u = SU["later"]
            small_start(u)
            b = sbank(u)
            for n, (parts) in enumerate((
                    [("after", 0), ("ones", 1)], [("before", 0)], [("after", 1)], [("before", 1), ("ones", 0)])):
                for m, (tri, t) in enumerate(parts):
                    ins = pe.matmul(b[:, 16 * n:16 * n + 16], const(tri), dA(2 + t), start=m == 0,
                                    stop=m == len(parts) - 1)
            ins.then_inc(small_ready, 1)
            pe.wait_ge(conv_act, 8)
            for t in range(2):
                flip(SU["xsrow"] + t, [(P * f, xsT[:, f, t * P:(t + 1) * P]) for f in range(4)])
            for t in range(2):
                flip(SU["xsrow"] + 2 + t, [(P * f, xsT[:, f, T + t * P:T + (t + 1) * P]) for f in range(4)])
            flip(SU["xsrow"] + 4, [(P * (2 * t + g), BT[:, g, T + t * P:T + (t + 1) * P])
                                   for t in range(2) for g in range(2)])
            small_gone(pe, SU["xsrow"] + 4)
            pe.wait_ge(xw_ready, 4)
            for d in range(2):
                u = SU["state"] + d
                small_start(u)
                for g in range(2):
                    for t in range(2):
                        ins = pe.matmul(sbank(u)[:, g * 256:(g + 1) * 256], Bcr[:, t, g, :],
                                        xw[:, t, d, g * 256:(g + 1) * 256], start=t == 0, stop=t == 1)
                ins.then_inc(small_ready, 1)
            for g in range(2):
                u = SU["cb"] + g
                small_start(u)
                for t in range(2):
                    ins = pe.matmul(sbank(u)[:, t * T:(t + 1) * T], BT[:, g, t * P:(t + 1) * P], CT[:, g, :],
                                    start=True, stop=True)
                ins.then_inc(small_ready, 1)
            pe.wait_ge(nqk_ready, 1)
            for n in range(2):
                flip(SU["nq"] + n, [(T * a + P * t, nqk[:, t, (2 * n + a) * P:(2 * n + a + 1) * P])
                                    for a in range(2) for t in range(2)])
            for n in range(2):
                flip(SU["nk"] + n, [(T * a + P * t, nqk[:, t, NA + (2 * n + a) * P:NA + (2 * n + a + 1) * P])
                                    for a in range(2) for t in range(2)])
            for u in range(SU["nq"], SU["nq"] + 4):
                small_gone(pe, u)
            for u in (GU["k"] + 2, GU["k"] + 5):
                gemm_gone(pe, u)
            for u in range(GU["v"], GU["v"] + 4):
                gemm_gone(pe, u)
            for kind, i in seq_w:
                if kind == "S":
                    u = SU["na"] + unit_w[(kind, i)]
                    h, t = i // 2, i % 2
                    a = 64 * (h % 2)
                    small_start(u)
                    pe.matmul(sbank(u)[:, :], nqT[a:a + 64, h // 2, t * P:(t + 1) * P], nkT[a:a + 64, h // 2, :],
                              start=True, stop=True).then_inc(small_ready, 1)
                elif kind == "P":
                    pe.wait_ge(probs_ready, 2 * H + i + 1)
                    pr = att[:, 1024 + 512 * (i % 2):1536 + 512 * (i % 2)]
                    flip(SU["na"] + unit_w[(kind, i)], [(P * k, pr[:, P * k:P * k + P]) for k in range(4)])
                else:
                    u = GU["na_o"] + i // 2
                    a = 64 * (i % 2)
                    for t in range(2):
                        small_gone(pe, SU["na"] + unit_w[("P", 2 * i + t)])
                    if i % 2 == 0:
                        gemm_start(u)
                    pt = view(att, 2048 + 1024 * (i % 2), 4, T)
                    for k in range(4):
                        val = (nv if k < 2 else ncv)[:, k % 2, i * 64:(i + 1) * 64]
                        ins = pe.matmul(gbank(u)[a:a + 64, 0:T], val, pt[:, k, :], start=k == 0, stop=k == 3)
                    if i % 2:
                        ins.then_inc(gemm_ready, 1)
            pe.wait_ge(select_in_sb, 16)
            for u in range(2):
                small_gone(pe, SU["xsrow"] + u)

            def segment(h):
                u = SU["seg"] + h
                small_start(u)
                for d in range(2):
                    ins = pe.matmul(sbank(u)[:, d * T:(d + 1) * T], select[:, (8 * d + h) * P:(8 * d + h + 1) * P],
                                    cum[:, d * T:(d + 1) * T], start=True, stop=True)
                ins.then_inc(small_ready, 1)

            for h in range(4):
                segment(h)
            yu = GU["y"]
            for u in (yu, yu + 1):
                gemm_start(u)
            for h in range(H):
                pe.wait_ge(w_mat, h + 1)
                wm = Wm[:, h % 2, :]
                for t, parts in enumerate(([(0, 0), (384, 0), (512, 1)], [(128, 0), (256, 1), (640, 1)])):
                    for m, (at, tile) in enumerate(parts):
                        ins = pe.matmul(gbank(yu + t)[:, h * 64:(h + 1) * 64], wm[:, at:at + P],
                                        xsr[:, tile, h * 64:(h + 1) * 64], start=m == 0, stop=m == 2)
                    if h == H - 1:
                        ins.then_inc(gemm_ready, 1)
                if h < H - 1:
                    ins.then_inc(y_used, 1)
                if h + 4 < H:
                    segment(h + 4)
            for d in range(2):
                small_gone(pe, SU["state"] + d)
            for t in range(2):
                for d in range(2):
                    u = SU["yoff"] + 2 * t + d
                    small_start(u)
                    for g in range(2):
                        ins = pe.matmul(sbank(u)[:, g * 256:(g + 1) * 256], CT[:, g, t * P:(t + 1) * P],
                                        h0T[:, d, g * 256:(g + 1) * 256], start=True, stop=True)
                    ins.then_inc(small_ready, 1)
            pe.wait_ge(normed, 13)
            for n in range(2):
                flip(SU["yT"] + n, [(T * a + P * t, yrow[:, t, (2 * n + a) * P:(2 * n + a + 1) * P])
                                    for a in range(2) for t in range(2)])
            for p in range(4):
                gemm_gone(pe, GU["na_o"] + p)
            for n in range(2):
                small_gone(pe, SU["yT"] + n)
            rows_gemm("out", 4, 4, 512, 512, rows_of(1), 2)
            rows_to_cols("m2", 13)
            pe.wait_ge(act_lo, LO["m2"])
            d0 = SU["d2"]

            def up(s, i=None):
                weights_in(GC["glu"] + s, i, 4)
                cols_unit(GC["glu"] + s, GU["glu"] + s, (0, 1), (0, 0), i)

            def down(s, i=None):
                pe.wait_ge(act_lo, LO0["glu"] + s + 1 if i is None else 4 * i + (LO0["glu"] + s + 1))
                pe.wait_ge(down_lo, s + 1 if i is None else 4 * i + (s + 1))
                at = 2 * (s % 2)
                for half_ in range(2):
                    for t in range(2):
                        ins = product(sbank(d0 + 2 * half_ + t)[:, :], act_pair(1, at, t * P, P),
                                      tuple(split_down[:, p, 512 * half_:512 * half_ + 512] for p in range(2)),
                                      i is None and s == 0, i is None and s == KF2 - 1)
                        if i is None and s == KF2 - 1:
                            ins.then_inc(small_ready, 1)
                if i is not None or s < KF2 - 1:
                    ins.then_inc(glu_used, 1)

            up(0)
            up(1)
            for u in range(d0, d0 + 4):
                small_start(u)
            down(0)
            with pe.Fori(0, 5) as i:
                for s in range(1, 5):
                    up(s + 1, i)
                    down(s, i)
            down(KF2 - 1)

        @block.scalar
        def _(act):
            for dst, src in ((cols[:, :], cols_in), (rows[:, :], rows_in), (consts[:, :], consts_in),
                             (posc[:, :], pos_col_in), (posr[:, :], pos_row_in)):
                act.dma_start(dst, src).then_inc(params_in, 16)
            act.dma_start(gates[:, :, :].rearrange("p a b -> p (a b)"), gates_dram).then_inc(gates_in, 16)

            def copy(out_, in_, scale=None):
                if scale is None:
                    return act.activation(out_, in_, ACT.Copy)
                return act.activation(out_, in_, ACT.Copy, scale=scale)

            def split_hi(c, i=None, pitch=0):
                loads = 16 * (c // 2 + 1)
                act.wait_ge(w_loaded[c % 2], loads if i is None else 8 * pitch * i + loads)
                n = chunk_width(c)
                copy(split[:, c % 2, 0, 0:n], raw[:, c % 2, 0:n]).then_inc(hi_ready, 1)

            def used(c, i=None, pitch=0):
                per = {"gemm": 4, "down": pitch // 2}.get(RELEASED[c][0], 0)
                released(act, c, i, per)
                if c + 2 < CHUNKS:
                    split_hi(c + 2, i, pitch)

            def empty(u, dst, n=512, scale=None, a=0):
                gemm_out(act, u)
                src = gbank(u)[:, a:a + n]
                copy(dst, src, scale).then_inc(gemm_free[u % 4], 1)

            def small_empty(u, dst, n=512, scale=None):
                small_out(act, u)
                copy(dst, sbank(u)[:, 0:n], scale).then_inc(small_free[u % 4], 1)

            def pair(buf, n):
                return buf[:, 2 * n:2 * n + 2, 0:T]

            def halves(u, n=2, m=T):
                return sbank(u)[:, 0:n * m].rearrange("p (a b) -> p a b", a=n)

            def pair_empty(u, dst, scale=None):
                small_out(act, u)
                copy(dst, halves(u), scale).then_inc(small_free[u % 4], 1)

            def cols_hi(name, which=0):
                for n in range(4):
                    small_gone(act, SU[name] + n)
                    copy(tokens_of(which, 0, 4 * (n % 2), n // 2), quarters_of(n)).then_inc(act_hi, 1)

            def mlp(name, steps, turns, hidden, beside=None):
                c0, seq = GC[name], alternate(steps)

                def chunk(n, i=None):
                    used(c0 + n, i, 8)
                    if not seq[n][0]:
                        hidden(seq[n][1], i)
                    if beside:
                        beside(n, i)

                for n in range(3):
                    chunk(n)
                with act.Fori(0, turns) as i:
                    for n in range(3, 11):
                        chunk(n, i)
                for n in range(3 + 8 * turns, len(seq)):
                    chunk(n)

            split_hi(0)
            split_hi(1)
            act.wait_ge(params_in, 80)
            act.activation(sc[:, :, :], col("c", 0, 16).rearrange("p (a b) -> p a b", a=2), ACT.Silu)\
                .then_inc(silu_c, 1)
            cols_hi("h0")
            act.wait_ge(angles, 1)
            act.activation(rot[:, :, :, :].rearrange("p a b c -> p (a b c)"), bias[:, 128:256], ACT.Sin)\
                .then_inc(rotations, 1)
            for n in range(4):
                used(GC["mla_in"] + n)
                for t in range(2 * (n % 2)):
                    empty(GU["mla_in"] + n - 1 + t, proj[:, t, 352 * (n // 2):352 * (n // 2) + 352], 352)
            for n, fs in enumerate((2, 2, 1)):
                small_out(act, SU["cT"] + n)
                for f in range(fs):
                    k = 2 * n + f
                    ins = copy(acts[:, 1, 0, k * T:(k + 1) * T], sbank(SU["cT"] + n)[:, f * T:(f + 1) * T],
                               col("c_norm", k, 1))
                ins.then_inc(act_hi, 1)
            n = 0
            for name, dst, each, per in (("mla_uq", q0, 192, 2), ("mla_ukv", kv, 256, 4)):
                for m in range(8):
                    u, t, p = GU[name] + m, m % 2, m // 2
                    if m % per == 0:
                        used(GC[name] + m // per)
                    gemm_out(act, u)
                    if n >= 2:
                        act.wait_ge(sq_used, n - 1)
                    w = 192 if each == 192 else NOPE
                    src = gbank(u)[:, 0:2 * each].rearrange("p (a b) -> p a b", a=2)[:, :, 0:w]
                    sq = att[:, 512 * (n % 2):512 * (n % 2) + 2 * w].rearrange("p (a b) -> p a b", a=2)
                    act.activation(sq, src, ACT.Square).then_inc(sq_ready, 1)
                    copy(dst[:, t, 2 * each * p:2 * each * (p + 1)], gbank(u)[:, 0:2 * each])\
                        .then_inc(gemm_free[u % 4], 1)
                    n += 1
            small_empty(SU["kpe"], kpT, T)
            for n in range(4):
                pair_empty(SU["qn"] + n, pair(qnT, n), col("q_nope"))
            for n in range(4):
                pair_empty(SU["kn"] + n, pair(knT, n), col("k_nope"))
            for n in range(2):
                pair_empty(SU["qp"] + n, pair(qpT, n))

            def causal_attention(name, count):
                def probabilities(h):
                    b = h % 2
                    act.wait_ge(max_ready, count + h + 1)
                    for tile, a, n in ((1, 0, 256), (0, 256, 128)):
                        ins = act.activation(att[:, 1024 + 512 * b + a:1024 + 512 * b + a + n],
                                             att[:, 512 * b + a:512 * b + a + n], ACT.Exp,
                                             bias=stat[:, 56 + 2 * b + tile:57 + 2 * b + tile],
                                             accum_out=stat[:, 60 + 2 * b + tile:61 + 2 * b + tile])
                    ins.then_inc(exp_done, 1)

                def transposed(h):
                    u = SU[name] + unit_c[("P", h)]
                    small_empty(u, att[:, 2048 + 1024 * (h % 2):2048 + 1024 * (h % 2) + 384], 384)

                def head_out(h):
                    u = SU[name] + unit_c[("O", h)]
                    small_out(act, u)
                    copy(acts[:, 1, 0, h * T:(h + 1) * T], sbank(u)[:, 0:T]).then_inc(out_hi, 1)

                for h in range(H + 2):
                    if h < H:
                        probabilities(h)
                    if 1 <= h <= H:
                        transposed(h - 1)
                    if h >= 2:
                        head_out(h - 2)

            causal_attention("att0", 0)

            def all_used(name, n):
                for j in range(n):
                    used(GC[name] + j)

            def t5_terms_of(n, i=None):
                b = n - 1
                if b < 1:
                    return
                k = 0 if i is None else i
                act.wait_ge(t5_above, 8 * k + b)
                if b >= 2:
                    act.wait_ge(pool_step, 40 * k + (5 * (b - 2) + 1))
                for h in range(3, H):
                    ins = copy(t5_term(b, h), above(b), deltas[:, bass.ds(8 * H * k + (H * b + h), 1)])
                ins.then_inc(t5_terms, 1)

            def square_relu(name, beside=None):
                def hidden(s, i=None):
                    u = GU[name] + s
                    act.activation(relu_t[:, s % 2, :], gbank(u)[:, :], ACT.Relu).then_inc(gemm_free[u % 4], 1)
                    act.wait_ge(gemm_free[u % 4], u // 4 + 1 if i is None else i + (u // 4 + 1))
                    act.activation(acts[:, 1, 0, 512 * (s % 2):512 * (s % 2) + 512], relu_t[:, s % 2, :], ACT.Square)\
                        .then_inc(hidden_hi, 1)

                mlp(name, 16, 3, hidden, beside)

            all_used("mla_o", 4)
            cols_hi("m0")
            square_relu("mlp0", t5_terms_of)
            t5_terms_of(BUCKETS)
            cols_hi("h1")
            c0, u0 = GC["qkv"], GU["qkv"]
            with act.Fori(0, 2) as i:
                for j in range(4):
                    used(c0 + j, i, 4)
                    for m in range(j - 1, j + 1) if j % 2 else ():
                        u = u0 + m
                        gemm_out(act, u, i)
                        act.wait_ge(sq_used, 4 * i + (15 + m))
                        act.activation(att[:, 512 * (m % 2):512 * (m % 2) + 512], gbank(u)[:, :], ACT.Square)\
                            .then_inc(sq_ready, 1)
                        copy(qkv[:, m % 2, bass.ds(i * 1024 + 512 * (m // 2), 512)], gbank(u)[:, :])\
                            .then_inc(gemm_free[u % 4], 1)
            for j in range(4):
                used(c0 + 8 + j)
                for m in range(j - 1, j + 1) if j % 2 else ():
                    empty(u0 + 8 + m, qkv[:, m % 2, 2048 + 512 * (m // 2):2560 + 512 * (m // 2)])
            for n in range(4):
                pair_empty(SU["q1"] + n, pair(q1T, n), col("moba_q"))
            for n in range(4):
                pair_empty(SU["k1"] + n, pair(k1T, n), col("moba_k"))
            causal_attention("att1", H)
            all_used("moba_o", 4)
            cols_hi("m1")
            square_relu("mlp1")

            cols_hi("hc", 1)
            cols_hi("hx")
            used(GC["dt"])
            act.wait_ge(sp_abs, 1)
            act.activation(tmp(2), tmp(1), ACT.Exp, scale=-1.0).then_inc(sp_exp, 1)
            act.activation(stat[:, 80:96], row("a_log"), ACT.Exp).then_inc(a_exp, 1)
            act.wait_ge(sp_u, 1)
            act.activation(tmp(4), tmp(3), ACT.Ln).then_inc(sp_ln, 1)
            conv_units = [(GU["xs"] + f, xsT[:, f, :], 512) for f in range(4)] \
                + [(GU["bc"] + g, BT[:, g, :], 512) for g in range(2)] \
                + [(GU["bc"] + 2 + g, CT[:, g, :], 256) for g in range(2)]
            for j in range(4):
                used(GC["xs"] + j)
                for n in (2 * j, 2 * j + 1):
                    u, y, m = conv_units[n]
                    gemm_out(act, u)
                    act.activation(y, gbank(u)[:, 0:m], ACT.Identity, scale=col("conv_w", 3 * n + 1, 1),
                                   bias=col("conv_b", n, 1)).then_inc(conv_mid, 1)
                for n in (2 * j, 2 * j + 1):
                    u, y, m = conv_units[n]
                    gemm_gone(act, u)
                    act.activation(y, y, ACT.Silu).then_inc(conv_act, 1)
            all_used("q", 2)
            for j in range(2):
                used(GC["k"] + j)
                u = GU["k"] + 3 * j + 2
                gemm_out(act, u)
                copy(nkT[:, 2 * j:2 * j + 2, T:2 * T], gbank(u)[:, :].rearrange("p (a b) -> p a b", a=2))\
                    .then_inc(gemm_free[u % 4], 1)
            all_used("z", 2)
            for t in range(2):
                u = GU["z"] + t
                gemm_out(act, u)
                act.activation(sz[:, t, :], gbank(u)[:, :], ACT.Silu).then_inc(gemm_free[u % 4], 1)
            all_used("v", 2)
            for m in range(4):
                empty(GU["v"] + m, (nv if m < 2 else ncv)[:, m % 2, :])
            small_gone(act, SU["cumcol"])
            act.activation(stat[:, 320:384], stat[:, 256:320], ACT.Exp).then_inc(ecum_ready, 1)
            u = SU["later"]
            small_out(act, u)
            act.activation(tmp(7), sbank(u)[:, 0:64], ACT.Exp).then_inc(small_free[u % 4], 1)
            for n in range(5):
                dst = (xsr[:, 0], xsr[:, 1], cxsr[:, 0], cxsr[:, 1], Bcr[:, :, :, :].rearrange("p a b c -> p (a b c)"))[n]
                small_empty(SU["xsrow"] + n, dst)
            for d in range(2):
                small_empty(SU["state"] + d, h0T[:, d, :])
            for n in range(2):
                pair_empty(SU["nq"] + n, pair(nqT, n), 0.125)
            for n in range(2):
                pair_empty(SU["nk"] + n, pair(nkT, n))

            def pair_out(p):
                gemm_out(act, GU["na_o"] + p)
                copy(acts[:, 1, 0, p * T:(p + 1) * T], gbank(GU["na_o"] + p)[:, 0:T]).then_inc(out_hi, 1)

            for i in range(2 * H + 1):
                if i < 2 * H:
                    u = SU["na"] + unit_w[("S", i)]
                    act.wait_ge(max_ready, 2 * H + i + 1)
                    act.activation(att[:, 1024 + 512 * (i % 2):1536 + 512 * (i % 2)], sbank(u)[:, :], ACT.Exp,
                                   bias=stat[:, 56 + i % 2:57 + i % 2], accum_out=stat[:, 60 + i % 2:61 + i % 2])\
                        .then_inc(small_free[u % 4], 1)
                if i:
                    h, t = (i - 1) // 2, (i - 1) % 2
                    u = SU["na"] + unit_w[("P", i - 1)]
                    small_out(act, u)
                    copy(view(att, 2048 + 1024 * (h % 2), 4, T)[:, :, t * P:(t + 1) * P], halves(u, 4, P))\
                        .then_inc(small_free[u % 4], 1)
                if i >= 8 and i % 4 == 0:
                    pair_out(i // 4 - 2)
            pair_out(3)
            for h in range(H):
                small_gone(act, SU["seg"] + h)
                act.activation(E[:, h % 2, :], E[:, h % 2, :], ACT.Exp).then_inc(seg_exp, 1)
            for n in range(2):
                u = SU["yT"] + n
                small_out(act, u)
                for a in range(2):
                    k = 4 + 2 * n + a
                    ins = copy(acts[:, 1, 0, k * T:(k + 1) * T], sbank(u)[:, T * a:T * (a + 1)],
                               col("ssd_norm", 2 * n + a, 1))
                ins.then_inc(act_hi, 1)
            all_used("out", 4)
            cols_hi("m2")

            def glu(s, i=None):
                u, b, k = GU["glu"] + s, s % 2, 0 if i is None else i
                w = cols[:, bass.ds(12 * k + (CA["fconv_w"] + 3 * s + 1), 1)]
                bb = cols[:, bass.ds(4 * k + (CA["fconv_b"] + s), 1)]
                released(act, GC["glu"] + s, i, 4)
                act.activation(gact[:, b, :], gbank(u)[:, 0:T], ACT.Identity, scale=w, bias=bb).then_inc(glu_mid, 1)
                if s + 2 < KF2:
                    split_hi(GC["glu"] + s + 2, i, 4)
                act.wait_ge(glu_taps, 4 * k + (s + 1))
                act.activation(gact[:, b, :], gact[:, b, :], ACT.Silu).then_inc(glu_act, 1)
                act.wait_ge(gemm_free[u % 4], u // 4 + 1 + k)
                copy(acts[:, 1, 0, 512 * b:512 * b + T], prod_t[:, b, :]).then_inc(hidden_hi, 1)
                act.wait_ge(down_loaded[b], 32 * k + 16 * (s // 2 + 1))
                if s:
                    act.wait_ge(glu_used, 4 * k + s)
                copy(split_down[:, 0, :], raw_down[:, b, :]).then_inc(down_hi, 1)

            glu(0)
            with act.Fori(0, 4) as i:
                for s in range(1, 5):
                    glu(s, i)
            for s in range(17, KF2):
                glu(s)

        @block.vector
        def _(v):
            st = Steps(v, dve_step)
            step, settle = st.step, st.settle
            roots = []

            def inverse_rms(at, widths):
                a = at
                for n, width in widths:
                    ins = v.tensor_scalar(stat[:, a:a + n], stat[:, a:a + n], 1.0 / width, EPS, ALU.mult, ALU.add)
                    a += n
                    if (n, width) != widths[-1] or a - at != sum(w[0] for w in widths):
                        step(ins)
                ins.then_inc(means_ready, 1)
                roots.append((at, a))
                assert roots[-1] == ROOTS[len(roots) - 1]
                v.wait_ge(roots_ready, len(roots))

            def sum_squares(src, junk, at):
                step(v.tensor_tensor_reduce(out=junk, in0=src, in1=src, scale=1.0, scalar=0.0, op0=ALU.mult,
                                            op1=ALU.add, accum_out=stat[:, at:at + 1]))

            def norm_rows(src, dst, junk):
                for t in range(2):
                    sum_squares(src[:, t, :], junk[:, t, :], t)
                settle()
                inverse_rms(0, [(2, D)])
                for t in range(2):
                    v.tensor_scalar(dst[:, t, :], src[:, t, :], stat[:, t:t + 1], None, ALU.mult).then_inc(normed, 1)

            def quarters(u):
                return sbank(u)[:, :].rearrange("p (a b) -> p a b", a=4)

            def split_lo(c, i=None, pitch=0):
                v.wait_ge(hi_ready, c + 1 if i is None else pitch * i + (c + 1))
                n = chunk_width(c)
                v.tensor_tensor(split[:, c % 2, 1, 0:n], raw[:, c % 2, 0:n], split[:, c % 2, 0, 0:n].bitcast(F32),
                                ALU.subtract).then_inc(lo_ready, 1)

            def used(c, i=None, pitch=0):
                if c + 2 < CHUNKS:
                    split_lo(c + 2, i, pitch)

            def all_used(name, n):
                for j in range(n):
                    used(GC[name] + j)

            def cols_out(name, gain, shift=None, which=0):
                for n in range(5):
                    if n < 4:
                        u, k = SU[name] + n, 4 * (n % 2)
                        dst = quarters_of(n)
                        small_out(v, u)
                        g = spread(gain[:, k:k + 4], 1, P)
                        if shift is None:
                            v.tensor_tensor(dst, quarters(u), g, ALU.mult).then_inc(small_free[u % 4], 1)
                        else:
                            step(v.tensor_tensor(dst, quarters(u), g, ALU.mult))
                            settle()
                            v.tensor_tensor(dst, dst, spread(shift[:, k:k + 4], 1, P), ALU.add)\
                                .then_inc(small_free[u % 4], 1)
                    if n:
                        m = n - 1
                        k, t = 4 * (m % 2), m // 2
                        v.wait_ge(act_hi, HI0[name] + m + 1)
                        v.tensor_tensor(tokens_of(which, 1, k, t), quarters_of(m),
                                        tokens_of(which, 0, k, t).bitcast(F32), ALU.subtract).then_inc(act_lo, 1)
                v.wait_ge(act_lo, LO[name])

            def scaled_lo(name, n, k0, tiles, gain, hi):
                u = SU[name] + n
                v.wait_ge(act_hi, hi)
                for a in range(tiles):
                    at = (k0 + a) * T
                    ins = v.scalar_tensor_tensor(acts[:, 1, 1, at:at + T], sbank(u)[:, a * T:(a + 1) * T],
                                                 gain[:, a:a + 1], acts[:, 1, 0, at:at + T].bitcast(F32),
                                                 ALU.mult, ALU.subtract)
                    if a < tiles - 1:
                        step(ins)
                ins.then_inc(small_free[u % 4], 1)

            def add_units(units, ns, small=False, gate=None):
                free, bank = (small_free, sbank) if small else (gemm_free, gbank)
                for n in ns:
                    u, half, t = units + n, n // 2, n % 2
                    dst = x[:, t, 512 * half:512 * (half + 1)]
                    (small_out if small else gemm_out)(v, u)
                    if gate is None:
                        v.tensor_tensor(dst, bank(u)[:, :], dst, ALU.add).then_inc(free[u % 4], 1)
                    else:
                        tm = att[:, 512 * n:512 * (n + 1)]
                        v.tensor_tensor(tm, bank(u)[:, :], gates[:, gate, 512 * half:512 * (half + 1)], ALU.mult)\
                            .then_inc(free[u % 4], 1)
                for n in ns:
                    (small_gone if small else gemm_gone)(v, units + n)
                if gate is not None:
                    for n in ns:
                        half, t = n // 2, n % 2
                        dst = x[:, t, 512 * half:512 * (half + 1)]
                        step(v.tensor_tensor(dst, dst, att[:, 512 * n:512 * (n + 1)], ALU.add))
                    settle()

            def project_to_x(name, gate=None):
                for j in range(4):
                    used(GC[name] + j)
                    if j % 2:
                        add_units(GU[name], (j - 1, j), gate=gate)

            def mlp(name, steps, turns, per, hidden, beside=None, peel=0):
                c0, seq = GC[name], alternate(steps)

                def chunk(n, i=None):
                    used(c0 + n, i, 8)
                    if not seq[n][0]:
                        hidden(seq[n][1], i)
                    if beside:
                        beside(n, i)

                for n in range(3 + 8 * peel):
                    chunk(n)
                with v.Fori(peel, turns) as i:
                    st.enter(i, per, peel)
                    for n in range(3, 11):
                        chunk(n, i)
                st.leave(turns - peel)
                for n in range(3 + 8 * turns, len(seq)):
                    chunk(n)

            v.wait_ge(x_in_sb, 16)
            norm_rows(x, xn, xn)
            v.wait_ge(params_in, 80)
            split_lo(0)
            split_lo(1)
            cols_out("h0", col("attn_norm", 0, 8))
            ang, turns, cosines, sines = (bias[:, a:a + 64] for a in (0, 64, 128, 192))
            step(v.tensor_copy(posf[:, :], posc[:, :]))
            settle()
            for t in range(2):
                step(v.tensor_scalar(ang[:, 32 * t:32 * t + 32], const("inv_freq"), posf[:, t:t + 1], None, ALU.mult))
            settle()
            step(v.tensor_scalar(turns, ang, 1.0 / (2 * math.pi), MAGIC, ALU.mult, ALU.add))
            settle()
            step(v.tensor_scalar(turns, turns, MAGIC, None, ALU.subtract))
            settle()
            rest = 2 * math.pi
            for bits in (3, 14, 34):
                part_ = math.floor(rest * 2 ** (bits + 2)) / 2 ** (bits + 2) if bits < 34 else rest
                rest -= part_
                step(v.scalar_tensor_tensor(ang, turns, -part_, ang, ALU.mult, ALU.add))
                settle()
            pi32 = 3.1415925
            step(v.tensor_scalar(sines, ang, pi32, -pi32, ALU.min, ALU.max))
            settle()
            step(v.scalar_tensor_tensor(cosines, sines, -1.0, sines, ALU.mult, ALU.min))
            settle()
            v.tensor_scalar(cosines, cosines, math.pi / 2, None, ALU.add).then_inc(angles, 1)
            all_used("mla_in", 4)
            for u in range(4):
                gemm_gone(v, GU["mla_in"] + u)
            widths = ((0, QR), (QR, KVR), (QR + KVR, ROPE))
            for s_, (a, n) in enumerate(widths):
                for t in range(2):
                    sum_squares(proj[:, t, a:a + n], xn[:, t, a:a + n], 2 + 2 * s_ + t)
            settle()
            inverse_rms(2, [(2, n) for _, n in widths])
            for s_, (a, n) in enumerate(widths[:2]):
                for t in range(2):
                    ins = v.tensor_scalar(proj[:, t, a:a + n], proj[:, t, a:a + n],
                                          stat[:, 2 + 2 * s_ + t:3 + 2 * s_ + t], None, ALU.mult)
                    if (s_, t) == (1, 1):
                        ins.then_inc(latents_normed, 1)
                    else:
                        step(ins)
            kp = [proj[:, t, QR + KVR:QR + KVR + ROPE] for t in range(2)]
            for t in range(2):
                step(v.scalar_tensor_tensor(kp[t], kp[t], stat[:, 6 + t:7 + t], row("k_rope"), ALU.mult, ALU.mult))
            settle()
            v.wait_ge(rotations, 1)
            kpv = proj[:, :, QR + KVR:QR + KVR + ROPE]
            kt = [view(att, 2048 + 64 * k, 2, 32) for k in range(4)]
            for k, (a, r) in enumerate(((0, 0), (1, 1), (1, 0), (0, 1))):
                step(v.tensor_tensor(kt[k], kpv[:, :, 32 * a:32 * a + 32], rot[:, r, :, :], ALU.mult))
            settle()
            step(v.tensor_tensor(kpe2[:, :, 0:32], kt[0], kt[1], ALU.subtract))
            step(v.tensor_tensor(kpe2[:, :, 32:64], kt[2], kt[3], ALU.add))
            settle()
            step(v.tensor_copy(kpe2[:, :, 64:128], kpe2[:, :, 0:64]))
            for n, fs in enumerate((2, 2, 1)):
                scaled_lo("cT", n, 2 * n, fs, col("c_norm", 2 * n, fs), HI0["cT"] + n + 1)
            for n in range(16):
                t, p = n % 2, n % 8 // 2
                if n < 8 and n % 2 == 0:
                    used(GC["mla_uq"] + n // 2)
                elif n % 4 == 0:
                    used(GC["mla_ukv"] + (n - 8) // 4)
                v.wait_ge(sq_ready, n + 1)
                w = 192 if n < 8 else NOPE
                sq = att[:, 512 * (n % 2):512 * (n % 2) + 2 * w].rearrange("p (a b) -> p a b", a=2)
                at = (8 if n < 8 else 40) + 8 * t + 2 * p
                if n < 8:
                    step(v.tensor_reduce(stat[:, at + 16:at + 18], sq[:, :, NOPE:192], AX.X, ALU.add))
                v.tensor_reduce(stat[:, at:at + 2], sq[:, :, 0:NOPE], AX.X, ALU.add).then_inc(sq_used, 1)
            v.wait_ge(sq_used, 16)
            settle()
            inverse_rms(8, [(16, NOPE), (16, ROPE), (16, NOPE)])
            for u in range(8):
                gemm_gone(v, GU["mla_uq"] + u)
                gemm_gone(v, GU["mla_ukv"] + u)
            qh = q0[:, :, :].rearrange("p t (h d) -> p (t h) d", d=192)
            kh = kv[:, :, :].rearrange("p t (h d) -> p (t h) d", d=256)
            step(v.tensor_tensor(qh[:, :, 0:NOPE], qh[:, :, 0:NOPE], spread(stat[:, 8:24], 1, NOPE), ALU.mult))
            v.tensor_tensor(kh[:, :, 0:NOPE], kh[:, :, 0:NOPE], spread(stat[:, 40:56], 1, NOPE), ALU.mult)\
                .then_inc(heads_normed, 1)
            qp = qh[:, :, NOPE:192]
            step(v.tensor_tensor(qp, qp, spread(stat[:, 24:40], 1, ROPE), ALU.mult))
            settle()
            step(v.tensor_tensor(qp, qp, spread(row("q_rope"), 0, 16), ALU.mult))
            settle()
            qr = q0[:, :, :].rearrange("p t (h d) -> p t h d", d=192)
            xr = xn[:, :, 0:512].rearrange("p t (h d) -> p t h d", d=64)
            tm = [view(att, 2048 + 512 * k, 2, 8, 32) for k in range(4)]
            for k, (a, r) in enumerate(((0, 0), (1, 1), (1, 0), (0, 1))):
                for t in range(2):
                    step(v.tensor_tensor(tm[k][:, t], qr[:, t, :, NOPE + 32 * a:NOPE + 32 * a + 32],
                                         spread(rot[:, r, t, :], 0, 8), ALU.mult))
            settle()
            for t in range(2):
                step(v.tensor_tensor(xr[:, t, :, 0:32], tm[0][:, t], tm[1][:, t], ALU.subtract))
                ins = v.tensor_tensor(xr[:, t, :, 32:64], tm[2][:, t], tm[3][:, t], ALU.add)
                if t:
                    ins.then_inc(heads_normed, 1)
                else:
                    step(ins)

            def causal_attention(name, scale, bias_of, count):
                def logits(h):
                    b = h % 2
                    u = SU[name] + unit_c[("S", h)]
                    small_out(v, u)
                    lg = att[:, 512 * b:512 * b + 384]
                    v.scalar_tensor_tensor(lg, sbank(u)[:, 0:384], scale, bias_of(h), ALU.mult, ALU.add)\
                        .then_inc(small_free[u % 4], 1)
                    small_gone(v, u)
                    step(v.tensor_reduce(stat[:, 57 + 2 * b:58 + 2 * b], lg[:, 0:256], AX.X, ALU.max, negate=True))
                    v.tensor_reduce(stat[:, 56 + 2 * b:57 + 2 * b], lg[:, 256:384], AX.X, ALU.max, negate=True)\
                        .then_inc(max_ready, 1)

                def normalise(h):
                    b = h % 2
                    v.wait_ge(exp_done, count + h + 1)
                    step(v.reciprocal(stat[:, 64 + 2 * b:66 + 2 * b], stat[:, 60 + 2 * b:62 + 2 * b]))
                    settle()
                    pr = att[:, 1024 + 512 * b:1024 + 512 * b + 384]
                    step(v.tensor_scalar(pr[:, 0:256], pr[:, 0:256], stat[:, 65 + 2 * b:66 + 2 * b], None, ALU.mult))
                    v.tensor_scalar(pr[:, 256:384], pr[:, 256:384], stat[:, 64 + 2 * b:65 + 2 * b], None, ALU.mult)\
                        .then_inc(probs_ready, 1)

                def head_lo(h):
                    u = SU[name] + unit_c[("O", h)]
                    v.wait_ge(out_hi, count + h + 1)
                    v.tensor_tensor(acts[:, 1, 1, h * T:(h + 1) * T], sbank(u)[:, 0:T],
                                    acts[:, 1, 0, h * T:(h + 1) * T].bitcast(F32), ALU.subtract)\
                        .then_inc(small_free[u % 4], 1)

                for h in range(H + 2):
                    if h < H:
                        logits(h)
                    if 1 <= h <= H:
                        normalise(h - 1)
                    if h >= 2:
                        head_lo(h - 2)

            causal_attention("att0", 1.0 / math.sqrt(NOPE + ROPE), lambda h: const("causal"), 0)
            project_to_x("mla_o")
            norm_rows(x, xn, xn)
            cols_out("m0", col("mlp_norm", 0, 8))

            def square_relu(name):
                def hidden(s, i=None):
                    u, b = GU[name] + s, s % 2
                    v.wait_ge(gemm_free[u % 4], u // 4 + 1 if i is None else i + (u // 4 + 1))
                    step(v.tensor_tensor(square_t[:, b, :], relu_t[:, b, :], relu_t[:, b, :], ALU.mult))
                    settle()
                    v.wait_ge(hidden_hi, HID0[name] + s + 1 if i is None else 4 * i + (HID0[name] + s + 1))
                    v.tensor_tensor(acts[:, 1, 1, 512 * b:512 * b + 512], square_t[:, b, :],
                                    acts[:, 1, 0, 512 * b:512 * b + 512].bitcast(F32), ALU.subtract)\
                        .then_inc(act_lo, 1)
                return hidden

            table = row("table")
            step(v.tensor_scalar(dist[:, 0:256], posr[:, :], -1.0, posf[:, 1:2], ALU.mult, ALU.add))
            step(v.tensor_scalar(dist[:, 256:384], posr[:, 0:P], -1.0, posf[:, 0:1], ALU.mult, ALU.add))
            step(v.tensor_tensor(deltas[:, H:], table[:, H:], table[:, 0:-H], ALU.subtract))
            for h in range(H):
                ins = v.tensor_scalar(bias[:, 384 * h:384 * h + 384], const("causal"), table[:, h:h + 1], None, ALU.add)
                if h < H - 1:
                    step(ins)
            ins.then_inc(t5_start, 1)
            v.wait_ge(t5_start, 1)

            def bucket_step(b, i=None):
                if b == 0:
                    return
                k = 0 if i is None else i
                settle()
                if b > 2:
                    v.wait_ge(t5_terms, 8 * k + (b - 2))
                v.tensor_scalar(above(b), dist, const("thresholds")[:, bass.ds(8 * k + b, 1)], None, ALU.is_ge)\
                    .then_inc(t5_above, 1)
                v.wait_ge(t5_above, 8 * k + b)
                for h in range(3):
                    acc = bias[:, 384 * h:384 * h + 384]
                    step(v.scalar_tensor_tensor(acc, above(b), deltas[:, bass.ds(8 * H * k + (H * b + h), 1)], acc,
                                                ALU.mult, ALU.add))

            mlp("mlp0", 16, 3, 28, square_relu("mlp0"), bucket_step)
            add_units(SU["d0"], range(4), small=True)
            norm_rows(x, xn, xn)
            cols_out("h1", col("attn_norm", 8, 8))
            with v.Fori(0, 2) as i:
                for j in range(4):
                    used(GC["qkv"] + j, i, 4)
                    for m in range(j - 1, j + 1) if j % 2 else ():
                        v.wait_ge(sq_ready, 4 * i + (17 + m))
                        sq = att[:, 512 * (m % 2):512 * (m % 2) + 512].rearrange("p (a b) -> p a b", a=4)
                        v.tensor_reduce(stat[:, bass.ds(8 * i + (8 + 16 * (m % 2) + 4 * (m // 2)), 4)], sq, AX.X,
                                        ALU.add).then_inc(sq_used, 1)
            used(GC["qkv"] + 8)
            v.wait_ge(sq_used, 24)
            inverse_rms(8, [(32, P)])
            for u in range(8):
                gemm_gone(v, GU["qkv"] + u)
            for t in range(2):
                used(GC["qkv"] + 9 + t)
                qk = qkv[:, t, 0:2 * D].rearrange("p (h d) -> p h d", d=P)
                ins = v.tensor_tensor(qk, qk, spread(stat[:, 8 + 16 * t:24 + 16 * t], 1, P), ALU.mult)
                if t:
                    ins.then_inc(heads_normed, 1)
                else:
                    step(ins)
            used(GC["qkv"] + 11)
            v.wait_ge(pool_step, 5 * (BUCKETS - 1) + 1)
            causal_attention("att1", 1.0 / math.sqrt(P), lambda h: bias[:, 384 * h:384 * h + 384], H)
            project_to_x("moba_o")
            norm_rows(x, xn, xn)
            cols_out("m1", col("mlp_norm", 8, 8))
            v.wait_ge(ctx_in_sb, 16)
            norm_rows(ctx, ctx, xn)
            v.wait_ge(silu_c, 1)

            def ada_half(n, i=None):
                if not 3 <= n < 3 + 24:
                    return
                k = 0 if i is None else i
                chunk, half_ = (n - 3) // 2, (n - 3) % 2
                v.wait_ge(ada_in[half_], 64 * k + 16 * (chunk + 1))
                if half_:
                    v.wait_ge(ada_used, 8 * k + (2 * chunk + 1))
                outs = [(0, chunk * 512)] + ([(1, (12 + chunk) * 512)] if i is None else [])
                for kk in range(4):
                    w = bias[:, 2048 * half_ + 512 * kk:2048 * half_ + 512 * (kk + 1)]
                    if kk:
                        settle()
                    for who, at in outs:
                        dst = arena[:, bass.ds(2048 * k + (4096 + at), 512)]
                        if half_ == 0 and kk == 0:
                            ins = v.tensor_scalar(dst, w, sc[:, who, 0:1], None, ALU.mult)
                        else:
                            ins = v.scalar_tensor_tensor(dst, w, sc[:, who, 4 * half_ + kk:4 * half_ + kk + 1], dst,
                                                         ALU.mult, ALU.add)
                        if kk == 3 and (who, at) == outs[-1]:
                            ins.then_inc(ada_used, 1)
                        else:
                            step(ins)

            mlp("mlp1", 16, 3, 28, square_relu("mlp1"), ada_half, peel=1)
            add_units(SU["d1"], range(4), small=True)
            norm_rows(x, xn, xn)
            u = SU["ada"]
            small_out(v, u)
            step(v.tensor_tensor(adac[:, 0:32], sbank(u)[:, 0:32], col("ada_cols"), ALU.add))
            v.tensor_tensor(adac[:, 32:48], sbank(u)[:, 32:48], col("ada_cols", 0, 16), ALU.add)\
                .then_inc(small_free[u % 4], 1)
            settle()
            small_gone(v, u)
            for dst, scale, gain in ((48, 8, "norm1"), (56, 24, "norm2"), (64, 40, "norm1")):
                step(v.scalar_tensor_tensor(adac[:, dst:dst + 8], adac[:, scale:scale + 8], 1.0, col(gain),
                                            ALU.add, ALU.mult))
            v.wait_ge(gates_in, 16)
            for g in range(4):
                u = SU["ada"] + 1 + g
                small_out(v, u)
                v.tensor_tensor(gates[:, g // 2, 512 * (g % 2):512 * (g % 2) + 512], sbank(u)[:, :],
                                gates[:, g // 2, 512 * (g % 2):512 * (g % 2) + 512], ALU.add).then_inc(small_free[u % 4], 1)
            settle()
            for g in range(4):
                small_gone(v, SU["ada"] + 1 + g)
            cols_out("hc", adac[:, 64:72], adac[:, 32:40], 1)
            cols_out("hx", adac[:, 48:56], adac[:, 0:8])
            z_, az, ez, uz, lz, se, mk = (tmp(k) for k in range(7))
            dt = stat[:, 96:160]
            used(GC["dt"])
            u = GU["dt"]
            gemm_out(v, u)
            v.tensor_tensor(z_.rearrange("p (a b) -> p a b", a=4), gbank(u)[:, 0:64].rearrange("p (a b) -> p a b", a=4),
                            spread(row("dt_bias"), 0, 4), ALU.add).then_inc(gemm_free[u % 4], 1)
            gemm_gone(v, u)
            v.scalar_tensor_tensor(az, z_, -1.0, z_, ALU.mult, ALU.max).then_inc(sp_abs, 1)
            v.wait_ge(sp_exp, 1)
            v.tensor_scalar(uz, ez, 1.0, None, ALU.add).then_inc(sp_u, 1)
            step(v.tensor_scalar(se, ez, 1.0 / 3, -0.5, ALU.mult, ALU.add))
            step(v.tensor_scalar(mk, ez, 0.01, None, ALU.is_lt))
            settle()
            step(v.tensor_tensor(se, se, ez, ALU.mult))
            settle()
            step(v.scalar_tensor_tensor(se, se, 1.0, ez, ALU.add, ALU.mult))
            settle()
            v.wait_ge(sp_ln, 1)
            for op, b in ((ALU.subtract, lz), (ALU.mult, mk), (ALU.add, lz)):
                step(v.tensor_tensor(se, se, b, op))
                settle()
            step(v.scalar_tensor_tensor(dt, z_, 0.0, se, ALU.max, ALU.add))
            settle()
            v.wait_ge(a_exp, 1)
            v.scalar_tensor_tensor(stat[:, 160:224].rearrange("p (a b) -> p a b", a=4), dt.rearrange("p (a b) -> p a b", a=4),
                                   -1.0, spread(stat[:, 80:96], 0, 4), ALU.mult, ALU.mult).then_inc(dA_ready, 1)
            conv_units = [(GU["xs"] + f, xsT[:, f, :], 2) for f in range(4)] \
                + [(GU["bc"] + g, BT[:, g, :], 2) for g in range(2)] + [(GU["bc"] + 2 + g, CT[:, g, :], 1) for g in range(2)]
            for n, (u, y, m) in enumerate(conv_units):
                if n % 2 == 0:
                    used(GC["xs"] + n // 2)
                v.wait_ge(conv_mid, n + 1)
                y = y.rearrange("p (a b) -> p a b", a=m)
                src = gbank(u)[:, 0:m * T].rearrange("p (a b) -> p a b", a=m)
                step(v.scalar_tensor_tensor(y[:, :, 1:T], src[:, :, 0:T - 1], col("conv_w", 3 * n, 1), y[:, :, 1:T],
                                            ALU.mult, ALU.add))
                settle()
                v.scalar_tensor_tensor(y[:, :, 0:T - 1], src[:, :, 1:T], col("conv_w", 3 * n + 2, 1), y[:, :, 0:T - 1],
                                       ALU.mult, ALU.add).then_inc(gemm_free[u % 4], 1)
            grid = const("grid")
            rotated = [(GU["q"] + t, t, 0, 8) for t in range(2)] \
                + [(GU["k"] + 3 * j + t, t, NA + 256 * j, 4) for j in range(2) for t in range(2)]
            for n, (u, t, at, heads_) in enumerate(rotated):
                if n == 0:
                    all_used("q", 2)
                elif n in (2, 4):
                    used(GC["k"] + n // 2 - 1)
                gemm_out(v, u)
                src = gbank(u)[:, 0:64 * heads_].rearrange("p (h d) -> p h d", d=64)
                tm = [view(att, 2048 + 1024 * (n % 2) + 256 * k, heads_, 32) for k in range(4)]
                for k, (a, r) in enumerate(((0, 0), (1, 1), (1, 0), (0, 1))):
                    ins = v.tensor_tensor(tm[k], src[:, :, 32 * a:32 * a + 32],
                                          spread(grid[:, 64 * t + 32 * r:64 * t + 32 * r + 32], 0, heads_), ALU.mult)
                    if k == 3:
                        ins.then_inc(gemm_free[u % 4], 1)
                    else:
                        step(ins)
                settle()
                gemm_gone(v, u)
                dst = nqk[:, t, at:at + 64 * heads_].rearrange("p (h d) -> p h d", d=64)
                step(v.tensor_tensor(dst[:, :, 0:32], tm[0], tm[1], ALU.subtract))
                ins = v.tensor_tensor(dst[:, :, 32:64], tm[2], tm[3], ALU.add)
                if n == len(rotated) - 1:
                    ins.then_inc(nqk_ready, 1)
                else:
                    step(ins)
            settle()
            all_used("z", 2)
            all_used("v", 2)
            u = SU["cum"]
            small_out(v, u)
            v.tensor_copy(cum, sbank(u)[0:16, :]).then_inc(small_free[u % 4], 1)
            u = SU["cumcol"]
            small_out(v, u)
            v.tensor_copy(stat[:, 256:320], sbank(u)[:, 0:64]).then_inc(small_free[u % 4], 1)
            small_gone(v, SU["later"])
            lx = tmp(7).rearrange("p (l d h) -> p l d h", l=2, d=2)
            wl = tmp(8)[:, 0:32].rearrange("p (l d h) -> p l d h", l=2, d=2)
            dtv = dt.rearrange("p (a b) -> p a b", a=4)
            for d in range(2):
                step(v.tensor_tensor(wl[:, :, d, :], lx[:, :, d, 8 * d:8 * d + 8], dtv[:, 2:4, 8 * d:8 * d + 8], ALU.mult))
            settle()
            for t in range(2):
                small_gone(v, SU["xsrow"] + 2 + t)
            for t in range(2):
                for d in range(2):
                    v.tensor_tensor(xw[:, t, d, :].rearrange("p (h q) -> p h q", q=64),
                                    cxsr[:, t, :].rearrange("p (h q) -> p h q", q=64),
                                    spread(wl[:, t, d, :], 1, 64), ALU.mult).then_inc(xw_ready, 1)
            v.wait_ge(xw_ready, 4)
            for g in range(2):
                u = SU["cb"] + g
                small_out(v, u)
                b = sbank(u)
                upto, since = const("upto", 0, P), const("since", P, P)
                step(v.tensor_tensor(cbm[:, g, 0:128], b[:, 0:128], upto, ALU.mult))
                step(v.tensor_copy(cbm[:, g, 128:256], b[:, 128:256]))
                step(v.tensor_tensor(cbm[:, g, 256:384], b[:, 384:512], upto, ALU.mult))
                step(v.tensor_tensor(cbm[:, g, 384:512], b[:, 0:128], since, ALU.mult))
                step(v.tensor_copy(cbm[:, g, 512:640], b[:, 256:384]))
                v.tensor_tensor(cbm[:, g, 640:768], b[:, 384:512], since, ALU.mult).then_inc(small_free[u % 4], 1)
            v.wait_ge(rpb_loaded, 16)

            def window_logits(i):
                h, t, b = i // 2, i % 2, i % 2
                u = SU["na"] + unit_w[("S", i)]
                small_out(v, u)
                bs = bias[:, (8 * t + h) * T:(8 * t + h + 1) * T]
                step(v.tensor_tensor(sbank(u)[:, 0:T], sbank(u)[:, 0:T], bs, ALU.add))
                settle()
                v.tensor_reduce(stat[:, 56 + b:57 + b], sbank(u)[:, :], AX.X, ALU.max, negate=True)\
                    .then_inc(max_ready, 1)

            def window_normalise(i):
                b = i % 2
                small_gone(v, SU["na"] + unit_w[("S", i)])
                step(v.reciprocal(stat[:, 64 + b:65 + b], stat[:, 60 + b:61 + b]))
                settle()
                pr = att[:, 1024 + 512 * b:1536 + 512 * b]
                v.tensor_scalar(pr, pr, stat[:, 64 + b:65 + b], None, ALU.mult).then_inc(probs_ready, 1)

            def pair_lo(p):
                u = GU["na_o"] + p
                v.wait_ge(out_hi, 2 * H + p + 1)
                v.tensor_tensor(acts[:, 1, 1, p * T:(p + 1) * T], gbank(u)[:, 0:T],
                                acts[:, 1, 0, p * T:(p + 1) * T].bitcast(F32), ALU.subtract)\
                    .then_inc(gemm_free[u % 4], 1)

            for i in range(2 * H + 1):
                if i < 2 * H:
                    window_logits(i)
                if i:
                    window_normalise(i - 1)
                if i >= 8 and i % 4 == 0:
                    pair_lo(i // 4 - 2)
            pair_lo(3)

            parts = ((0, 256, 0, 0), (256, 384, 128, 1), (384, 512, 256, 0), (512, 768, 256, 1))

            def decay(h):
                u = SU["seg"] + h
                small_out(v, u)
                if h >= 2:
                    v.wait_ge(w_mat, h - 1)
                for n, (a, e, src, t) in enumerate(parts):
                    c = 256 + 16 * t + h if n < 2 else 256 + 32 + 16 * t + 8 + h
                    ins = v.tensor_scalar(E[:, h % 2, a:e], sbank(u)[:, src:src + e - a], stat[:, c:c + 1], 0.0,
                                          ALU.subtract, ALU.min)
                    if n == 3:
                        ins.then_inc(small_free[u % 4], 1)
                    else:
                        step(ins)

            def matrix(h):
                v.wait_ge(seg_exp, h + 1)
                if h >= 2:
                    v.wait_ge(y_used, h - 1)
                for n, (a, e, src, t) in enumerate(parts):
                    c = 96 + 16 * t + h if n < 2 else 96 + 16 * t + 8 + h
                    ins = v.scalar_tensor_tensor(Wm[:, h % 2, a:e], E[:, h % 2, a:e], stat[:, c:c + 1],
                                                 cbm[:, h // 4, a:e], ALU.mult, ALU.mult)
                    if n == 3:
                        ins.then_inc(w_mat, 1)
                    else:
                        step(ins)

            for g in range(2):
                small_gone(v, SU["cb"] + g)
            small_gone(v, SU["cumcol"])
            settle()
            decay(0)
            for h in range(H):
                if h + 1 < H:
                    decay(h + 1)
                matrix(h)
            v.wait_ge(ecum_ready, 1)
            for t in range(2):
                small_gone(v, SU["xsrow"] + t)
            heads = lambda ap: ap.rearrange("p (h q) -> p h q", q=64)
            for t in range(2):
                step(v.tensor_tensor(heads(yrow[:, t, :]), heads(xsr[:, t, :]), spread(row("ssd_d"), 1, 64), ALU.mult))
            settle()
            for t in range(2):
                u = GU["y"] + t
                gemm_out(v, u)
                v.tensor_tensor(yrow[:, t, :], gbank(u)[:, :], yrow[:, t, :], ALU.add).then_inc(gemm_free[u % 4], 1)
                gemm_gone(v, u)
                for d in range(2):
                    u = SU["yoff"] + 2 * t + d
                    tm = att[:, 512 * d:512 * (d + 1)]
                    small_out(v, u)
                    c = 320 + 32 * d + 16 * t + 8 * d
                    v.tensor_tensor(heads(tm), heads(sbank(u)[:, :]), spread(stat[:, c:c + 8], 1, 64), ALU.mult)\
                        .then_inc(small_free[u % 4], 1)
                    small_gone(v, u)
                    step(v.tensor_tensor(yrow[:, t, :], yrow[:, t, :], tm, ALU.add))
                    settle()
                step(v.tensor_tensor(yrow[:, t, :], yrow[:, t, :], sz[:, t, :], ALU.mult))
            settle()
            for t in range(2):
                sum_squares(yrow[:, t, :], att[:, 512 * t:512 * (t + 1)], t)
            settle()
            inverse_rms(0, [(2, NA)])
            for t in range(2):
                ins = v.tensor_scalar(yrow[:, t, :], yrow[:, t, :], stat[:, t:t + 1], None, ALU.mult)
                if t:
                    ins.then_inc(normed, 1)
                else:
                    step(ins)
            for n in range(2):
                scaled_lo("yT", n, 4 + 2 * n, 2, col("ssd_norm", 2 * n, 2), HI0["yT"] + n + 1)
            project_to_x("out", 0)
            norm_rows(x, xn, xn)
            cols_out("m2", adac[:, 56:64], adac[:, 16:24])

            def glu(s, i=None):
                u, b, k = GU["glu"] + s, s % 2, 0 if i is None else i
                v.wait_ge(glu_mid, 4 * k + (s + 1))
                for tap in (0, 2):
                    w = cols[:, bass.ds(12 * k + (CA["fconv_w"] + 3 * s + tap), 1)]
                    y = gact[:, b, 1:T] if tap == 0 else gact[:, b, 0:T - 1]
                    src = gbank(u)[:, 0:T - 1] if tap == 0 else gbank(u)[:, 1:T]
                    if tap:
                        settle()
                    ins = v.scalar_tensor_tensor(y, src, w, y, ALU.mult, ALU.add)
                    if tap:
                        ins.then_inc(glu_taps, 1)
                    else:
                        step(ins)
                if s + 2 < KF2:
                    split_lo(GC["glu"] + s + 2, i, 4)
                v.wait_ge(glu_act, 4 * k + (s + 1))
                v.tensor_tensor(prod_t[:, b, :], gbank(u)[:, T:2 * T], gact[:, b, :], ALU.mult)\
                    .then_inc(gemm_free[u % 4], 1)
                v.wait_ge(hidden_hi, 4 * k + (HID0["glu"] + s + 1))
                v.tensor_tensor(acts[:, 1, 1, 512 * b:512 * b + T], prod_t[:, b, :],
                                acts[:, 1, 0, 512 * b:512 * b + T].bitcast(F32), ALU.subtract).then_inc(act_lo, 1)
                v.wait_ge(down_hi, 4 * k + (s + 1))
                v.tensor_tensor(split_down[:, 1, :], raw_down[:, b, :], split_down[:, 0, :].bitcast(F32), ALU.subtract)\
                    .then_inc(down_lo, 1)

            glu(0)
            with v.Fori(0, 4) as i:
                st.enter(i, 4)
                for s in range(1, 5):
                    glu(s, i)
            st.leave(4)
            for s in range(17, KF2):
                glu(s)
            add_units(SU["d2"], range(4), small=True, gate=1)
            for t in range(2):
                sum_squares(x[:, t, :], xn[:, t, :], t)
            settle()
            inverse_rms(0, [(2, D)])
            v.wait_ge(final_in, 16)
            for t in range(2):
                v.scalar_tensor_tensor(xn[:, t, :], x[:, t, :], stat[:, t:t + 1], final, ALU.mult, ALU.mult)\
                    .then_inc(out_ready, 1)



def t5_thresholds():
    n = np.arange(1, 4096)
    exact = BUCKETS // 2
    large = exact + (np.log(n.astype(np.float32) / np.float32(exact)) / np.float32(math.log(1024 / exact))
                     * np.float32(BUCKETS - exact)).astype(np.int32)
    bucket = np.where(n < exact, n, np.minimum(large, BUCKETS - 1))
    return np.array([0] + [n[bucket >= b][0] for b in range(1, BUCKETS)], np.float32)


def constants():
    i = np.arange(P)
    upto = (i[:, None] <= i[None, :]).astype(np.float32)
    one = np.ones((P, P), np.float32)
    c = np.zeros((P, KA[None]), np.float32)

    def put(name, a):
        c[:, KA[name]:KA[name] + CONSTS[name]] = a

    mask = np.where(i[None, :] <= i[:, None], 0.0, NEG)
    put("ident", np.eye(P))
    put("upto", np.concatenate([upto, one], 1))
    put("since", np.concatenate([one, upto.T], 1))
    put("after", (i[:, None] > i[None, :]))
    put("before", (i[:, None] < i[None, :]))
    put("ones", one)
    put("causal", np.concatenate([np.zeros((P, P)), mask, mask], 1))
    tok = np.arange(T)
    freqs = np.float32(10000.0) ** (-np.arange(16, dtype=np.float32) / np.float32(16))
    ang = np.concatenate([(tok // 64).astype(np.float32)[:, None] * freqs, (tok % 64).astype(np.float32)[:, None] * freqs], 1)
    grid = np.stack([np.cos(ang), np.sin(ang)], 1)
    put("grid", grid.reshape(2, P, 64).transpose(1, 0, 2).reshape(P, 128))
    put("inv_freq", np.float32(10000.0) ** (-np.arange(0, 64, 2, dtype=np.float32) / np.float32(64)))
    put("thresholds", t5_thresholds())
    select = np.zeros((16, 16, P), np.float32)
    select[np.arange(16), np.arange(16)] = 1.0
    return c, select.reshape(16, 16 * P)


def kernel(**inputs):
    import concourse.bacc as bacc
    from concourse.bass_utils import run_bass_kernel_spmd as run

    g = {k: np.asarray(a) for k, a in inputs.items()}

    def chunks(w, kts, width):
        k, n = w.shape
        w = w.reshape(k // (P * kts), kts, P, n // width, width)
        return np.ascontiguousarray(w.transpose(3, 0, 2, 1, 4).reshape(-1, P, kts * width))

    w2 = g["w_in_2"][0]
    up, nf = g["ffn_w_up_2"][0], FF2 // P
    glu_up = np.concatenate([chunks(up[:, :FF2], KD, P).reshape(nf, P, KD, P),
                             chunks(up[:, FF2:], KD, P).reshape(nf, P, KD, P)], 3).reshape(nf, P, SLOT)

    def mlp(layer):
        parts = (chunks(g["mlp_w_in"][layer], KD, 256), chunks(g["mlp_w_out"][layer], 2, D))
        return np.stack([parts[down][step] for down, step in alternate(FF // 256)])

    ada = g["ada_w_2"][0].reshape(2, 4, P, 12, 512).transpose(3, 0, 2, 1, 4).reshape(24, P, 2048)
    weights = {
        "mla_in": chunks(g["mla_w_in"][0], 4, 352), "mla_uq": chunks(g["mla_w_uq"][0], 3, 384),
        "mla_ukv": chunks(g["mla_w_ukv"][0], 2, 1024), "mla_o": chunks(g["mla_w_o"][0], 4, 512),
        "mlp0": mlp(0), "qkv": chunks(g["moba_w_qkv"][0], 4, 512), "moba_o": chunks(g["moba_w_o"][0], 4, 512),
        "mlp1": mlp(1), "ada": np.ascontiguousarray(ada), "dt": chunks(w2[:, 3072:], 8, 16),
        "xs": chunks(w2[:, 2048:2560], 8, 256), "bc": chunks(w2[:, 2560:3072], 8, 256),
        "q": chunks(w2[:, 0:512], 4, 512), "k": chunks(w2[:, 512:1024], 8, 256),
        "v": chunks(w2[:, 1024:1536], 4, 512), "z": chunks(w2[:, 1536:2048], 4, 512),
        "out": chunks(g["w_out_2"][0], 4, 512), "glu": glu_up, "glu_down": chunks(g["ffn_w_down_2"][0], 1, D),
    }

    def tiles(a):
        return a.reshape(-1, P).T

    ada_b = g["ada_b_2"][0].reshape(6, D)
    col = {
        "attn_norm": tiles(g["attn_norm"]), "mlp_norm": tiles(g["mlp_norm"]),
        "c_norm": np.concatenate([tiles(g["mla_q_a_norm"]), tiles(g["mla_kv_a_norm"])], 1),
        "q_nope": tiles(g["mla_q_nope_norm"]), "k_nope": tiles(g["mla_k_nope_norm"]),
        "moba_q": tiles(g["moba_q_norm"]), "moba_k": tiles(g["moba_k_norm"]),
        "norm1": tiles(g["norm1_w_2"]), "norm2": tiles(g["norm2_w_2"]),
        "ada_cols": tiles(ada_b[[0, 1, 3, 4]]),
        "conv_w": g["ssd_conv_w_2"][0].reshape(3, 8, P).transpose(2, 1, 0).reshape(P, 24),
        "conv_b": tiles(g["ssd_conv_b_2"]),
        "fconv_w": g["ffn_conv_w_2"][0].reshape(3, KF2, P).transpose(2, 1, 0).reshape(P, 3 * KF2),
        "fconv_b": tiles(g["ffn_conv_b_2"]), "ssd_norm": tiles(g["ssd_norm_w_2"]),
        "c": tiles(g["c_2"]), "c_ctx": tiles(g["c_ctx_2"]),
    }
    row = {
        "q_rope": g["mla_q_rope_norm"], "k_rope": g["mla_k_rope_norm"], "table": g["rel_bias_table"],
        "dt_bias": g["dt_bias_2"], "a_log": g["a_log_2"], "ssd_d": g["ssd_d_2"],
    }
    rpb = g["rpb_2"][0]
    wide = np.full((H, 15, 64 + 127), NEG, np.float32)
    wide[:, :, 48:79] = rpb
    col_start = np.clip(np.arange(64) - 8, 0, 48)
    per_w = np.full((64, H, 15, 64), NEG, np.float32)
    for w in range(64):
        a = col_start[w]
        per_w[w, :, :, a:a + 16] = wide[:, :, 63 - w + a:63 - w + a + 16]
    rpb_l = np.empty((2, 64, 2, H, 4, 64), np.float32)
    for r in range(4):
        rpb_l[r % 2, :, r // 2] = per_w[:, :, 7 - r:11 - r, :]

    consts, select = constants()
    rows_tiled = lambda a: np.ascontiguousarray(a.reshape(2, P, D).transpose(1, 0, 2))
    data = {
        "x": rows_tiled(g["x"][0]), "ctx": rows_tiled(g["ctx_2"][0]),
        "cols": np.ascontiguousarray(np.concatenate([col[k] for k in COLS], 1)),
        "rows": np.concatenate([row[k].reshape(-1) for k in ROWS])[None],
        "consts": consts, "select": select,
        "pos_col": np.ascontiguousarray(g["positions"].reshape(2, P).T), "pos_row": g["positions"].reshape(1, T),
        "rpb": np.ascontiguousarray(rpb_l.reshape(P, 4096)),
        "gates": np.ascontiguousarray(ada_b[[2, 5]].reshape(1, 2 * D)), "final": g["final_norm_w_2"].reshape(1, D),
    }
    nc = bacc.Bacc("TRN2", target_bir_lowering=False, num_devices=1)
    arrays = {}

    def dram(name, a):
        arrays[name] = a
        return nc.dram_tensor(name, a.shape, mybir.dt.from_np(a.dtype), kind="ExternalInput").ap()

    w_aps = {k: dram("w_" + k, a) for k, a in weights.items()}
    d = {k: dram("in_" + k, a) for k, a in data.items()}
    for k in ("rows", "pos_row", "gates", "final"):
        d[k] = bass.AP(d[k].tensor, 0, [[0, P], [1, data[k].shape[1]]])
    out = nc.dram_tensor("out", (P, 2, D), F32, kind="ExternalOutput").ap()
    program(nc, w_aps, d["x"], d["ctx"], d["cols"], d["rows"], d["consts"], d["select"], d["pos_col"], d["pos_row"],
            d["rpb"], d["gates"], d["final"], out)
    got = run(nc, [arrays], core_ids=[0]).results[0]["out"]
    return np.ascontiguousarray(got.reshape(P, 2, D).transpose(1, 0, 2).reshape(1, T, D))
```

```python
import math
from contextlib import ExitStack

import numpy as np

import concourse.bass as bass
from concourse import mybir

F32 = mybir.dt.float32
F32R = mybir.dt.float32r
I32 = mybir.dt.int32
ALU = mybir.AluOpType
ACT = mybir.ActivationFunctionType
AX = mybir.AxisListType

P = 128
T = 256
D = 1024
KD = D // P
EPS = 1e-6
H = 8
QR, KVR, NOPE, ROPE, VD = 384, 256, 128, 64, 128
FF = 4096
BUCKETS = 32
NA = 512
NST = 128
FF2 = 2816
KF2 = FF2 // P
NEG = -1e30
SLOT = 2048
MAGIC = 12582912.0

COLS = dict(attn_norm=16, mlp_norm=16, c_norm=5, q_nope=1, k_nope=1, moba_q=1, moba_k=1, norm1=8, norm2=8,
            ada_cols=32, conv_w=24, conv_b=8, fconv_w=3 * KF2, fconv_b=KF2, ssd_norm=4, c=8, c_ctx=8)
ROWS = dict(q_rope=ROPE, k_rope=ROPE, table=BUCKETS * H, dt_bias=16, a_log=16, ssd_d=8)
CONSTS = dict(ident=128, upto=256, since=256, after=128, before=128, ones=128, causal=384, grid=128, inv_freq=32,
              thresholds=32)


def starts(sizes):
    at, out = 0, {}
    for name, n in sizes.items():
        out[name] = at
        at += n
    out[None] = at
    return out


CA, RA, KA = starts(COLS), starts(ROWS), starts(CONSTS)

GEMMS = [("mla_in", 4, 4, 2), ("mla_uq", 4, 8, 1), ("mla_ukv", 2, 8, 1), ("mla_o", 4, 4, 2), ("mlp0", 32, 16, 1),
         ("qkv", 12, 12, 2), ("moba_o", 4, 4, 2), ("mlp1", 32, 16, 1),
         ("dt", 1, 1, 1), ("xs", 2, 4, 1), ("bc", 2, 4, 1), ("q", 2, 2, 2), ("k", 2, 6, 1), ("z", 2, 2, 2),
         ("v", 2, 4, 2), ("out", 4, 4, 2), ("glu", 22, 22, 1)]


def alternate(steps):
    seq = [(0, 0), (0, 1), (1, 0)]
    for s in range(1, steps):
        seq += [(0, s + 1)] if s + 1 < steps else []
        seq.append((1, s))
    return seq


SMALL = [("h0", 4), ("cT", 3), ("kpe", 1), ("qn", 4), ("kn", 4), ("qp", 2), ("att0", 24), ("m0", 4), ("d0", 4),
         ("h1", 4), ("q1", 4), ("k1", 4), ("att1", 24), ("m1", 4), ("d1", 4), ("hx", 4), ("dtrow", 1),
         ("cum", 1), ("cumcol", 1), ("later", 1), ("xsrow", 5), ("state", 2), ("cb", 2),
         ("nq", 2), ("nk", 2), ("na", 32), ("seg", 8), ("yoff", 4), ("yT", 2), ("m2", 4), ("d2", 4)]


def plan():
    small, at = {}, 0
    for name, n in SMALL:
        small[name] = at
        at += n
    chunk, unit, down = 0, 0, 0
    first_chunk, first_unit, released = {}, {}, []
    for name, n, units, group in GEMMS:
        first_chunk[name], first_unit[name] = chunk, unit
        if name in MLPS:
            for is_down, step in alternate(n // 2):
                if not is_down:
                    released.append(("gemm", unit + step + 1))
                elif step < n // 2 - 1:
                    down += 1
                    released.append(("down", down))
                else:
                    released.append(("small", small[MLPS[name]] + 4))
        else:
            per = units * group // n
            for j in range(n):
                if (j + 1) % group:
                    down += 1
                    released.append(("down", down))
                else:
                    released.append(("gemm", unit + per * (j // group + 1)))
        chunk += n
        unit += units
        if name == "mlp1":
            first_unit["ada"], first_unit["hc"] = unit, unit + 5
            unit += 9
        if name == "v":
            first_unit["na_o"], first_unit["y"] = unit, unit + 4
            unit += 6
    return first_chunk, first_unit, released, small


MLPS = {"mlp0": "d0", "mlp1": "d1"}
GC, GU, RELEASED, SU = plan()
ROOTS = [(0, 2), (2, 8), (8, 40), (40, 56), (0, 2), (0, 2), (8, 40), (0, 2), (0, 2), (0, 2), (0, 2), (0, 2), (0, 2)]


HI0 = dict(h0=0, cT=4, m0=7, h1=11, m1=15, hc=19, hx=23, yT=27, m2=29)
LO = dict(h0=4, m0=8, h1=28, m1=32, hc=52, hx=56, m2=60)
LO0 = dict(mlp0=8, mlp1=32, glu=60)
HID0 = dict(mlp0=0, mlp1=16, glu=32)


def causal_order():
    seq = [("S", 0), ("S", 1), ("S", 2)]
    for h in range(H):
        seq.append(("P", h))
        if h + 3 < H:
            seq.append(("S", h + 3))
        seq.append(("O", h))
    return seq, {x: n for n, x in enumerate(seq)}


def window_order():
    seq = [("S", 0), ("S", 1), ("S", 2)]
    for i in range(2 * H):
        seq.append(("P", i))
        if i + 3 < 2 * H:
            seq.append(("S", i + 3))
        if i % 2 == 0 and i:
            seq.append(("O", i // 2 - 1))
    seq.append(("O", H - 1))
    units, n = {}, 0
    for kind, i in seq:
        if kind != "O":
            units[(kind, i)] = n
            n += 1
    return seq, units


def spread(ap, at, n):
    dims = [list(x) for x in ap.ap]
    dims.insert(1 + at, [0, n])
    return bass.AP(ap.tensor, ap.offset, dims)


def program(nc, weights, x_in, ctx_in, cols_in, rows_in, consts_in, select_in, pos_col_in, pos_row_in, rpb_in, gates_dram,
            final_dram, out):
    with ExitStack() as stack:
        def sbuf(name, shape, dt=F32):
            return stack.enter_context(nc.sbuf_tensor(name, shape, dt))

        def sem(name):
            return stack.enter_context(nc.semaphore(name))

        raw = sbuf("raw", [P, 2, SLOT])
        split = sbuf("split", [P, 2, 2, SLOT], F32R)
        acts = sbuf("acts", [P, 2, 2, 2048], F32R)
        x = sbuf("x", [P, 2, D])
        work = sbuf("work", [P, 6144])
        bias = sbuf("bias", [P, 4096])
        gates = sbuf("gates", [P, 2, D])
        arena = sbuf("arena", [P, 14336])
        cols = sbuf("cols", [P, CA[None]])
        rows = sbuf("rows", [P, RA[None]])
        consts = sbuf("consts", [P, KA[None]])
        stat = sbuf("stat", [P, 384])
        half = sbuf("half", [P, 48])
        posc = sbuf("posc", [P, 2], I32)
        posr = sbuf("posr", [P, T], I32)
        posf = sbuf("posf", [P, 2])
        rot = sbuf("rot", [P, 2, 2, 32])
        adac = sbuf("adac", [P, 80])
        sc = sbuf("sc", [P, 2, 8])
        ps = [stack.enter_context(nc.psum_tensor(f"bank{i}", [P, 512], F32)) for i in range(8)]

        def col(name, a=0, n=None):
            n = COLS[name] - a if n is None else n
            return cols[:, CA[name] + a:CA[name] + a + n]

        def row(name, a=0, n=None):
            n = ROWS[name] - a if n is None else n
            return rows[:, RA[name] + a:RA[name] + a + n]

        def const(name, a=0, n=None):
            n = CONSTS[name] - a if n is None else n
            return consts[:, KA[name] + a:KA[name] + a + n]

        def view(buf, at, *shape):
            n = int(np.prod(shape))
            flat = buf[:, at:at + n]
            if len(shape) == 1:
                return flat
            names = "abcd"[:len(shape)]
            return flat.rearrange(f"p ({' '.join(names)}) -> p {' '.join(names)}", **dict(zip(names, shape)))

        att = work[:, 0:4096]
        xn = view(work, 4096, 2, D)
        part = view(arena, 4096, 16, 512)
        ident = const("ident")
        q0 = view(arena, 0, 2, H * 192)
        kv = view(arena, 3072, 2, H * 256)
        qnT = view(arena, 7168, H, T)
        knT = view(arena, 9216, H, T)
        qpT = view(arena, 11264, 4, T)
        kpT = view(arena, 12288, T)
        kpe2 = view(arena, 12544, 2, 128)
        proj = view(arena, 7168, 2, 704)
        dist, deltas = bias[:, 3072:3456], bias[:, 3840:4096]
        qkv = view(arena, 0, 2, 3 * D)
        q1T = view(arena, 6144, H, T)
        k1T = view(arena, 8192, H, T)
        relu_t = view(arena, 0, 2, 512)
        square_t = view(arena, 1024, 2, 512)
        ctx = view(work, 0, 2, D)
        nqk = view(arena, 0, 2, 2 * NA)
        nv = view(arena, 2048, 2, NA)
        ncv = view(arena, 3072, 2, NA)
        sz = view(arena, 4096, 2, NA)
        nqT = view(arena, 5120, 4, T)
        nkT = view(arena, 6144, 4, 2 * T)
        BT = view(arena, 8192, 2, 2 * T)
        CT = view(arena, 9216, 2, T)
        xsr = view(arena, 9728, 2, NA)
        cxsr = view(arena, 10752, 2, NA)
        Bcr = view(arena, 11776, 2, 2, P)
        cbm = view(arena, 12288, 2, 768)
        cum = arena[0:16, 13824:14336]
        tmp = lambda k: arena[:, 12288 + 64 * k:12352 + 64 * k]
        E = view(arena, 6144, 2, 768)
        Wm = view(arena, 2048, 2, 768)
        select = arena[0:16, 0:2048]
        xsT = view(work, 4096, 4, 2 * T)
        xw = view(work, 2048, 2, 2, NA)
        yrow = view(work, 4096, 2, NA)
        h0T = view(work, 5120, 2, NA)
        gact = view(arena, 1024, 2, T)
        prod_t = view(arena, 2048, 2, T)
        final = arena[:, 8192:8192 + D]
        raw_down = view(arena, 4096, 2, D)
        split_down = acts[:, 1, :, 1024:2048]

        def above(b):
            return bias[:, 3456:3840] if b % 2 else arena[:, 12032:12416]

        def t5_term(b, h):
            at = 8192 + 384 * (5 * (b % 2) + h - 3)
            return arena[:, at:at + 384]

        CTX0 = 5 * (BUCKETS - 1) + 1

        def ctx_term(n, kk):
            at = (12288 if n % 2 else 2048) + 512 * kk
            return arena[:, at:at + 512]

        def act_pair(which, k, a, n):
            return tuple(acts[:, which, p, k * T + a:k * T + a + n] for p in range(2))

        x_in_sb = sem("x_loaded")
        ctx_in_sb = sem("ctx_loaded")
        params_in, consts_in_sb = sem("params_loaded"), sem("consts_loaded")
        select_in_sb = sem("select_loaded")
        rpb_loaded = sem("rpb_loaded")
        w_loaded = [sem(f"w_loaded{i}") for i in range(2)]
        hi_ready, lo_ready = sem("w_hi_ready"), sem("w_lo_ready")
        gemm_ready, down_used = sem("gemm_ready"), sem("chunk_used")
        out_hi, hidden_hi, glu_taps = sem("head_out_hi_ready"), sem("hidden_hi_ready"), sem("glu_outer_taps")
        down_loaded = [sem(f"glu_down_loaded{i}") for i in range(2)]
        down_hi, down_lo, glu_used = sem("glu_down_hi"), sem("glu_down_lo"), sem("glu_down_used")
        act_hi, act_lo = sem("activation_hi_ready"), sem("activation_lo_ready")
        final_in, gates_in = sem("final_loaded"), sem("gates_loaded")
        t5_start, t5_above, t5_terms = sem("t5_started"), sem("t5_above"), sem("t5_terms")
        gemm_free = [sem(f"gemm_free{i}") for i in range(4)]
        small_ready = sem("small_ready")
        small_free = [sem(f"small_free{i}") for i in range(4)]
        dve_step, pool_step = sem("dve_step"), sem("pool_step")
        normed = sem("rows_normed")
        x_normed = [sem(f"x_normed{t}") for t in range(2)]
        x_added, x_sq = sem("gated_product_added"), sem("x_squares_summed")
        latents_normed, heads_normed = sem("latents_normed"), sem("heads_normed")
        sq_ready, sq_used = sem("squares_ready"), sem("squares_used")
        angles, rotations = sem("angles_ready"), sem("rotations_ready")
        max_ready, exp_done, probs_ready = sem("max_ready"), sem("exp_done"), sem("probs_ready")
        silu_c, squared = sem("silu_c"), sem("relu_squared")
        ada_in = [sem(f"ada_in{i}") for i in range(2)]
        ada_used, ctx_terms = sem("ada_used"), sem("ctx_terms")
        means_ready, roots_ready = sem("means_ready"), sem("roots_ready")
        conv_mid, conv_act = sem("conv_centre"), sem("conv_activated")
        sp_abs, sp_exp, sp_u, sp_ln = (sem("softplus_" + n) for n in ("abs", "exp", "one_plus", "ln"))
        a_exp, dA_ready, ecum_ready = sem("a_exp"), sem("dA_ready"), sem("exp_cum")
        xw_ready, seg_exp = sem("xw_ready"), sem("seg_exp")
        w_mat, y_used, nqk_ready = sem("mask_matrix_ready"), sem("mask_matrix_used"), sem("nqk_rotated")
        glu_mid, glu_act = sem("glu_centre"), sem("glu_activated")
        out_ready, stored = sem("out_ready"), sem("stored")

        def gbank(u):
            return ps[u % 4]

        def sbank(u):
            return ps[4 + u % 4]

        def gemm_out(eng, u, i=None):
            eng.wait_ge(gemm_ready, u + 1 if i is None else 4 * i + (u + 1))

        def gemm_gone(eng, u):
            eng.wait_ge(gemm_free[u % 4], u // 4 + 1)

        def small_out(eng, u):
            eng.wait_ge(small_ready, u + 1)

        def small_gone(eng, u):
            eng.wait_ge(small_free[u % 4], u // 4 + 1)

        class Steps:

            def __init__(self, eng, semaphore):
                self.eng, self.sem, self.n, self.turn = eng, semaphore, 0, 0

            def step(self, ins):
                ins.then_inc(self.sem, 1)
                self.n += 1

            def settle(self):
                self.eng.wait_ge(self.sem, self.n + self.turn)

            def enter(self, i, per, first=0):
                self.turn, self.per, self.before = per * i - per * first if first else per * i, per, self.n

            def leave(self, turns):
                assert self.n == self.before + self.per
                self.turn, self.n = 0, self.before + self.per * turns

        seq_c, unit_c = causal_order()
        seq_w, unit_w = window_order()

        def released(eng, c, i=None, per=0):
            kind, value = RELEASED[c]
            semaphore = {"gemm": gemm_ready, "down": down_used, "small": small_ready}[kind]
            eng.wait_ge(semaphore, value if i is None else per * i + value)

        def chunk_width(c):
            for name, n, _, _ in GEMMS:
                j = c - GC[name]
                if 0 <= j < n:
                    return weights[name].shape[2]

        CHUNKS = GC["glu"] + KF2

        def quarters_of(n):
            return att[:, 2048 + 512 * n:2560 + 512 * n].rearrange("p (a b) -> p a b", a=4)

        def tokens_of(which, part_, k, t):
            return acts[:, which, part_, :].rearrange("p (k n) -> p k n", n=T)[:, k:k + 4, t * P:(t + 1) * P]

        block = stack.enter_context(nc.Block())

        @block.sync
        def _(sp):
            sp.dma_start(x[:, :, :], x_in).then_inc(x_in_sb, 16)

            def load(name, j, i=None, pitch=0):
                c = GC[name] + j
                w, at = weights[name], j
                if c >= 2:
                    sp.wait_ge(lo_ready, c - 1 if i is None else pitch * i + (c - 1))
                src = w[at] if i is None else w[pitch * i + at]
                sp.dma_start(raw[:, c % 2, 0:w.shape[2]], src).then_inc(w_loaded[c % 2], 16)

            def load_all(name):
                for j in range(weights[name].shape[0]):
                    load(name, j)

            def load_loop(name, a, pitch, turns):
                with sp.Fori(0, turns) as i:
                    for j in range(pitch):
                        load(name, a + j, i, pitch)

            def load_mlp(name, turns, first=0):
                for j in range(first, 3):
                    load(name, j)
                load_loop(name, 3, 8, turns)
                for j in range(3 + 8 * turns, weights[name].shape[0]):
                    load(name, j)

            for name in ("mla_in", "mla_uq", "mla_ukv", "mla_o"):
                load_all(name)
            load_mlp("mlp0", 3)
            load_loop("qkv", 0, 4, 3)
            sp.dma_start(gates[:, :, :].rearrange("p a b -> p (a b)"), gates_dram).then_inc(gates_in, 16)
            load_all("moba_o")
            for j in range(3):
                load("mlp1", j)
            sp.wait_ge(gemm_ready, GU["mlp1"])
            sp.dma_start(ctx, ctx_in).then_inc(ctx_in_sb, 16)
            load_mlp("mlp1", 3, 3)
            sp.wait_ge(ada_used, 24)
            sp.dma_start(bias[:, :], rpb_in).then_inc(rpb_loaded, 16)
            for name in ("dt", "xs", "bc", "q", "k", "z", "v"):
                load_all(name)
            load("out", 0)
            load("out", 1)
            small_out(sp, SU["nk"] + 1)
            sp.dma_start(select, select_in).then_inc(select_in_sb, 16)
            load("out", 2)
            load("out", 3)
            load("glu", 0)
            load("glu", 1)
            sp.wait_ge(gemm_ready, GU["out"])
            sp.dma_start(final, final_dram).then_inc(final_in, 16)

            def load_down(step, i=None):
                if i is not None or step >= 2:
                    sp.wait_ge(down_lo, step - 1 if i is None else 4 * i + (step - 1))
                w = weights["glu_down"]
                sp.dma_start(raw_down[:, step % 2, :], w[step] if i is None else w[4 * i + step])\
                    .then_inc(down_loaded[step % 2], 16)

            sp.wait_ge(normed, 5)
            load_down(0)
            load("glu", 2)
            load_down(1)
            load("glu", 3)
            with sp.Fori(0, 4) as i:
                for step in range(2, 6):
                    load_down(step, i)
                    load("glu", step + 2, i, 4)
            load_down(18)
            load("glu", 20)
            load_down(19)
            load("glu", 21)
            load_down(20)
            load_down(21)
            for t in range(2):
                sp.wait_ge(out_ready, t + 1)
                sp.dma_start(out[:, t, :], xn[:, t, :]).then_inc(stored, 16)
            sp.wait_ge(stored, 32)

        @block.gpsimd
        def _(pool):
            pool.memset(half[:, :], -0.5).then_inc(pool_step, 1)
            pool.wait_ge(pool_step, 1)

            def roots(first, last):
                for n in range(first, last):
                    a, b = ROOTS[n]
                    pool.wait_ge(means_ready, n + 1)
                    pool.tensor_tensor(stat[:, a:b], stat[:, a:b], half[:, 0:b - a], ALU.pow).then_inc(roots_ready, 1)

            roots(0, 5)
            pool.wait_ge(t5_start, 1)
            def add_terms(b, i=None):
                pool.wait_ge(t5_terms, b if i is None else 2 * i + b)
                for h in range(3, H):
                    acc = bias[:, 384 * h:384 * (h + 1)]
                    pool.tensor_tensor(acc, acc, t5_term(b, h), ALU.add).then_inc(pool_step, 1)

            with pool.Fori(0, (BUCKETS - 4) // 2) as i:
                add_terms(1, i)
                pool.wait_ge(pool_step, 10 * i + 6)
                add_terms(2, i)
                pool.wait_ge(pool_step, 10 * i + 11)
            roots(5, 6)
            for b in range(BUCKETS - 3, BUCKETS):
                add_terms(b)
                pool.wait_ge(pool_step, 5 * b + 1)
            roots(6, 7)
            pool.wait_ge(small_ready, SU["att1"] + 24)
            for j in range(2):
                pool.dma_start(bias[:, 2048 * j:2048 * j + 2048], weights["ada"][j]).then_inc(ada_in[j], 16)
            roots(7, 9)
            for n in range(8):
                pool.wait_ge(ctx_terms, n + 1)
                pool.wait_ge(ada_used, n + 1)
                u = n % 2
                pool.dma_start(bias[:, 2048 * u:2048 * u + 2048], weights["ada"][n + 2]).then_inc(ada_in[u], 16)
                acc, t = part[:, 12 + n // 2, :], [ctx_term(n, kk) for kk in range(4)]
                sums = [(t[0], t[0], t[1]), (t[2], t[2], t[3])] + ([(t[0], t[0], t[2]), (acc, acc, t[0])] if n % 2
                                                                   else [(acc, t[0], t[2])])
                for m, (dst, a, b) in enumerate(sums):
                    if m > 1:
                        pool.wait_ge(pool_step, CTX0 + 7 * (n // 2) + 3 * (n % 2) + m)
                    pool.tensor_tensor(dst, a, b, ALU.add).then_inc(pool_step, 1)
            with pool.Fori(5, 12) as i:
                for u in range(2):
                    pool.wait_ge(ada_used, 2 * i + (u - 1))
                    pool.dma_start(bias[:, 2048 * u:2048 * u + 2048], weights["ada"][2 * i + u])\
                        .then_inc(ada_in[u], 16)
            roots(9, len(ROOTS))

        @block.tensor
        def _(pe):
            def small_start(u):
                if u >= 4:
                    pe.wait_ge(small_free[u % 4], u // 4)

            def gemm_start(u, i=None):
                if u >= 4:
                    pe.wait_ge(gemm_free[u % 4], u // 4 if i is None else i + u // 4)

            def weights_in(c, i=None, pitch=0):
                pe.wait_ge(lo_ready, c + 1 if i is None else pitch * i + (c + 1))

            def slot(c, kts, width):
                return tuple(split[:, c % 2, p, 0:kts * width].rearrange("p (k n) -> p k n", k=kts) for p in range(2))

            def product(out_, a, b, first, last):
                pe.matmul(out_, a[0], b[0], start=first, stop=False)
                pe.matmul(out_, a[0], b[1], start=False, stop=False)
                return pe.matmul(out_, a[1], b[0], start=False, stop=last)

            def flip(u, pieces, large=False):
                (gemm_start if large else small_start)(u)
                for at, src in pieces:
                    k, m = src.shape[0], src.shape[1]
                    ins = pe.transpose((gbank if large else sbank)(u)[0:m, at:at + k], src, ident[0:k, 0:k])
                ins.then_inc(gemm_ready if large else small_ready, 1)

            def rows_to_cols(name, norm=0):
                for t in range(2):
                    if norm:
                        pe.wait_ge(x_normed[t], norm)
                    else:
                        pe.wait_ge(normed, t + 1)
                    for half in range(2):
                        flip(SU[name] + 2 * t + half,
                             [(P * f, xn[:, t, (4 * half + f) * P:(4 * half + f + 1) * P]) for f in range(4)])

            def rows_units(c, u, kts, width, piece, lhs, group=1, i=None, pitch=0):
                pieces = range(0, width, piece)
                for g in range(group):
                    weights_in(c + g, i, pitch)
                    w = slot(c + g, kts, width)
                    for m, a in enumerate(pieces):
                        for t in range(len(lhs)):
                            n = u + len(lhs) * m + t
                            if g == 0:
                                gemm_start(n, i)
                            for k in range(kts):
                                ins = product(gbank(n)[:, 0:piece], lhs[t](kts * g + k),
                                              tuple(p[:, k, a:a + piece] for p in w),
                                              g == 0 and k == 0, g == group - 1 and k == kts - 1)
                            if g == group - 1:
                                ins.then_inc(gemm_ready, 1)
                    if g < group - 1:
                        ins.then_inc(down_used, 1)

            def rows_gemm(name, chunks, kts, width, piece, lhs, group=1):
                per = len(lhs) * (width // piece)
                for j in range(0, chunks, group):
                    rows_units(GC[name] + j, GU[name] + per * (j // group), kts, width, piece, lhs, group)

            def rows_of(which, kts=0):
                return [lambda k, t=t: act_pair(which, kts + k, t * P, P) for t in range(2)]

            def cols_unit(c, u, feats, which, i=None, pitch=0, start_=True):
                w = slot(c, KD, 256)
                gemm_start(u, i)
                for n, (f, wh) in enumerate(zip(feats, which)):
                    for k in range(KD):
                        ins = product(gbank(u)[:, n * T:(n + 1) * T], tuple(p[:, k, f * P:(f + 1) * P] for p in w),
                                      act_pair(wh, k, 0, T), k == 0, k == KD - 1)
                ins.then_inc(gemm_ready, 1)

            def mlp(name, steps, tiles, turns, after=None):
                c0, u0, d0 = GC[name], GU[name], SU[MLPS[name]]
                seq = alternate(steps)

                def up(n, s, i=None):
                    weights_in(c0 + n, i, 8)
                    cols_unit(c0 + n, u0 + s, (0, 1), (0, 0), i)

                def down(n, s, i=None):
                    weights_in(c0 + n, i, 8)
                    pe.wait_ge(act_lo, LO0[name] + s + 1 if i is None else 4 * i + (LO0[name] + s + 1))
                    w = slot(c0 + n, tiles, D)
                    for half_ in range(2):
                        for t in range(2):
                            for k in range(tiles):
                                kt = (s % 2) * 2 + k
                                ins = product(sbank(d0 + 2 * half_ + t)[:, :], act_pair(1, kt, t * P, P),
                                              tuple(p[:, k, 512 * half_:512 * half_ + 512] for p in w),
                                              i is None and s == 0 and k == 0,
                                              i is None and s == steps - 1 and k == tiles - 1)
                            if i is None and s == steps - 1:
                                ins.then_inc(small_ready, 1)
                    if i is not None or s < steps - 1:
                        ins.then_inc(down_used, 1)

                for n in range(3):
                    if n == 2:
                        for u in range(d0, d0 + 4):
                            small_start(u)
                    (down if seq[n][0] else up)(n, seq[n][1])
                with pe.Fori(0, turns) as i:
                    for n in range(3, 11):
                        (down if seq[n][0] else up)(n, seq[n][1], i)
                for n in range(3 + 8 * turns, len(seq)):
                    (down if seq[n][0] else up)(n, seq[n][1])
                    if after:
                        after(n)

            def causal_attention(name, scores, value, count):
                for kind, h in seq_c:
                    u = SU[name] + unit_c[(kind, h)]
                    if kind == "S":
                        small_start(u)
                        scores(u, h)
                    elif kind == "P":
                        pe.wait_ge(probs_ready, count + h + 1)
                        pr = att[:, 1024 + 512 * (h % 2):1024 + 512 * (h % 2) + 384]
                        flip(u, [(0, pr[:, 256:384]), (P, pr[:, 0:128]), (2 * P, pr[:, 128:256])])
                    else:
                        small_gone(pe, SU[name] + unit_c[("P", h)])
                        small_start(u)
                        pt = att[:, 2048 + 1024 * (h % 2):2048 + 1024 * (h % 2) + 384]
                        pe.matmul(sbank(u)[:, 0:T], value(0, h), pt[:, 0:T], start=True, stop=False)
                        pe.matmul(sbank(u)[:, P:T], value(1, h), pt[:, T:384], start=False, stop=True)\
                            .then_inc(small_ready, 1)

            pe.wait_ge(consts_in_sb, 16)
            rows_to_cols("h0")
            pe.wait_ge(act_lo, LO["h0"])
            rows_gemm("mla_in", 4, 4, 352, 352, rows_of(0), 2)
            pe.wait_ge(latents_normed, 1)
            for n, fs in enumerate(((0, 1), (2, 3), (4,))):
                flip(SU["cT"] + n, [(T * a + P * t, proj[:, t, f * P:(f + 1) * P])
                                    for a, f in enumerate(fs) for t in range(2)])
            for n in range(3):
                small_gone(pe, SU["cT"] + n)
            rows_gemm("mla_uq", 4, 3, 384, 384, rows_of(1))
            rows_gemm("mla_ukv", 2, 2, 1024, 512, rows_of(1, 3))
            pe.wait_ge(heads_normed, 1)
            flip(SU["kpe"], [(P * t, kpe2[:, t, :]) for t in range(2)])
            for n in range(4):
                flip(SU["qn"] + n, [(T * a + P * t, q0[:, t, (2 * n + a) * 192:(2 * n + a) * 192 + NOPE])
                                    for a in range(2) for t in range(2)])
            for n in range(4):
                flip(SU["kn"] + n, [(T * a + P * t, kv[:, t, (2 * n + a) * 256:(2 * n + a) * 256 + NOPE])
                                    for a in range(2) for t in range(2)])
            pe.wait_ge(heads_normed, 2)
            for n in range(2):
                flip(SU["qp"] + n, [(T * a + P * t, xn[:, t, (2 * n + a) * P:(2 * n + a + 1) * P])
                                    for a in range(2) for t in range(2)])
            for u in range(SU["kpe"], SU["qp"] + 2):
                small_gone(pe, u)

            def scores0(u, h):
                a = 64 * (h % 2)
                b = sbank(u)
                pe.matmul(b[:, 0:T], qnT[:, h, P:T], knT[:, h, :], start=True, stop=False)
                pe.matmul(b[:, 0:T], qpT[a:a + 64, h // 2, P:T], kpT[a:a + 64, :], start=False, stop=True)
                pe.matmul(b[:, T:384], qnT[:, h, 0:P], knT[:, h, 0:P], start=True, stop=False)
                pe.matmul(b[:, T:384], qpT[a:a + 64, h // 2, 0:P], kpT[a:a + 64, 0:P], start=False, stop=True)\
                    .then_inc(small_ready, 1)

            causal_attention("att0", scores0, lambda t, h: kv[:, t, h * 256 + NOPE:(h + 1) * 256], 0)
            for h in range(H):
                small_gone(pe, SU["att0"] + unit_c[("O", h)])
            rows_gemm("mla_o", 4, 4, 512, 512, rows_of(1), 2)
            rows_to_cols("m0", 1)
            pe.wait_ge(act_lo, LO["m0"])
            mlp("mlp0", 16, 2, 3)
            rows_to_cols("h1", 2)
            pe.wait_ge(act_lo, LO["h1"])
            with pe.Fori(0, 3) as i:
                for j in range(2):
                    rows_units(GC["qkv"] + 2 * j, GU["qkv"] + 2 * j, 4, 512, 512, rows_of(0), 2, i, 4)
            pe.wait_ge(heads_normed, 3)
            for n in range(8):
                flip(SU["q1"] + n, [(T * a + P * t, qkv[:, t, (2 * n + a) * P:(2 * n + a + 1) * P])
                                    for a in range(2) for t in range(2)])
            for u in range(SU["q1"], SU["q1"] + 8):
                small_gone(pe, u)

            def scores1(u, h):
                b = sbank(u)
                pe.matmul(b[:, 0:T], q1T[:, h, P:T], k1T[:, h, :], start=True, stop=True)
                pe.matmul(b[:, T:384], q1T[:, h, 0:P], k1T[:, h, 0:P], start=True, stop=True)\
                    .then_inc(small_ready, 1)

            causal_attention("att1", scores1, lambda t, h: qkv[:, t, 2 * D + h * P:2 * D + (h + 1) * P], H)
            for h in range(H):
                small_gone(pe, SU["att1"] + unit_c[("O", h)])
            rows_gemm("moba_o", 4, 4, 512, 512, rows_of(1), 2)
            rows_to_cols("m1", 3)
            pe.wait_ge(act_lo, LO["m1"])

            def ada_and_context(n):
                u = GU["ada"]
                if n == 29:
                    pe.wait_ge(ada_used, 24)
                    pe.wait_ge(pool_step, CTX0 + 28)
                    gemm_start(u)
                    m = 0
                    for chunk in (0, 1, 2, 3, 6, 7, 8, 9, 12, 13, 14, 15):
                        for f in range(4):
                            ins = pe.matmul(gbank(u)[:, m:m + 1], part[:, chunk, f * P:(f + 1) * P],
                                            const("ones", 0, 1), start=True, stop=True)
                            m += 1
                    ins.then_inc(gemm_ready, 1)
                for g, chunk in enumerate((4, 5, 10, 11)):
                    if n == (29 if g < 3 else 30):
                        gemm_start(u + 1 + g)
                        pe.matmul(gbank(u + 1 + g)[:, :], const("ones"), part[:, chunk, :], start=True, stop=True)\
                            .then_inc(gemm_ready, 1)
                if n == 30:
                    pe.wait_ge(normed, 4)
                    for t in range(2):
                        for half in range(2):
                            flip(GU["hc"] + 2 * t + half,
                                 [(P * f, ctx[:, t, (4 * half + f) * P:(4 * half + f + 1) * P]) for f in range(4)], True)

            mlp("mlp1", 16, 2, 3, ada_and_context)

            rows_to_cols("hx", 4)
            pe.wait_ge(act_lo, LO["hx"])

            both = rows_of(0) + rows_of(1)
            c, u = GC["dt"], GU["dt"]
            weights_in(c)
            gemm_start(u)
            w = slot(c, KD, 16)
            for n in range(2):
                for k in range(KD):
                    ins = product(gbank(u)[0:16, T * n:T * n + T], tuple(p[:, k, :] for p in w),
                                  act_pair(n, k, 0, T), k == 0, k == KD - 1)
            ins.then_inc(gemm_ready, 1)
            for j in range(2):
                weights_in(GC["xs"] + j)
                for f in range(2):
                    cols_unit(GC["xs"] + j, GU["xs"] + 2 * j + f, (f, f), (0, 1))
                if j == 0:
                    gemm_gone(pe, GU["dt"])
                    small_start(SU["dtrow"])
                    for n in range(4):
                        ins = pe.transpose(sbank(SU["dtrow"])[:, 16 * n:16 * n + 16], cum[:, P * n:P * n + P],
                                           ident[0:16, 0:16])
                    ins.then_inc(small_ready, 1)
            weights_in(GC["bc"])
            for f in range(2):
                cols_unit(GC["bc"], GU["bc"] + f, (f, f), (0, 1))
            weights_in(GC["bc"] + 1)
            for f in range(2):
                cols_unit(GC["bc"] + 1, GU["bc"] + 2 + f, (f,), (0,))
            rows_gemm("q", 2, 4, 512, 512, both[:2], 2)
            for j in range(2):
                c, u = GC["k"] + j, GU["k"] + 3 * j
                rows_units(c, u, KD, 256, 256, both[:2])
                cols_unit(c, u + 2, (0, 1), (1, 1))
            rows_gemm("z", 2, 4, 512, 512, both[:2], 2)
            rows_gemm("v", 2, 4, 512, 512, both, 2)

            pe.wait_ge(dA_ready, 1)
            dA = lambda t: stat[:, 160 + 16 * t:176 + 16 * t]
            u = SU["cum"]
            small_start(u)
            b = sbank(u)
            pe.matmul(b[0:16, 0:T], dA(0), const("upto"), start=True, stop=False)
            pe.matmul(b[0:16, P:T], dA(1), const("upto", 0, P), start=False, stop=True)
            pe.matmul(b[0:16, T:2 * T], dA(1), const("since"), start=True, stop=False)
            pe.matmul(b[0:16, T:T + P], dA(0), const("since", P, P), start=False, stop=True).then_inc(small_ready, 1)
            small_gone(pe, u)
            u = SU["cumcol"]
            small_start(u)
            for n in range(4):
                ins = pe.transpose(sbank(u)[:, 16 * n:16 * n + 16], cum[:, P * n:P * n + P], ident[0:16, 0:16])
            ins.then_inc(small_ready, 1)
            u = SU["later"]
            small_start(u)
            b = sbank(u)
            for n, (parts) in enumerate((
                    [("after", 0), ("ones", 1)], [("before", 0)], [("after", 1)], [("before", 1), ("ones", 0)])):
                for m, (tri, t) in enumerate(parts):
                    ins = pe.matmul(b[:, 16 * n:16 * n + 16], const(tri), dA(2 + t), start=m == 0,
                                    stop=m == len(parts) - 1)
            ins.then_inc(small_ready, 1)
            pe.wait_ge(conv_act, 8)
            for t in range(2):
                flip(SU["xsrow"] + t, [(P * f, xsT[:, f, t * P:(t + 1) * P]) for f in range(4)])
            for t in range(2):
                flip(SU["xsrow"] + 2 + t, [(P * f, xsT[:, f, T + t * P:T + (t + 1) * P]) for f in range(4)])
            flip(SU["xsrow"] + 4, [(P * (2 * t + g), BT[:, g, T + t * P:T + (t + 1) * P])
                                   for t in range(2) for g in range(2)])
            small_gone(pe, SU["xsrow"] + 4)
            pe.wait_ge(xw_ready, 4)
            for d in range(2):
                u = SU["state"] + d
                small_start(u)
                for g in range(2):
                    for t in range(2):
                        ins = pe.matmul(sbank(u)[:, g * 256:(g + 1) * 256], Bcr[:, t, g, :],
                                        xw[:, t, d, g * 256:(g + 1) * 256], start=t == 0, stop=t == 1)
                ins.then_inc(small_ready, 1)
            for g in range(2):
                u = SU["cb"] + g
                small_start(u)
                for t in range(2):
                    ins = pe.matmul(sbank(u)[:, t * T:(t + 1) * T], BT[:, g, t * P:(t + 1) * P], CT[:, g, :],
                                    start=True, stop=True)
                ins.then_inc(small_ready, 1)
            pe.wait_ge(nqk_ready, 1)
            for n in range(2):
                flip(SU["nq"] + n, [(T * a + P * t, nqk[:, t, (2 * n + a) * P:(2 * n + a + 1) * P])
                                    for a in range(2) for t in range(2)])
            for n in range(2):
                flip(SU["nk"] + n, [(T * a + P * t, nqk[:, t, NA + (2 * n + a) * P:NA + (2 * n + a + 1) * P])
                                    for a in range(2) for t in range(2)])
            for u in range(SU["nq"], SU["nq"] + 4):
                small_gone(pe, u)
            for u in (GU["k"] + 2, GU["k"] + 5):
                gemm_gone(pe, u)
            for u in range(GU["v"], GU["v"] + 4):
                gemm_gone(pe, u)
            for kind, i in seq_w:
                if kind == "S":
                    u = SU["na"] + unit_w[(kind, i)]
                    h, t = i // 2, i % 2
                    a = 64 * (h % 2)
                    small_start(u)
                    pe.matmul(sbank(u)[:, :], nqT[a:a + 64, h // 2, t * P:(t + 1) * P], nkT[a:a + 64, h // 2, :],
                              start=True, stop=True).then_inc(small_ready, 1)
                elif kind == "P":
                    pe.wait_ge(probs_ready, 2 * H + i + 1)
                    pr = att[:, 1024 + 512 * (i % 2):1536 + 512 * (i % 2)]
                    flip(SU["na"] + unit_w[(kind, i)], [(P * k, pr[:, P * k:P * k + P]) for k in range(4)])
                else:
                    u = GU["na_o"] + i // 2
                    a = 64 * (i % 2)
                    for t in range(2):
                        small_gone(pe, SU["na"] + unit_w[("P", 2 * i + t)])
                    if i % 2 == 0:
                        gemm_start(u)
                    pt = view(att, 2048 + 1024 * (i % 2), 4, T)
                    for k in range(4):
                        val = (nv if k < 2 else ncv)[:, k % 2, i * 64:(i + 1) * 64]
                        ins = pe.matmul(gbank(u)[a:a + 64, 0:T], val, pt[:, k, :], start=k == 0, stop=k == 3)
                    if i % 2:
                        ins.then_inc(gemm_ready, 1)
            pe.wait_ge(select_in_sb, 16)
            for u in range(2):
                small_gone(pe, SU["xsrow"] + u)

            def segment(h):
                u = SU["seg"] + h
                small_start(u)
                for d in range(2):
                    ins = pe.matmul(sbank(u)[:, d * T:(d + 1) * T], select[:, (8 * d + h) * P:(8 * d + h + 1) * P],
                                    cum[:, d * T:(d + 1) * T], start=True, stop=True)
                ins.then_inc(small_ready, 1)

            for h in range(4):
                segment(h)
            yu = GU["y"]
            for u in (yu, yu + 1):
                gemm_start(u)
            for h in range(H):
                pe.wait_ge(w_mat, h + 1)
                wm = Wm[:, h % 2, :]
                for t, parts in enumerate(([(0, 0), (384, 0), (512, 1)], [(128, 0), (256, 1), (640, 1)])):
                    for m, (at, tile) in enumerate(parts):
                        ins = pe.matmul(gbank(yu + t)[:, h * 64:(h + 1) * 64], wm[:, at:at + P],
                                        xsr[:, tile, h * 64:(h + 1) * 64], start=m == 0, stop=m == 2)
                    if h == H - 1:
                        ins.then_inc(gemm_ready, 1)
                if h < H - 1:
                    ins.then_inc(y_used, 1)
                if h + 4 < H:
                    segment(h + 4)
            for d in range(2):
                small_gone(pe, SU["state"] + d)
            for t in range(2):
                for d in range(2):
                    u = SU["yoff"] + 2 * t + d
                    small_start(u)
                    for g in range(2):
                        ins = pe.matmul(sbank(u)[:, g * 256:(g + 1) * 256], CT[:, g, t * P:(t + 1) * P],
                                        h0T[:, d, g * 256:(g + 1) * 256], start=True, stop=True)
                    ins.then_inc(small_ready, 1)
            pe.wait_ge(normed, 5)
            for n in range(2):
                flip(SU["yT"] + n, [(T * a + P * t, yrow[:, t, (2 * n + a) * P:(2 * n + a + 1) * P])
                                    for a in range(2) for t in range(2)])
            for p in range(4):
                gemm_gone(pe, GU["na_o"] + p)
            for n in range(2):
                small_gone(pe, SU["yT"] + n)
            rows_gemm("out", 4, 4, 512, 512, rows_of(1), 2)
            rows_to_cols("m2", 5)
            pe.wait_ge(act_lo, LO["m2"])
            d0 = SU["d2"]

            def up(s, i=None):
                weights_in(GC["glu"] + s, i, 4)
                cols_unit(GC["glu"] + s, GU["glu"] + s, (0, 1), (0, 0), i)

            def down(s, i=None):
                pe.wait_ge(act_lo, LO0["glu"] + s + 1 if i is None else 4 * i + (LO0["glu"] + s + 1))
                pe.wait_ge(down_lo, s + 1 if i is None else 4 * i + (s + 1))
                at = 2 * (s % 2)
                for half_ in range(2):
                    for t in range(2):
                        ins = product(sbank(d0 + 2 * half_ + t)[:, :], act_pair(1, at, t * P, P),
                                      tuple(split_down[:, p, 512 * half_:512 * half_ + 512] for p in range(2)),
                                      i is None and s == 0, i is None and s == KF2 - 1)
                        if i is None and s == KF2 - 1:
                            ins.then_inc(small_ready, 1)
                if i is not None or s < KF2 - 1:
                    ins.then_inc(glu_used, 1)

            up(0)
            up(1)
            for u in range(d0, d0 + 4):
                small_start(u)
            down(0)
            with pe.Fori(0, 5) as i:
                for s in range(1, 5):
                    up(s + 1, i)
                    down(s, i)
            down(KF2 - 1)

        @block.scalar
        def _(act):
            act.dma_start(consts[:, :], consts_in).then_inc(consts_in_sb, 16)
            for dst, src in ((cols[:, :], cols_in), (rows[:, :], rows_in),
                             (posc[:, :], pos_col_in), (posr[:, :], pos_row_in)):
                act.dma_start(dst, src).then_inc(params_in, 16)

            def copy(out_, in_, scale=None):
                if scale is None:
                    return act.activation(out_, in_, ACT.Copy)
                return act.activation(out_, in_, ACT.Copy, scale=scale)

            def split_hi(c, i=None, pitch=0):
                loads = 16 * (c // 2 + 1)
                act.wait_ge(w_loaded[c % 2], loads if i is None else 8 * pitch * i + loads)
                n = chunk_width(c)
                copy(split[:, c % 2, 0, 0:n], raw[:, c % 2, 0:n]).then_inc(hi_ready, 1)

            def used(c, i=None, pitch=0):
                per = {"gemm": 4, "down": pitch // 2}.get(RELEASED[c][0], 0)
                released(act, c, i, per)
                if c + 2 < CHUNKS:
                    split_hi(c + 2, i, pitch)

            def empty(u, dst, n=512, scale=None, a=0):
                gemm_out(act, u)
                src = gbank(u)[:, a:a + n]
                copy(dst, src, scale).then_inc(gemm_free[u % 4], 1)

            def small_empty(u, dst, n=512, scale=None):
                small_out(act, u)
                copy(dst, sbank(u)[:, 0:n], scale).then_inc(small_free[u % 4], 1)

            def pair(buf, n):
                return buf[:, 2 * n:2 * n + 2, 0:T]

            def halves(u, n=2, m=T):
                return sbank(u)[:, 0:n * m].rearrange("p (a b) -> p a b", a=n)

            def pair_empty(u, dst, scale=None):
                small_out(act, u)
                copy(dst, halves(u), scale).then_inc(small_free[u % 4], 1)

            def cols_hi(name, which=0):
                for n in range(4):
                    if which:
                        gemm_gone(act, GU[name] + n)
                    else:
                        small_gone(act, SU[name] + n)
                    copy(tokens_of(which, 0, 4 * (n % 2), n // 2), quarters_of(n)).then_inc(act_hi, 1)

            def x_squares(units, ns, small=False, gated=None):
                for n in ns:
                    if gated is None:
                        (small_gone if small else gemm_gone)(act, units + n)
                    else:
                        act.wait_ge(x_added, gated + n + 1)
                    t, a = n % 2, 512 * (n // 2)
                    act.activation(xn[:, t, a:a + 512], x[:, t, a:a + 512], ACT.Square,
                                   accum_out=stat[:, 72 + n:73 + n]).then_inc(x_sq, 1)

            def norm_second_tile(root):
                act.wait_ge(roots_ready, root)
                copy(xn[:, 1, :], x[:, 1, :], stat[:, 1:2]).then_inc(x_normed[1], 1)

            def project_to_x(name, gated=None):
                for j in range(4):
                    if j < 3:
                        used(GC[name] + j)
                    if j % 2:
                        x_squares(GU[name], (j - 1, j), gated=gated)

            def mlp(name, steps, turns, hidden, beside=None, peel=0):
                c0, seq = GC[name], alternate(steps)

                def chunk(n, i=None):
                    used(c0 + n, i, 8)
                    if not seq[n][0]:
                        hidden(seq[n][1], i)
                    if beside:
                        beside(n, i)

                for n in range(3 + 8 * peel):
                    chunk(n)
                with act.Fori(peel, turns) as i:
                    for n in range(3, 11):
                        chunk(n, i)
                for n in range(3 + 8 * turns, len(seq) - 1):
                    chunk(n)

            split_hi(0)
            split_hi(1)
            cols_hi("h0")
            act.wait_ge(params_in, 64)
            act.activation(sc[:, :, :], col("c", 0, 16).rearrange("p (a b) -> p a b", a=2), ACT.Silu)\
                .then_inc(silu_c, 1)
            act.wait_ge(angles, 1)
            act.activation(rot[:, :, :, :].rearrange("p a b c -> p (a b c)"), bias[:, 128:256], ACT.Sin)\
                .then_inc(rotations, 1)
            for n in range(4):
                if n < 3:
                    used(GC["mla_in"] + n)
                for t in range(2 * (n % 2)):
                    empty(GU["mla_in"] + n - 1 + t, proj[:, t, 352 * (n // 2):352 * (n // 2) + 352], 352)
            for n, fs in enumerate((2, 2, 1)):
                small_out(act, SU["cT"] + n)
                for f in range(fs):
                    k = 2 * n + f
                    ins = copy(acts[:, 1, 0, k * T:(k + 1) * T], sbank(SU["cT"] + n)[:, f * T:(f + 1) * T],
                               col("c_norm", k, 1))
                ins.then_inc(act_hi, 1)
            used(GC["mla_in"] + 3)
            n = 0
            for name, dst, each, per in (("mla_uq", q0, 192, 2), ("mla_ukv", kv, 256, 4)):
                for m in range(8):
                    u, t, p = GU[name] + m, m % 2, m // 2
                    if m % per == 0 and (name, m) != ("mla_ukv", 4):
                        used(GC[name] + m // per)
                    gemm_out(act, u)
                    if n >= 2:
                        act.wait_ge(sq_used, n - 1)
                    w = 192 if each == 192 else NOPE
                    src = gbank(u)[:, 0:2 * each].rearrange("p (a b) -> p a b", a=2)[:, :, 0:w]
                    sq = att[:, 512 * (n % 2):512 * (n % 2) + 2 * w].rearrange("p (a b) -> p a b", a=2)
                    act.activation(sq, src, ACT.Square).then_inc(sq_ready, 1)
                    copy(dst[:, t, 2 * each * p:2 * each * (p + 1)], gbank(u)[:, 0:2 * each])\
                        .then_inc(gemm_free[u % 4], 1)
                    n += 1
            small_empty(SU["kpe"], kpT, T)
            for n in range(4):
                pair_empty(SU["qn"] + n, pair(qnT, n), col("q_nope"))
            for n in range(4):
                pair_empty(SU["kn"] + n, pair(knT, n), col("k_nope"))
            for n in range(2):
                pair_empty(SU["qp"] + n, pair(qpT, n))
            used(GC["mla_ukv"] + 1)

            def causal_attention(name, count):
                def probabilities(h):
                    b = h % 2
                    act.wait_ge(max_ready, count + h + 1)
                    for tile, a, n in ((1, 0, 256), (0, 256, 128)):
                        ins = act.activation(att[:, 1024 + 512 * b + a:1024 + 512 * b + a + n],
                                             att[:, 512 * b + a:512 * b + a + n], ACT.Exp,
                                             bias=stat[:, 56 + 2 * b + tile:57 + 2 * b + tile],
                                             accum_out=stat[:, 60 + 2 * b + tile:61 + 2 * b + tile])
                    ins.then_inc(exp_done, 1)

                def transposed(h):
                    u = SU[name] + unit_c[("P", h)]
                    small_empty(u, att[:, 2048 + 1024 * (h % 2):2048 + 1024 * (h % 2) + 384], 384)

                def head_out(h):
                    u = SU[name] + unit_c[("O", h)]
                    small_out(act, u)
                    copy(acts[:, 1, 0, h * T:(h + 1) * T], sbank(u)[:, 0:T]).then_inc(out_hi, 1)

                for h in range(H + 2):
                    if h < H:
                        probabilities(h)
                    if h >= 2:
                        head_out(h - 2)
                    if 1 <= h <= H:
                        transposed(h - 1)

            causal_attention("att0", 0)

            def all_used(name, n):
                for j in range(n):
                    used(GC[name] + j)

            def t5_terms_of(n, i=None):
                b = n - 1
                if b < 1:
                    return
                k = 0 if i is None else i
                act.wait_ge(t5_above, 8 * k + b)
                if b >= 2:
                    act.wait_ge(pool_step, 40 * k + (5 * (b - 2) + 1))
                for h in range(3, H):
                    ins = copy(t5_term(b, h), above(b), deltas[:, bass.ds(8 * H * k + (H * b + h), 1)])
                ins.then_inc(t5_terms, 1)

            def square_relu(name, beside=None, peel=0):
                def hidden(s, i=None):
                    u = GU[name] + s
                    act.activation(relu_t[:, s % 2, :], gbank(u)[:, :], ACT.Relu).then_inc(gemm_free[u % 4], 1)
                    act.wait_ge(gemm_free[u % 4], u // 4 + 1 if i is None else i + (u // 4 + 1))
                    hi = acts[:, 1, 0, 512 * (s % 2):512 * (s % 2) + 512]
                    if name == "mlp0":
                        act.activation(hi, relu_t[:, s % 2, :], ACT.Square).then_inc(hidden_hi, 1)
                        return
                    act.activation(square_t[:, s % 2, :], relu_t[:, s % 2, :], ACT.Square).then_inc(squared, 1)
                    act.wait_ge(squared, s + 1 if i is None else 4 * i + (s + 1))
                    copy(hi, square_t[:, s % 2, :]).then_inc(hidden_hi, 1)

                mlp(name, 16, 3, hidden, beside, peel)

            project_to_x("mla_o")
            norm_second_tile(5)
            cols_hi("m0")
            used(GC["mla_o"] + 3)
            square_relu("mlp0", t5_terms_of)
            x_squares(SU["d0"], range(4), True)
            norm_second_tile(6)
            cols_hi("h1")
            used(GC["mlp0"] + 31)
            t5_terms_of(BUCKETS - 1)
            t5_terms_of(BUCKETS)
            c0, u0 = GC["qkv"], GU["qkv"]
            with act.Fori(0, 2) as i:
                for j in range(4):
                    used(c0 + j, i, 4)
                    for m in range(j - 1, j + 1) if j % 2 else ():
                        u = u0 + m
                        gemm_out(act, u, i)
                        act.wait_ge(sq_used, 4 * i + (15 + m))
                        act.activation(att[:, 512 * (m % 2):512 * (m % 2) + 512], gbank(u)[:, :], ACT.Square)\
                            .then_inc(sq_ready, 1)
                        copy(qkv[:, m % 2, bass.ds(i * 1024 + 512 * (m // 2), 512)], gbank(u)[:, :])\
                            .then_inc(gemm_free[u % 4], 1)
            for j in range(4):
                used(c0 + 8 + j)
                for m in range(j - 1, j + 1) if j % 2 else ():
                    empty(u0 + 8 + m, qkv[:, m % 2, 2048 + 512 * (m // 2):2560 + 512 * (m // 2)])
            for n in range(4):
                pair_empty(SU["q1"] + n, pair(q1T, n), col("moba_q"))
            for n in range(4):
                pair_empty(SU["k1"] + n, pair(k1T, n), col("moba_k"))
            causal_attention("att1", H)
            project_to_x("moba_o")
            norm_second_tile(8)
            cols_hi("m1")
            used(GC["moba_o"] + 3)
            act.wait_ge(silu_c, 1)

            def ctx_products(n, i=None):
                n -= 3
                if i is not None or not 0 <= n < 8:
                    return
                act.wait_ge(ada_in[n % 2], 16 * (n // 2 + 1))
                if n >= 2:
                    act.wait_ge(pool_step, CTX0 + 7 * (n // 2 - 1) + (7 if n % 2 else 3))
                for kk in range(4):
                    k = 4 * (n % 2) + kk
                    ins = copy(ctx_term(n, kk), bias[:, 2048 * (n % 2) + 512 * kk:2048 * (n % 2) + 512 * (kk + 1)],
                               sc[:, 1, k:k + 1])
                ins.then_inc(ctx_terms, 1)

            square_relu("mlp1", ctx_products, 1)

            x_squares(SU["d1"], range(4), True)
            cols_hi("hc", 1)
            norm_second_tile(10)
            cols_hi("hx")
            used(GC["mlp1"] + 31)
            conv_units = [(GU["xs"] + f, xsT[:, f, :], 512) for f in range(4)] \
                + [(GU["bc"] + g, BT[:, g, :], 512) for g in range(2)] \
                + [(GU["bc"] + 2 + g, CT[:, g, :], 256) for g in range(2)]
            def softplus():
                act.wait_ge(sp_abs, 1)
                act.activation(tmp(2), tmp(1), ACT.Exp, scale=-1.0).then_inc(sp_exp, 1)
                act.activation(stat[:, 80:96], row("a_log"), ACT.Exp).then_inc(a_exp, 1)
                act.wait_ge(sp_u, 1)
                act.activation(tmp(4), tmp(3), ACT.Ln).then_inc(sp_ln, 1)

            used(GC["dt"])
            for j in range(4):
                if j == 1:
                    softplus()
                used(GC["xs"] + j)
                for n in (2 * j, 2 * j + 1):
                    u, y, m = conv_units[n]
                    gemm_out(act, u)
                    act.activation(y, gbank(u)[:, 0:m], ACT.Identity, scale=col("conv_w", 3 * n + 1, 1),
                                   bias=col("conv_b", n, 1)).then_inc(conv_mid, 1)
                for n in (2 * j, 2 * j + 1):
                    u, y, m = conv_units[n]
                    gemm_gone(act, u)
                    act.activation(y, y, ACT.Silu).then_inc(conv_act, 1)
            all_used("q", 2)
            for j in range(2):
                used(GC["k"] + j)
                u = GU["k"] + 3 * j + 2
                gemm_out(act, u)
                copy(nkT[:, 2 * j:2 * j + 2, T:2 * T], gbank(u)[:, :].rearrange("p (a b) -> p a b", a=2))\
                    .then_inc(gemm_free[u % 4], 1)
            all_used("z", 2)
            for t in range(2):
                u = GU["z"] + t
                gemm_out(act, u)
                act.activation(sz[:, t, :], gbank(u)[:, :], ACT.Silu).then_inc(gemm_free[u % 4], 1)
            all_used("v", 2)
            for m in range(4):
                empty(GU["v"] + m, (nv if m < 2 else ncv)[:, m % 2, :])
            small_gone(act, SU["cumcol"])
            act.activation(stat[:, 320:384], stat[:, 256:320], ACT.Exp).then_inc(ecum_ready, 1)
            u = SU["later"]
            small_out(act, u)
            act.activation(tmp(7), sbank(u)[:, 0:64], ACT.Exp).then_inc(small_free[u % 4], 1)
            for n in range(5):
                dst = (xsr[:, 0], xsr[:, 1], cxsr[:, 0], cxsr[:, 1], Bcr[:, :, :, :].rearrange("p a b c -> p (a b c)"))[n]
                small_empty(SU["xsrow"] + n, dst)
            for d in range(2):
                small_empty(SU["state"] + d, h0T[:, d, :])
            for n in range(2):
                pair_empty(SU["nq"] + n, pair(nqT, n), 0.125)
            for n in range(2):
                pair_empty(SU["nk"] + n, pair(nkT, n))

            def pair_out(p):
                gemm_out(act, GU["na_o"] + p)
                copy(acts[:, 1, 0, p * T:(p + 1) * T], gbank(GU["na_o"] + p)[:, 0:T]).then_inc(out_hi, 1)

            for i in range(2 * H + 1):
                if i < 2 * H:
                    u = SU["na"] + unit_w[("S", i)]
                    act.wait_ge(max_ready, 2 * H + i + 1)
                    act.activation(att[:, 1024 + 512 * (i % 2):1536 + 512 * (i % 2)], sbank(u)[:, :], ACT.Exp,
                                   bias=stat[:, 56 + i % 2:57 + i % 2], accum_out=stat[:, 60 + i % 2:61 + i % 2])\
                        .then_inc(small_free[u % 4], 1)
                if i:
                    h, t = (i - 1) // 2, (i - 1) % 2
                    u = SU["na"] + unit_w[("P", i - 1)]
                    small_out(act, u)
                    copy(view(att, 2048 + 1024 * (h % 2), 4, T)[:, :, t * P:(t + 1) * P], halves(u, 4, P))\
                        .then_inc(small_free[u % 4], 1)
                if i >= 8 and i % 4 == 0:
                    pair_out(i // 4 - 2)
            pair_out(3)
            for h in range(H):
                small_gone(act, SU["seg"] + h)
                act.activation(E[:, h % 2, :], E[:, h % 2, :], ACT.Exp).then_inc(seg_exp, 1)
            for n in range(2):
                u = SU["yT"] + n
                small_out(act, u)
                for a in range(2):
                    k = 4 + 2 * n + a
                    ins = copy(acts[:, 1, 0, k * T:(k + 1) * T], sbank(u)[:, T * a:T * (a + 1)],
                               col("ssd_norm", 2 * n + a, 1))
                ins.then_inc(act_hi, 1)
            project_to_x("out", 0)
            norm_second_tile(12)
            cols_hi("m2")
            used(GC["out"] + 3)

            def glu(s, i=None):
                u, b, k = GU["glu"] + s, s % 2, 0 if i is None else i
                w = cols[:, bass.ds(12 * k + (CA["fconv_w"] + 3 * s + 1), 1)]
                bb = cols[:, bass.ds(4 * k + (CA["fconv_b"] + s), 1)]
                released(act, GC["glu"] + s, i, 4)
                act.activation(gact[:, b, :], gbank(u)[:, 0:T], ACT.Identity, scale=w, bias=bb).then_inc(glu_mid, 1)
                if s + 2 < KF2:
                    split_hi(GC["glu"] + s + 2, i, 4)
                act.wait_ge(glu_taps, 4 * k + (s + 1))
                act.activation(gact[:, b, :], gact[:, b, :], ACT.Silu).then_inc(glu_act, 1)
                act.wait_ge(gemm_free[u % 4], u // 4 + 1 + k)
                copy(acts[:, 1, 0, 512 * b:512 * b + T], prod_t[:, b, :]).then_inc(hidden_hi, 1)
                act.wait_ge(down_loaded[b], 32 * k + 16 * (s // 2 + 1))
                if s:
                    act.wait_ge(glu_used, 4 * k + s)
                copy(split_down[:, 0, :], raw_down[:, b, :]).then_inc(down_hi, 1)

            glu(0)
            with act.Fori(0, 4) as i:
                for s in range(1, 5):
                    glu(s, i)
            for s in range(17, KF2):
                glu(s)
            x_squares(SU["d2"], range(4), gated=4)

        @block.vector
        def _(v):
            st = Steps(v, dve_step)
            step, settle = st.step, st.settle
            roots = []

            def inverse_rms(at, widths):
                a = at
                for n, width in widths:
                    ins = v.tensor_scalar(stat[:, a:a + n], stat[:, a:a + n], 1.0 / width, EPS, ALU.mult, ALU.add)
                    a += n
                    if (n, width) != widths[-1] or a - at != sum(w[0] for w in widths):
                        step(ins)
                ins.then_inc(means_ready, 1)
                roots.append((at, a))
                assert roots[-1] == ROOTS[len(roots) - 1]
                v.wait_ge(roots_ready, len(roots))

            def sum_squares(src, junk, at):
                step(v.tensor_tensor_reduce(out=junk, in0=src, in1=src, scale=1.0, scalar=0.0, op0=ALU.mult,
                                            op1=ALU.add, accum_out=stat[:, at:at + 1]))

            def norm_rows(src, dst, junk):
                for t in range(2):
                    sum_squares(src[:, t, :], junk[:, t, :], t)
                settle()
                inverse_rms(0, [(2, D)])
                for t in range(2):
                    v.tensor_scalar(dst[:, t, :], src[:, t, :], stat[:, t:t + 1], None, ALU.mult).then_inc(normed, 1)

            def sum_squares_of_x(norm):
                v.wait_ge(x_sq, 4 * norm)
                step(v.tensor_tensor(stat[:, 0:2], stat[:, 72:74], stat[:, 74:76], ALU.add))
                settle()
                inverse_rms(0, [(2, D)])

            def norm_x(norm):
                sum_squares_of_x(norm)
                v.tensor_scalar(xn[:, 0, :], x[:, 0, :], stat[:, 0:1], None, ALU.mult).then_inc(x_normed[0], 1)

            def split_lo(c, i=None, pitch=0):
                v.wait_ge(hi_ready, c + 1 if i is None else pitch * i + (c + 1))
                n = chunk_width(c)
                v.tensor_tensor(split[:, c % 2, 1, 0:n], raw[:, c % 2, 0:n], split[:, c % 2, 0, 0:n].bitcast(F32),
                                ALU.subtract).then_inc(lo_ready, 1)

            def used(c, i=None, pitch=0):
                if c + 2 < CHUNKS:
                    split_lo(c + 2, i, pitch)

            def all_used(name, n):
                for j in range(n):
                    used(GC[name] + j)

            def cols_scale(name, n, gain, shift=None, large=False):
                u, k = (GU if large else SU)[name] + n, 4 * (n % 2)
                free = (gemm_free if large else small_free)[u % 4]
                dst = quarters_of(n)
                (gemm_out if large else small_out)(v, u)
                src = (gbank if large else sbank)(u)[:, :].rearrange("p (a b) -> p a b", a=4)
                g = spread(gain[:, k:k + 4], 1, P)
                if shift is None:
                    v.tensor_tensor(dst, src, g, ALU.mult).then_inc(free, 1)
                else:
                    step(v.tensor_tensor(dst, src, g, ALU.mult))
                    settle()
                    v.tensor_tensor(dst, dst, spread(shift[:, k:k + 4], 1, P), ALU.add).then_inc(free, 1)

            def cols_lo(name, n, which=0):
                k, t = 4 * (n % 2), n // 2
                v.wait_ge(act_hi, HI0[name] + n + 1)
                v.tensor_tensor(tokens_of(which, 1, k, t), quarters_of(n), tokens_of(which, 0, k, t).bitcast(F32),
                                ALU.subtract).then_inc(act_lo, 1)
                if n == 3:
                    v.wait_ge(act_lo, LO[name])

            def cols_out(name, gain, shift=None):
                for n in range(5):
                    if n < 4:
                        cols_scale(name, n, gain, shift)
                    if n:
                        cols_lo(name, n - 1)

            def scaled_lo(name, n, k0, tiles, gain, hi):
                u = SU[name] + n
                v.wait_ge(act_hi, hi)
                for a in range(tiles):
                    at = (k0 + a) * T
                    ins = v.scalar_tensor_tensor(acts[:, 1, 1, at:at + T], sbank(u)[:, a * T:(a + 1) * T],
                                                 gain[:, a:a + 1], acts[:, 1, 0, at:at + T].bitcast(F32),
                                                 ALU.mult, ALU.subtract)
                    if a < tiles - 1:
                        step(ins)
                ins.then_inc(small_free[u % 4], 1)

            def add_units(units, ns, small=False, gate=None):
                free, bank = (small_free, sbank) if small else (gemm_free, gbank)
                for n in ns:
                    u, half, t = units + n, n // 2, n % 2
                    dst = x[:, t, 512 * half:512 * (half + 1)]
                    (small_out if small else gemm_out)(v, u)
                    if gate is None:
                        v.tensor_tensor(dst, bank(u)[:, :], dst, ALU.add).then_inc(free[u % 4], 1)
                    else:
                        tm = att[:, 512 * n:512 * (n + 1)]
                        v.tensor_tensor(tm, bank(u)[:, :], gates[:, gate, 512 * half:512 * (half + 1)], ALU.mult)\
                            .then_inc(free[u % 4], 1)
                for n in ns:
                    (small_gone if small else gemm_gone)(v, units + n)
                if gate is not None:
                    for n in ns:
                        half, t = n // 2, n % 2
                        dst = x[:, t, 512 * half:512 * (half + 1)]
                        v.tensor_tensor(dst, dst, att[:, 512 * n:512 * (n + 1)], ALU.add).then_inc(x_added, 1)
                    v.wait_ge(x_added, 4 * gate + max(ns) + 1)

            def project_to_x(name, gate=None):
                for j in range(4):
                    if j < 3:
                        used(GC[name] + j)
                    if j % 2:
                        add_units(GU[name], (j - 1, j), gate=gate)

            def mlp(name, steps, turns, per, hidden, beside=None, peel=0, after=None):
                c0, seq = GC[name], alternate(steps)

                def chunk(n, i=None):
                    used(c0 + n, i, 8)
                    if not seq[n][0]:
                        hidden(seq[n][1], i)
                    if beside:
                        beside(n, i)

                for n in range(3 + 8 * peel):
                    chunk(n)
                with v.Fori(peel, turns) as i:
                    st.enter(i, per, peel)
                    for n in range(3, 11):
                        chunk(n, i)
                st.leave(turns - peel)
                for n in range(3 + 8 * turns, len(seq) - 1):
                    chunk(n)
                    if after:
                        after(n)

            v.wait_ge(x_in_sb, 16)
            norm_rows(x, xn, xn)
            v.wait_ge(params_in, 64)
            v.wait_ge(consts_in_sb, 16)
            split_lo(0)
            cols_out("h0", col("attn_norm", 0, 8))
            split_lo(1)
            ang, turns, cosines, sines = (bias[:, a:a + 64] for a in (0, 64, 128, 192))
            step(v.tensor_copy(posf[:, :], posc[:, :]))
            settle()
            for t in range(2):
                step(v.tensor_scalar(ang[:, 32 * t:32 * t + 32], const("inv_freq"), posf[:, t:t + 1], None, ALU.mult))
            settle()
            step(v.tensor_scalar(turns, ang, 1.0 / (2 * math.pi), MAGIC, ALU.mult, ALU.add))
            settle()
            step(v.tensor_scalar(turns, turns, MAGIC, None, ALU.subtract))
            settle()
            rest = 2 * math.pi
            for bits in (3, 14, 34):
                part_ = math.floor(rest * 2 ** (bits + 2)) / 2 ** (bits + 2) if bits < 34 else rest
                rest -= part_
                step(v.scalar_tensor_tensor(ang, turns, -part_, ang, ALU.mult, ALU.add))
                settle()
            pi32 = 3.1415925
            step(v.tensor_scalar(sines, ang, pi32, -pi32, ALU.min, ALU.max))
            settle()
            step(v.scalar_tensor_tensor(cosines, sines, -1.0, sines, ALU.mult, ALU.min))
            settle()
            v.tensor_scalar(cosines, cosines, math.pi / 2, None, ALU.add).then_inc(angles, 1)
            all_used("mla_in", 3)
            for u in range(4):
                gemm_gone(v, GU["mla_in"] + u)
            widths = ((0, QR), (QR, KVR), (QR + KVR, ROPE))
            for s_, (a, n) in enumerate(widths):
                for t in range(2):
                    sum_squares(proj[:, t, a:a + n], xn[:, t, a:a + n], 2 + 2 * s_ + t)
            settle()
            inverse_rms(2, [(2, n) for _, n in widths])
            for s_, (a, n) in enumerate(widths[:2]):
                for t in range(2):
                    ins = v.tensor_scalar(proj[:, t, a:a + n], proj[:, t, a:a + n],
                                          stat[:, 2 + 2 * s_ + t:3 + 2 * s_ + t], None, ALU.mult)
                    if (s_, t) == (1, 1):
                        ins.then_inc(latents_normed, 1)
                    else:
                        step(ins)
            kp = [proj[:, t, QR + KVR:QR + KVR + ROPE] for t in range(2)]
            for t in range(2):
                step(v.scalar_tensor_tensor(kp[t], kp[t], stat[:, 6 + t:7 + t], row("k_rope"), ALU.mult, ALU.mult))
            settle()
            v.wait_ge(rotations, 1)
            kpv = proj[:, :, QR + KVR:QR + KVR + ROPE]
            kt = [view(att, 2048 + 64 * k, 2, 32) for k in range(4)]
            for k, (a, r) in enumerate(((0, 0), (1, 1), (1, 0), (0, 1))):
                step(v.tensor_tensor(kt[k], kpv[:, :, 32 * a:32 * a + 32], rot[:, r, :, :], ALU.mult))
            settle()
            step(v.tensor_tensor(kpe2[:, :, 0:32], kt[0], kt[1], ALU.subtract))
            step(v.tensor_tensor(kpe2[:, :, 32:64], kt[2], kt[3], ALU.add))
            settle()
            step(v.tensor_copy(kpe2[:, :, 64:128], kpe2[:, :, 0:64]))
            for n, fs in enumerate((2, 2, 1)):
                scaled_lo("cT", n, 2 * n, fs, col("c_norm", 2 * n, fs), HI0["cT"] + n + 1)
            used(GC["mla_in"] + 3)
            qh = q0[:, :, :].rearrange("p t (h d) -> p (t h) d", d=192)
            kh = kv[:, :, :].rearrange("p t (h d) -> p (t h) d", d=256)
            for n in range(16):
                t, p = n % 2, n % 8 // 2
                if n < 8 and n % 2 == 0:
                    used(GC["mla_uq"] + n // 2)
                elif n == 8:
                    used(GC["mla_ukv"])
                elif n == 12:
                    v.wait_ge(sq_used, 12)
                    settle()
                    inverse_rms(8, [(16, NOPE), (16, ROPE)])
                    for u in range(8):
                        gemm_gone(v, GU["mla_uq"] + u)
                    step(v.tensor_tensor(qh[:, :, 0:NOPE], qh[:, :, 0:NOPE], spread(stat[:, 8:24], 1, NOPE), ALU.mult))
                v.wait_ge(sq_ready, n + 1)
                w = 192 if n < 8 else NOPE
                sq = att[:, 512 * (n % 2):512 * (n % 2) + 2 * w].rearrange("p (a b) -> p a b", a=2)
                at = (8 if n < 8 else 40) + 8 * t + 2 * p
                if n < 8:
                    step(v.tensor_reduce(stat[:, at + 16:at + 18], sq[:, :, NOPE:192], AX.X, ALU.add))
                v.tensor_reduce(stat[:, at:at + 2], sq[:, :, 0:NOPE], AX.X, ALU.add).then_inc(sq_used, 1)
            v.wait_ge(sq_used, 16)
            settle()
            inverse_rms(40, [(16, NOPE)])
            for u in range(8):
                gemm_gone(v, GU["mla_ukv"] + u)
            v.tensor_tensor(kh[:, :, 0:NOPE], kh[:, :, 0:NOPE], spread(stat[:, 40:56], 1, NOPE), ALU.mult)\
                .then_inc(heads_normed, 1)
            qp = qh[:, :, NOPE:192]
            step(v.tensor_tensor(qp, qp, spread(stat[:, 24:40], 1, ROPE), ALU.mult))
            settle()
            step(v.tensor_tensor(qp, qp, spread(row("q_rope"), 0, 16), ALU.mult))
            settle()
            qr = q0[:, :, :].rearrange("p t (h d) -> p t h d", d=192)
            xr = xn[:, :, 0:512].rearrange("p t (h d) -> p t h d", d=64)
            tm = [view(att, 2048 + 512 * k, 2, 8, 32) for k in range(4)]
            for k, (a, r) in enumerate(((0, 0), (1, 1), (1, 0), (0, 1))):
                for t in range(2):
                    step(v.tensor_tensor(tm[k][:, t], qr[:, t, :, NOPE + 32 * a:NOPE + 32 * a + 32],
                                         spread(rot[:, r, t, :], 0, 8), ALU.mult))
            settle()
            for t in range(2):
                step(v.tensor_tensor(xr[:, t, :, 0:32], tm[0][:, t], tm[1][:, t], ALU.subtract))
                ins = v.tensor_tensor(xr[:, t, :, 32:64], tm[2][:, t], tm[3][:, t], ALU.add)
                if t:
                    ins.then_inc(heads_normed, 1)
                else:
                    step(ins)

            used(GC["mla_ukv"] + 1)

            def causal_attention(name, scale, bias_of, count):
                def logits(h):
                    b = h % 2
                    u = SU[name] + unit_c[("S", h)]
                    small_out(v, u)
                    lg = att[:, 512 * b:512 * b + 384]
                    v.scalar_tensor_tensor(lg, sbank(u)[:, 0:384], scale, bias_of(h), ALU.mult, ALU.add)\
                        .then_inc(small_free[u % 4], 1)
                    small_gone(v, u)
                    step(v.tensor_reduce(stat[:, 57 + 2 * b:58 + 2 * b], lg[:, 0:256], AX.X, ALU.max, negate=True))
                    v.tensor_reduce(stat[:, 56 + 2 * b:57 + 2 * b], lg[:, 256:384], AX.X, ALU.max, negate=True)\
                        .then_inc(max_ready, 1)

                def normalise(h):
                    b = h % 2
                    v.wait_ge(exp_done, count + h + 1)
                    step(v.reciprocal(stat[:, 64 + 2 * b:66 + 2 * b], stat[:, 60 + 2 * b:62 + 2 * b]))
                    settle()
                    pr = att[:, 1024 + 512 * b:1024 + 512 * b + 384]
                    step(v.tensor_scalar(pr[:, 0:256], pr[:, 0:256], stat[:, 65 + 2 * b:66 + 2 * b], None, ALU.mult))
                    v.tensor_scalar(pr[:, 256:384], pr[:, 256:384], stat[:, 64 + 2 * b:65 + 2 * b], None, ALU.mult)\
                        .then_inc(probs_ready, 1)

                def head_lo(h):
                    u = SU[name] + unit_c[("O", h)]
                    v.wait_ge(out_hi, count + h + 1)
                    v.tensor_tensor(acts[:, 1, 1, h * T:(h + 1) * T], sbank(u)[:, 0:T],
                                    acts[:, 1, 0, h * T:(h + 1) * T].bitcast(F32), ALU.subtract)\
                        .then_inc(small_free[u % 4], 1)

                for h in range(H + 3):
                    if h < H:
                        logits(h)
                    if h >= 3:
                        head_lo(h - 3)
                    if 1 <= h <= H:
                        normalise(h - 1)

            causal_attention("att0", 1.0 / math.sqrt(NOPE + ROPE), lambda h: const("causal"), 0)
            project_to_x("mla_o")
            norm_x(1)
            cols_out("m0", col("mlp_norm", 0, 8))
            used(GC["mla_o"] + 3)

            def square_relu(name):
                def hidden(s, i=None):
                    u, b = GU[name] + s, s % 2
                    if name == "mlp0":
                        v.wait_ge(gemm_free[u % 4], u // 4 + 1 if i is None else i + (u // 4 + 1))
                        step(v.tensor_tensor(square_t[:, b, :], relu_t[:, b, :], relu_t[:, b, :], ALU.mult))
                        settle()
                    v.wait_ge(hidden_hi, HID0[name] + s + 1 if i is None else 4 * i + (HID0[name] + s + 1))
                    v.tensor_tensor(acts[:, 1, 1, 512 * b:512 * b + 512], square_t[:, b, :],
                                    acts[:, 1, 0, 512 * b:512 * b + 512].bitcast(F32), ALU.subtract)\
                        .then_inc(act_lo, 1)
                return hidden

            table = row("table")
            step(v.tensor_scalar(dist[:, 0:256], posr[:, :], -1.0, posf[:, 1:2], ALU.mult, ALU.add))
            step(v.tensor_scalar(dist[:, 256:384], posr[:, 0:P], -1.0, posf[:, 0:1], ALU.mult, ALU.add))
            step(v.tensor_tensor(deltas[:, H:], table[:, H:], table[:, 0:-H], ALU.subtract))
            for h in range(H):
                ins = v.tensor_scalar(bias[:, 384 * h:384 * h + 384], const("causal"), table[:, h:h + 1], None, ALU.add)
                if h < H - 1:
                    step(ins)
            ins.then_inc(t5_start, 1)
            v.wait_ge(t5_start, 1)

            def bucket_step(b, i=None):
                if b == 0:
                    return
                k = 0 if i is None else i
                settle()
                if b > 2:
                    v.wait_ge(t5_terms, 8 * k + (b - 2))
                v.tensor_scalar(above(b), dist, const("thresholds")[:, bass.ds(8 * k + b, 1)], None, ALU.is_ge)\
                    .then_inc(t5_above, 1)
                v.wait_ge(t5_above, 8 * k + b)
                for h in range(3):
                    acc = bias[:, 384 * h:384 * h + 384]
                    step(v.scalar_tensor_tensor(acc, above(b), deltas[:, bass.ds(8 * H * k + (H * b + h), 1)], acc,
                                                ALU.mult, ALU.add))

            mlp("mlp0", 16, 3, 28, square_relu("mlp0"), bucket_step)
            add_units(SU["d0"], range(4), small=True)
            norm_x(2)
            cols_out("h1", col("attn_norm", 8, 8))
            used(GC["mlp0"] + 31)
            bucket_step(BUCKETS - 1)
            with v.Fori(0, 2) as i:
                for j in range(4):
                    used(GC["qkv"] + j, i, 4)
                    for m in range(j - 1, j + 1) if j % 2 else ():
                        v.wait_ge(sq_ready, 4 * i + (17 + m))
                        sq = att[:, 512 * (m % 2):512 * (m % 2) + 512].rearrange("p (a b) -> p a b", a=4)
                        v.tensor_reduce(stat[:, bass.ds(8 * i + (8 + 16 * (m % 2) + 4 * (m // 2)), 4)], sq, AX.X,
                                        ALU.add).then_inc(sq_used, 1)
            used(GC["qkv"] + 8)
            v.wait_ge(sq_used, 24)
            inverse_rms(8, [(32, P)])
            for u in range(8):
                gemm_gone(v, GU["qkv"] + u)
            for t in range(2):
                used(GC["qkv"] + 9 + t)
                qk = qkv[:, t, 0:2 * D].rearrange("p (h d) -> p h d", d=P)
                ins = v.tensor_tensor(qk, qk, spread(stat[:, 8 + 16 * t:24 + 16 * t], 1, P), ALU.mult)
                if t:
                    ins.then_inc(heads_normed, 1)
                else:
                    step(ins)
            used(GC["qkv"] + 11)
            v.wait_ge(pool_step, 5 * (BUCKETS - 1) + 1)
            causal_attention("att1", 1.0 / math.sqrt(P), lambda h: bias[:, 384 * h:384 * h + 384], H)
            project_to_x("moba_o")
            norm_x(3)
            cols_out("m1", col("mlp_norm", 8, 8))
            used(GC["moba_o"] + 3)
            v.wait_ge(ctx_in_sb, 16)
            norm_rows(ctx, ctx, xn)
            v.wait_ge(silu_c, 1)

            def ada_half(n, i=None):
                if not 3 <= n < 3 + 24:
                    return
                k = 0 if i is None else i
                chunk, half_ = (n - 3) // 2, (n - 3) % 2
                v.wait_ge(ada_in[half_], 64 * k + 16 * (chunk + 1))
                if half_:
                    v.wait_ge(ada_used, 8 * k + (2 * chunk + 1))
                dst = arena[:, bass.ds(2048 * k + (4096 + 512 * chunk), 512)]
                for kk in range(4):
                    w = bias[:, 2048 * half_ + 512 * kk:2048 * half_ + 512 * (kk + 1)]
                    if kk:
                        settle()
                    if half_ == 0 and kk == 0:
                        ins = v.tensor_scalar(dst, w, sc[:, 0, 0:1], None, ALU.mult)
                    else:
                        ins = v.scalar_tensor_tensor(dst, w, sc[:, 0, 4 * half_ + kk:4 * half_ + kk + 1], dst,
                                                     ALU.mult, ALU.add)
                    if kk == 3:
                        ins.then_inc(ada_used, 1)
                    else:
                        step(ins)

            def gate_out(g):
                u = GU["ada"] + 1 + g
                gemm_out(v, u)
                dst = gates[:, g // 2, 512 * (g % 2):512 * (g % 2) + 512]
                v.tensor_tensor(dst, gbank(u)[:, :], dst, ALU.add).then_inc(gemm_free[u % 4], 1)

            def ada_and_context(n):
                u = GU["ada"]
                if n == 29:
                    gemm_out(v, u)
                    step(v.tensor_tensor(adac[:, 0:32], gbank(u)[:, 0:32], col("ada_cols"), ALU.add))
                    v.tensor_tensor(adac[:, 32:48], gbank(u)[:, 32:48], col("ada_cols", 0, 16), ALU.add)\
                        .then_inc(gemm_free[u % 4], 1)
                    settle()
                    gemm_gone(v, u)
                    for dst, scale, gain in ((48, 8, "norm1"), (56, 24, "norm2"), (64, 40, "norm1")):
                        step(v.scalar_tensor_tensor(adac[:, dst:dst + 8], adac[:, scale:scale + 8], 1.0, col(gain),
                                                    ALU.add, ALU.mult))
                    v.wait_ge(gates_in, 16)
                    for g in range(3):
                        gate_out(g)
                    settle()
                if n == 30:
                    gate_out(3)
                    for m in range(4):
                        cols_scale("hc", m, adac[:, 64:72], adac[:, 32:40], True)

            mlp("mlp1", 16, 3, 24, square_relu("mlp1"), ada_half, after=ada_and_context)
            add_units(SU["d1"], range(4), small=True)
            norm_x(4)
            for n in range(4):
                cols_lo("hc", n, 1)
            for g in range(4):
                gemm_gone(v, GU["ada"] + 1 + g)
            cols_out("hx", adac[:, 48:56], adac[:, 0:8])
            used(GC["mlp1"] + 31)
            z_, az, ez, uz, lz, se, mk = (tmp(k) for k in range(7))
            dt = stat[:, 96:160]
            used(GC["dt"])
            u = GU["dt"]
            gemm_out(v, u)
            v.tensor_copy(cum, gbank(u)[0:16, :]).then_inc(gemm_free[u % 4], 1)
            conv_units = [(GU["xs"] + f, xsT[:, f, :], 2) for f in range(4)] \
                + [(GU["bc"] + g, BT[:, g, :], 2) for g in range(2)] + [(GU["bc"] + 2 + g, CT[:, g, :], 1) for g in range(2)]
            def outer_taps(n):
                u, y, m = conv_units[n]
                if n % 2 == 0:
                    used(GC["xs"] + n // 2)
                v.wait_ge(conv_mid, n + 1)
                y = y.rearrange("p (a b) -> p a b", a=m)
                src = gbank(u)[:, 0:m * T].rearrange("p (a b) -> p a b", a=m)
                step(v.scalar_tensor_tensor(y[:, :, 1:T], src[:, :, 0:T - 1], col("conv_w", 3 * n, 1), y[:, :, 1:T],
                                            ALU.mult, ALU.add))
                settle()
                v.scalar_tensor_tensor(y[:, :, 0:T - 1], src[:, :, 1:T], col("conv_w", 3 * n + 2, 1), y[:, :, 0:T - 1],
                                       ALU.mult, ALU.add).then_inc(gemm_free[u % 4], 1)

            outer_taps(0)
            outer_taps(1)
            u = SU["dtrow"]
            small_out(v, u)
            v.tensor_tensor(z_.rearrange("p (a b) -> p a b", a=4), sbank(u)[:, 0:64].rearrange("p (a b) -> p a b", a=4),
                            spread(row("dt_bias"), 0, 4), ALU.add).then_inc(small_free[u % 4], 1)
            small_gone(v, u)
            v.scalar_tensor_tensor(az, z_, -1.0, z_, ALU.mult, ALU.max).then_inc(sp_abs, 1)
            v.wait_ge(sp_exp, 1)
            v.tensor_scalar(uz, ez, 1.0, None, ALU.add).then_inc(sp_u, 1)
            step(v.tensor_scalar(se, ez, 1.0 / 3, -0.5, ALU.mult, ALU.add))
            step(v.tensor_scalar(mk, ez, 0.01, None, ALU.is_lt))
            settle()
            step(v.tensor_tensor(se, se, ez, ALU.mult))
            settle()
            step(v.scalar_tensor_tensor(se, se, 1.0, ez, ALU.add, ALU.mult))
            settle()
            v.wait_ge(sp_ln, 1)
            for op, b in ((ALU.subtract, lz), (ALU.mult, mk), (ALU.add, lz)):
                step(v.tensor_tensor(se, se, b, op))
                settle()
            step(v.scalar_tensor_tensor(dt, z_, 0.0, se, ALU.max, ALU.add))
            settle()
            v.wait_ge(a_exp, 1)
            v.scalar_tensor_tensor(stat[:, 160:224].rearrange("p (a b) -> p a b", a=4), dt.rearrange("p (a b) -> p a b", a=4),
                                   -1.0, spread(stat[:, 80:96], 0, 4), ALU.mult, ALU.mult).then_inc(dA_ready, 1)
            for n in range(2, 8):
                outer_taps(n)
            grid = const("grid")
            rotated = [(GU["q"] + t, t, 0, 8) for t in range(2)] \
                + [(GU["k"] + 3 * j + t, t, NA + 256 * j, 4) for j in range(2) for t in range(2)]
            for n, (u, t, at, heads_) in enumerate(rotated):
                if n == 0:
                    all_used("q", 2)
                elif n in (2, 4):
                    used(GC["k"] + n // 2 - 1)
                gemm_out(v, u)
                src = gbank(u)[:, 0:64 * heads_].rearrange("p (h d) -> p h d", d=64)
                tm = [view(att, 2048 + 1024 * (n % 2) + 256 * k, heads_, 32) for k in range(4)]
                for k, (a, r) in enumerate(((0, 0), (1, 1), (1, 0), (0, 1))):
                    ins = v.tensor_tensor(tm[k], src[:, :, 32 * a:32 * a + 32],
                                          spread(grid[:, 64 * t + 32 * r:64 * t + 32 * r + 32], 0, heads_), ALU.mult)
                    if k == 3:
                        ins.then_inc(gemm_free[u % 4], 1)
                    else:
                        step(ins)
                settle()
                gemm_gone(v, u)
                dst = nqk[:, t, at:at + 64 * heads_].rearrange("p (h d) -> p h d", d=64)
                step(v.tensor_tensor(dst[:, :, 0:32], tm[0], tm[1], ALU.subtract))
                ins = v.tensor_tensor(dst[:, :, 32:64], tm[2], tm[3], ALU.add)
                if n == len(rotated) - 1:
                    ins.then_inc(nqk_ready, 1)
                else:
                    step(ins)
            settle()
            all_used("z", 2)
            all_used("v", 2)
            u = SU["cum"]
            small_out(v, u)
            v.tensor_copy(cum, sbank(u)[0:16, :]).then_inc(small_free[u % 4], 1)
            u = SU["cumcol"]
            small_out(v, u)
            v.tensor_copy(stat[:, 256:320], sbank(u)[:, 0:64]).then_inc(small_free[u % 4], 1)
            small_gone(v, SU["later"])
            lx = tmp(7).rearrange("p (l d h) -> p l d h", l=2, d=2)
            wl = tmp(8)[:, 0:32].rearrange("p (l d h) -> p l d h", l=2, d=2)
            dtv = dt.rearrange("p (a b) -> p a b", a=4)
            for d in range(2):
                step(v.tensor_tensor(wl[:, :, d, :], lx[:, :, d, 8 * d:8 * d + 8], dtv[:, 2:4, 8 * d:8 * d + 8], ALU.mult))
            settle()
            for t in range(2):
                small_gone(v, SU["xsrow"] + 2 + t)
            for t in range(2):
                for d in range(2):
                    v.tensor_tensor(xw[:, t, d, :].rearrange("p (h q) -> p h q", q=64),
                                    cxsr[:, t, :].rearrange("p (h q) -> p h q", q=64),
                                    spread(wl[:, t, d, :], 1, 64), ALU.mult).then_inc(xw_ready, 1)
            v.wait_ge(xw_ready, 4)
            for g in range(2):
                u = SU["cb"] + g
                small_out(v, u)
                b = sbank(u)
                upto, since = const("upto", 0, P), const("since", P, P)
                step(v.tensor_tensor(cbm[:, g, 0:128], b[:, 0:128], upto, ALU.mult))
                step(v.tensor_copy(cbm[:, g, 128:256], b[:, 128:256]))
                step(v.tensor_tensor(cbm[:, g, 256:384], b[:, 384:512], upto, ALU.mult))
                step(v.tensor_tensor(cbm[:, g, 384:512], b[:, 0:128], since, ALU.mult))
                step(v.tensor_copy(cbm[:, g, 512:640], b[:, 256:384]))
                v.tensor_tensor(cbm[:, g, 640:768], b[:, 384:512], since, ALU.mult).then_inc(small_free[u % 4], 1)
            v.wait_ge(rpb_loaded, 16)

            def window_logits(i):
                h, t, b = i // 2, i % 2, i % 2
                u = SU["na"] + unit_w[("S", i)]
                small_out(v, u)
                bs = bias[:, (8 * t + h) * T:(8 * t + h + 1) * T]
                step(v.tensor_tensor(sbank(u)[:, 0:T], sbank(u)[:, 0:T], bs, ALU.add))
                settle()
                v.tensor_reduce(stat[:, 56 + b:57 + b], sbank(u)[:, :], AX.X, ALU.max, negate=True)\
                    .then_inc(max_ready, 1)

            def window_normalise(i):
                b = i % 2
                small_gone(v, SU["na"] + unit_w[("S", i)])
                step(v.reciprocal(stat[:, 64 + b:65 + b], stat[:, 60 + b:61 + b]))
                settle()
                pr = att[:, 1024 + 512 * b:1536 + 512 * b]
                v.tensor_scalar(pr, pr, stat[:, 64 + b:65 + b], None, ALU.mult).then_inc(probs_ready, 1)

            def pair_lo(p):
                u = GU["na_o"] + p
                v.wait_ge(out_hi, 2 * H + p + 1)
                v.tensor_tensor(acts[:, 1, 1, p * T:(p + 1) * T], gbank(u)[:, 0:T],
                                acts[:, 1, 0, p * T:(p + 1) * T].bitcast(F32), ALU.subtract)\
                    .then_inc(gemm_free[u % 4], 1)

            for i in range(2 * H + 1):
                if i < 2 * H:
                    window_logits(i)
                if i:
                    window_normalise(i - 1)
                if i >= 8 and i % 4 == 0:
                    pair_lo(i // 4 - 2)
            pair_lo(3)

            parts = ((0, 256, 0, 0), (256, 384, 128, 1), (384, 512, 256, 0), (512, 768, 256, 1))

            def decay(h):
                u = SU["seg"] + h
                small_out(v, u)
                if h >= 2:
                    v.wait_ge(w_mat, h - 1)
                for n, (a, e, src, t) in enumerate(parts):
                    c = 256 + 16 * t + h if n < 2 else 256 + 32 + 16 * t + 8 + h
                    ins = v.tensor_scalar(E[:, h % 2, a:e], sbank(u)[:, src:src + e - a], stat[:, c:c + 1], 0.0,
                                          ALU.subtract, ALU.min)
                    if n == 3:
                        ins.then_inc(small_free[u % 4], 1)
                    else:
                        step(ins)

            def matrix(h):
                v.wait_ge(seg_exp, h + 1)
                if h >= 2:
                    v.wait_ge(y_used, h - 1)
                for n, (a, e, src, t) in enumerate(parts):
                    c = 96 + 16 * t + h if n < 2 else 96 + 16 * t + 8 + h
                    ins = v.scalar_tensor_tensor(Wm[:, h % 2, a:e], E[:, h % 2, a:e], stat[:, c:c + 1],
                                                 cbm[:, h // 4, a:e], ALU.mult, ALU.mult)
                    if n == 3:
                        ins.then_inc(w_mat, 1)
                    else:
                        step(ins)

            for g in range(2):
                small_gone(v, SU["cb"] + g)
            small_gone(v, SU["cumcol"])
            settle()
            decay(0)
            for h in range(H):
                if h + 1 < H:
                    decay(h + 1)
                matrix(h)
            v.wait_ge(ecum_ready, 1)
            for t in range(2):
                small_gone(v, SU["xsrow"] + t)
            heads = lambda ap: ap.rearrange("p (h q) -> p h q", q=64)
            for t in range(2):
                step(v.tensor_tensor(heads(yrow[:, t, :]), heads(xsr[:, t, :]), spread(row("ssd_d"), 1, 64), ALU.mult))
            settle()
            for t in range(2):
                u = GU["y"] + t
                gemm_out(v, u)
                v.tensor_tensor(yrow[:, t, :], gbank(u)[:, :], yrow[:, t, :], ALU.add).then_inc(gemm_free[u % 4], 1)
                gemm_gone(v, u)
                for d in range(2):
                    u = SU["yoff"] + 2 * t + d
                    tm = att[:, 512 * d:512 * (d + 1)]
                    small_out(v, u)
                    c = 320 + 32 * d + 16 * t + 8 * d
                    v.tensor_tensor(heads(tm), heads(sbank(u)[:, :]), spread(stat[:, c:c + 8], 1, 64), ALU.mult)\
                        .then_inc(small_free[u % 4], 1)
                    small_gone(v, u)
                    step(v.tensor_tensor(yrow[:, t, :], yrow[:, t, :], tm, ALU.add))
                    settle()
                step(v.tensor_tensor(yrow[:, t, :], yrow[:, t, :], sz[:, t, :], ALU.mult))
            settle()
            for t in range(2):
                sum_squares(yrow[:, t, :], att[:, 512 * t:512 * (t + 1)], t)
            settle()
            inverse_rms(0, [(2, NA)])
            for t in range(2):
                ins = v.tensor_scalar(yrow[:, t, :], yrow[:, t, :], stat[:, t:t + 1], None, ALU.mult)
                if t:
                    ins.then_inc(normed, 1)
                else:
                    step(ins)
            for n in range(2):
                scaled_lo("yT", n, 4 + 2 * n, 2, col("ssd_norm", 2 * n, 2), HI0["yT"] + n + 1)
            project_to_x("out", 0)
            norm_x(5)
            cols_out("m2", adac[:, 56:64], adac[:, 16:24])
            used(GC["out"] + 3)

            def glu(s, i=None):
                u, b, k = GU["glu"] + s, s % 2, 0 if i is None else i
                v.wait_ge(glu_mid, 4 * k + (s + 1))
                for tap in (0, 2):
                    w = cols[:, bass.ds(12 * k + (CA["fconv_w"] + 3 * s + tap), 1)]
                    y = gact[:, b, 1:T] if tap == 0 else gact[:, b, 0:T - 1]
                    src = gbank(u)[:, 0:T - 1] if tap == 0 else gbank(u)[:, 1:T]
                    if tap:
                        settle()
                    ins = v.scalar_tensor_tensor(y, src, w, y, ALU.mult, ALU.add)
                    if tap:
                        ins.then_inc(glu_taps, 1)
                    else:
                        step(ins)
                if s + 2 < KF2:
                    split_lo(GC["glu"] + s + 2, i, 4)
                v.wait_ge(glu_act, 4 * k + (s + 1))
                v.tensor_tensor(prod_t[:, b, :], gbank(u)[:, T:2 * T], gact[:, b, :], ALU.mult)\
                    .then_inc(gemm_free[u % 4], 1)
                v.wait_ge(hidden_hi, 4 * k + (HID0["glu"] + s + 1))
                v.tensor_tensor(acts[:, 1, 1, 512 * b:512 * b + T], prod_t[:, b, :],
                                acts[:, 1, 0, 512 * b:512 * b + T].bitcast(F32), ALU.subtract).then_inc(act_lo, 1)
                v.wait_ge(down_hi, 4 * k + (s + 1))
                v.tensor_tensor(split_down[:, 1, :], raw_down[:, b, :], split_down[:, 0, :].bitcast(F32), ALU.subtract)\
                    .then_inc(down_lo, 1)

            glu(0)
            with v.Fori(0, 4) as i:
                st.enter(i, 4)
                for s in range(1, 5):
                    glu(s, i)
            st.leave(4)
            for s in range(17, KF2):
                glu(s)
            add_units(SU["d2"], range(4), small=True, gate=1)
            sum_squares_of_x(6)
            v.wait_ge(final_in, 16)
            for t in range(2):
                v.scalar_tensor_tensor(xn[:, t, :], x[:, t, :], stat[:, t:t + 1], final, ALU.mult, ALU.mult)\
                    .then_inc(out_ready, 1)



def t5_thresholds():
    n = np.arange(1, 4096)
    exact = BUCKETS // 2
    large = exact + (np.log(n.astype(np.float32) / np.float32(exact)) / np.float32(math.log(1024 / exact))
                     * np.float32(BUCKETS - exact)).astype(np.int32)
    bucket = np.where(n < exact, n, np.minimum(large, BUCKETS - 1))
    return np.array([0] + [n[bucket >= b][0] for b in range(1, BUCKETS)], np.float32)


def constants():
    i = np.arange(P)
    upto = (i[:, None] <= i[None, :]).astype(np.float32)
    one = np.ones((P, P), np.float32)
    c = np.zeros((P, KA[None]), np.float32)

    def put(name, a):
        c[:, KA[name]:KA[name] + CONSTS[name]] = a

    mask = np.where(i[None, :] <= i[:, None], 0.0, NEG)
    put("ident", np.eye(P))
    put("upto", np.concatenate([upto, one], 1))
    put("since", np.concatenate([one, upto.T], 1))
    put("after", (i[:, None] > i[None, :]))
    put("before", (i[:, None] < i[None, :]))
    put("ones", one)
    put("causal", np.concatenate([np.zeros((P, P)), mask, mask], 1))
    tok = np.arange(T)
    freqs = np.float32(10000.0) ** (-np.arange(16, dtype=np.float32) / np.float32(16))
    ang = np.concatenate([(tok // 64).astype(np.float32)[:, None] * freqs, (tok % 64).astype(np.float32)[:, None] * freqs], 1)
    grid = np.stack([np.cos(ang), np.sin(ang)], 1)
    put("grid", grid.reshape(2, P, 64).transpose(1, 0, 2).reshape(P, 128))
    put("inv_freq", np.float32(10000.0) ** (-np.arange(0, 64, 2, dtype=np.float32) / np.float32(64)))
    put("thresholds", t5_thresholds())
    select = np.zeros((16, 16, P), np.float32)
    select[np.arange(16), np.arange(16)] = 1.0
    return c, select.reshape(16, 16 * P)


def kernel(**inputs):
    import concourse.bacc as bacc
    from concourse.bass_utils import run_bass_kernel_spmd as run

    g = {k: np.asarray(a) for k, a in inputs.items()}

    def chunks(w, kts, width):
        k, n = w.shape
        w = w.reshape(k // (P * kts), kts, P, n // width, width)
        return np.ascontiguousarray(w.transpose(3, 0, 2, 1, 4).reshape(-1, P, kts * width))

    w2 = g["w_in_2"][0]
    up, nf = g["ffn_w_up_2"][0], FF2 // P
    glu_up = np.concatenate([chunks(up[:, :FF2], KD, P).reshape(nf, P, KD, P),
                             chunks(up[:, FF2:], KD, P).reshape(nf, P, KD, P)], 3).reshape(nf, P, SLOT)

    def mlp(layer):
        parts = (chunks(g["mlp_w_in"][layer], KD, 256), chunks(g["mlp_w_out"][layer], 2, D))
        return np.stack([parts[down][step] for down, step in alternate(FF // 256)])

    ada = g["ada_w_2"][0].reshape(2, 4, P, 12, 512).transpose(3, 0, 2, 1, 4).reshape(24, P, 2048)
    weights = {
        "mla_in": chunks(g["mla_w_in"][0], 4, 352), "mla_uq": chunks(g["mla_w_uq"][0], 3, 384),
        "mla_ukv": chunks(g["mla_w_ukv"][0], 2, 1024), "mla_o": chunks(g["mla_w_o"][0], 4, 512),
        "mlp0": mlp(0), "qkv": chunks(g["moba_w_qkv"][0], 4, 512), "moba_o": chunks(g["moba_w_o"][0], 4, 512),
        "mlp1": mlp(1), "ada": np.ascontiguousarray(ada), "dt": chunks(w2[:, 3072:], 8, 16),
        "xs": chunks(w2[:, 2048:2560], 8, 256), "bc": chunks(w2[:, 2560:3072], 8, 256),
        "q": chunks(w2[:, 0:512], 4, 512), "k": chunks(w2[:, 512:1024], 8, 256),
        "v": chunks(w2[:, 1024:1536], 4, 512), "z": chunks(w2[:, 1536:2048], 4, 512),
        "out": chunks(g["w_out_2"][0], 4, 512), "glu": glu_up, "glu_down": chunks(g["ffn_w_down_2"][0], 1, D),
    }

    def tiles(a):
        return a.reshape(-1, P).T

    ada_b = g["ada_b_2"][0].reshape(6, D)
    col = {
        "attn_norm": tiles(g["attn_norm"]), "mlp_norm": tiles(g["mlp_norm"]),
        "c_norm": np.concatenate([tiles(g["mla_q_a_norm"]), tiles(g["mla_kv_a_norm"])], 1),
        "q_nope": tiles(g["mla_q_nope_norm"]), "k_nope": tiles(g["mla_k_nope_norm"]),
        "moba_q": tiles(g["moba_q_norm"]), "moba_k": tiles(g["moba_k_norm"]),
        "norm1": tiles(g["norm1_w_2"]), "norm2": tiles(g["norm2_w_2"]),
        "ada_cols": tiles(ada_b[[0, 1, 3, 4]]),
        "conv_w": g["ssd_conv_w_2"][0].reshape(3, 8, P).transpose(2, 1, 0).reshape(P, 24),
        "conv_b": tiles(g["ssd_conv_b_2"]),
        "fconv_w": g["ffn_conv_w_2"][0].reshape(3, KF2, P).transpose(2, 1, 0).reshape(P, 3 * KF2),
        "fconv_b": tiles(g["ffn_conv_b_2"]), "ssd_norm": tiles(g["ssd_norm_w_2"]),
        "c": tiles(g["c_2"]), "c_ctx": tiles(g["c_ctx_2"]),
    }
    row = {
        "q_rope": g["mla_q_rope_norm"], "k_rope": g["mla_k_rope_norm"], "table": g["rel_bias_table"],
        "dt_bias": g["dt_bias_2"], "a_log": g["a_log_2"], "ssd_d": g["ssd_d_2"],
    }
    rpb = g["rpb_2"][0]
    wide = np.full((H, 15, 64 + 127), NEG, np.float32)
    wide[:, :, 48:79] = rpb
    col_start = np.clip(np.arange(64) - 8, 0, 48)
    per_w = np.full((64, H, 15, 64), NEG, np.float32)
    for w in range(64):
        a = col_start[w]
        per_w[w, :, :, a:a + 16] = wide[:, :, 63 - w + a:63 - w + a + 16]
    rpb_l = np.empty((2, 64, 2, H, 4, 64), np.float32)
    for r in range(4):
        rpb_l[r % 2, :, r // 2] = per_w[:, :, 7 - r:11 - r, :]

    consts, select = constants()
    rows_tiled = lambda a: np.ascontiguousarray(a.reshape(2, P, D).transpose(1, 0, 2))
    data = {
        "x": rows_tiled(g["x"][0]), "ctx": rows_tiled(g["ctx_2"][0]),
        "cols": np.ascontiguousarray(np.concatenate([col[k] for k in COLS], 1)),
        "rows": np.concatenate([row[k].reshape(-1) for k in ROWS])[None],
        "consts": consts, "select": select,
        "pos_col": np.ascontiguousarray(g["positions"].reshape(2, P).T), "pos_row": g["positions"].reshape(1, T),
        "rpb": np.ascontiguousarray(rpb_l.reshape(P, 4096)),
        "gates": np.ascontiguousarray(ada_b[[2, 5]].reshape(1, 2 * D)), "final": g["final_norm_w_2"].reshape(1, D),
    }
    nc = bacc.Bacc("TRN2", target_bir_lowering=False, num_devices=1)
    arrays = {}

    def dram(name, a):
        arrays[name] = a
        return nc.dram_tensor(name, a.shape, mybir.dt.from_np(a.dtype), kind="ExternalInput").ap()

    w_aps = {k: dram("w_" + k, a) for k, a in weights.items()}
    d = {k: dram("in_" + k, a) for k, a in data.items()}
    for k in ("rows", "pos_row", "gates", "final"):
        d[k] = bass.AP(d[k].tensor, 0, [[0, P], [1, data[k].shape[1]]])
    out = nc.dram_tensor("out", (P, 2, D), F32, kind="ExternalOutput").ap()
    program(nc, w_aps, d["x"], d["ctx"], d["cols"], d["rows"], d["consts"], d["select"], d["pos_col"], d["pos_row"],
            d["rpb"], d["gates"], d["final"], out)
    got = run(nc, [arrays], core_ids=[0]).results[0]["out"]
    return np.ascontiguousarray(got.reshape(P, 2, D).transpose(1, 0, 2).reshape(1, T, D))
```
